# Optimizing a Trainium2 kernel written in Bass

```python
import math
import jax, jax.numpy as jnp
from jax import lax
import numpy as np

D_MODEL = 1024
BATCH = 1
SEQ = 1024
DEPTH = 1
DEC_BATCH = 1
DEC_SEQ = 512
PAST_LEN = 128

N_META = 16
GRID_W = 64
WIN_H = 8
WIN_W = 16
Q_BLOCK_W = 16
K_BLOCK_W = 32
N_COL_BLOCKS = GRID_W // Q_BLOCK_W
N_HEADS_ATT = 8
HEAD_DIM = 64
D_ATT = N_HEADS_ATT * HEAD_DIM
D_CONV = D_MODEL
CONV_W = 3
N_GROUPS = 4
EXPERTS_PER_GROUP = 8
N_EXPERTS = N_GROUPS * EXPERTS_PER_GROUP
TOP_K_INNER = 2
D_EXPERT = D_MODEL // 2
MOE_BLOCK = 128
ALPHA = (2.0 * DEPTH) ** 0.25
BETA = (8.0 * DEPTH) ** -0.25
LN_EPS = 1e-5
D_IN_PROJ = 3 * D_ATT + 3 * D_CONV + 2 * D_MODEL

kernel_name = "hybrid_na_shortconv_hmoe_encoder"

def _col_tables():
    cb = np.arange(N_COL_BLOCKS)
    k_start = np.clip(cb * Q_BLOCK_W - (K_BLOCK_W - Q_BLOCK_W) // 2, 0, GRID_W - K_BLOCK_W)
    key_cols = k_start[:, None] + np.arange(K_BLOCK_W)[None, :]
    q_cols = cb[:, None] * Q_BLOCK_W + np.arange(Q_BLOCK_W)[None, :]
    w_start = np.clip(q_cols - WIN_W // 2, 0, GRID_W - WIN_W)
    kc = key_cols[:, None, :]
    valid = (kc >= w_start[:, :, None]) & (kc < w_start[:, :, None] + WIN_W)
    dx_idx = np.clip(kc - q_cols[:, :, None] + WIN_W - 1, 0, 2 * WIN_W - 2)
    return key_cols.astype(np.int32), valid, dx_idx.astype(np.int32)

def _layer_norm(x, g, b):
    xf = x.astype(jnp.float32)
    mu = jnp.mean(xf, axis=-1, keepdims=True)
    var = jnp.mean(jnp.square(xf - mu), axis=-1, keepdims=True)
    return ((xf - mu) * lax.rsqrt(var + LN_EPS) * g.astype(jnp.float32) + b.astype(jnp.float32)).astype(x.dtype)

def _neighbourhood_attention(q, k, v, rpb):
    bsz, L = q.shape[0], q.shape[1]
    T = L - N_META
    rows = T // GRID_W
    kh = min(WIN_H, rows)
    q = q * (HEAD_DIM ** -0.5)
    qm, km, vm = q[:, :N_META], k[:, :N_META], v[:, :N_META]
    s_meta = jnp.einsum('bqhd,bkhd->bhqk', qm, km).astype(jnp.float32)
    p_meta = jax.nn.softmax(s_meta, axis=-1).astype(v.dtype)
    o_meta = jnp.einsum('bhqk,bkhd->bqhd', p_meta, vm)
    qg = q[:, N_META:].reshape(bsz, rows, N_COL_BLOCKS, Q_BLOCK_W, N_HEADS_ATT, HEAD_DIM)
    kg = k[:, N_META:].reshape(bsz, rows, GRID_W, N_HEADS_ATT, HEAD_DIM)
    vg = v[:, N_META:].reshape(bsz, rows, GRID_W, N_HEADS_ATT, HEAD_DIM)
    key_cols, valid_np, dx_idx = _col_tables()
    valid = jnp.asarray(valid_np)[None, None, :, :, None, :]

    def row_fn(r):
        rs = jnp.clip(r - kh // 2, 0, rows - kh)
        q_r = lax.dynamic_index_in_dim(qg, r, axis=1, keepdims=False)
        k_r = lax.dynamic_slice_in_dim(kg, rs, kh, axis=1)
        v_r = lax.dynamic_slice_in_dim(vg, rs, kh, axis=1)
        k_blk = k_r[:, :, key_cols]
        v_blk = v_r[:, :, key_cols]
        s_loc = jnp.einsum('bcqhd,bkcmhd->bhcqkm', q_r, k_blk).astype(jnp.float32)
        dy = rs + jnp.arange(kh) - r
        bias = rpb[:, dy + WIN_H - 1][:, :, dx_idx]
        bias = jnp.transpose(bias, (0, 2, 3, 1, 4)).astype(jnp.float32)
        s_loc = jnp.where(valid, s_loc + bias[None], -jnp.inf)
        s_loc = s_loc.reshape(bsz, N_HEADS_ATT, N_COL_BLOCKS, Q_BLOCK_W, kh * K_BLOCK_W)
        s_mk = jnp.einsum('bcqhd,bkhd->bhcqk', q_r, km).astype(jnp.float32)
        p = jax.nn.softmax(jnp.concatenate([s_mk, s_loc], axis=-1), axis=-1).astype(v.dtype)
        p_m = p[..., :N_META]
        p_l = p[..., N_META:].reshape(bsz, N_HEADS_ATT, N_COL_BLOCKS, Q_BLOCK_W, kh, K_BLOCK_W)
        o = jnp.einsum('bhcqk,bkhd->bcqhd', p_m, vm) + jnp.einsum('bhcqkm,bkcmhd->bcqhd', p_l, v_blk)
        return o.reshape(bsz, GRID_W, N_HEADS_ATT, HEAD_DIM)

    o_real = lax.map(row_fn, jnp.arange(rows, dtype=jnp.int32))
    o_real = jnp.transpose(o_real, (1, 0, 2, 3, 4)).reshape(bsz, T, N_HEADS_ATT, HEAD_DIM)
    return jnp.concatenate([o_meta, o_real], axis=1)

def _short_conv(u, w, b):
    up = jnp.pad(u, ((0, 0), (1, 1), (0, 0)))
    return up[:, :-2] * w[0] + up[:, 1:-1] * w[1] + up[:, 2:] * w[2] + b

def _mixer(x, w_in, rpb, conv_w, conv_b, w_att_proj, w_conv_proj, w_out):
    bsz, L, _ = x.shape
    proj = x @ w_in
    splits = [D_ATT, 2 * D_ATT, 3 * D_ATT, 3 * D_ATT + D_CONV, 3 * D_ATT + 2 * D_CONV,
              3 * D_ATT + 3 * D_CONV, 3 * D_ATT + 3 * D_CONV + D_MODEL]
    q, k, v, b_gate, c_gate, x_conv, g_att, g_conv = jnp.split(proj, splits, axis=-1)
    hs = (bsz, L, N_HEADS_ATT, HEAD_DIM)
    att = _neighbourhood_attention(q.reshape(hs), k.reshape(hs), v.reshape(hs), rpb)
    att = att.reshape(bsz, L, D_ATT) @ w_att_proj
    conv = (b_gate * _short_conv(c_gate * x_conv, conv_w, conv_b)) @ w_conv_proj
    merged = jax.nn.sigmoid(g_att) * att + jax.nn.sigmoid(g_conv) * conv
    return merged @ w_out

def _hier_moe(x, w_router_group, w_router_expert, w_e_gate, w_e_up, w_e_down):
    shp = x.shape
    xf = x.reshape(-1, D_MODEL)
    n = xf.shape[0]
    lg = (xf @ w_router_group).astype(jnp.float32)
    pg = jax.nn.softmax(lg, axis=-1)
    grp = jnp.argmax(lg, axis=-1).astype(jnp.int32)
    pg_sel = jnp.take_along_axis(pg, grp[:, None], axis=-1)
    le = (xf @ w_router_expert).astype(jnp.float32).reshape(n, N_GROUPS, EXPERTS_PER_GROUP)
    le_sel = jnp.take_along_axis(le, grp[:, None, None], axis=1)[:, 0]
    top_v, top_i = lax.top_k(le_sel, TOP_K_INNER)
    gate = pg_sel * jax.nn.softmax(top_v, axis=-1)
    expert = grp[:, None] * EXPERTS_PER_GROUP + top_i.astype(jnp.int32)
    nk = n * TOP_K_INNER
    e_flat = expert.reshape(-1)
    tok_flat = jnp.broadcast_to(jnp.arange(n, dtype=jnp.int32)[:, None], (n, TOP_K_INNER)).reshape(-1)
    g_flat = gate.reshape(-1)
    order = jnp.argsort(e_flat)
    e_s, tok_s, g_s = e_flat[order], tok_flat[order], g_flat[order]
    counts = jnp.bincount(e_flat, length=N_EXPERTS).astype(jnp.int32)
    padded = (counts + MOE_BLOCK - 1) // MOE_BLOCK * MOE_BLOCK
    start = jnp.cumsum(counts) - counts
    pend = jnp.cumsum(padded)
    pstart = pend - padded
    dest = pstart[e_s] + (jnp.arange(nk, dtype=jnp.int32) - start[e_s])
    n_blocks = (nk + N_EXPERTS * (MOE_BLOCK - 1) + MOE_BLOCK - 1) // MOE_BLOCK
    P = n_blocks * MOE_BLOCK
    buf_tok = jnp.full((P,), n, dtype=jnp.int32).at[dest].set(tok_s)
    buf_gate = jnp.zeros((P,), dtype=jnp.float32).at[dest].set(g_s)
    blk_expert = jnp.clip(jnp.searchsorted(pend, jnp.arange(n_blocks, dtype=jnp.int32) * MOE_BLOCK, side='right'),
                          0, N_EXPERTS - 1).astype(jnp.int32)
    x_pad = jnp.concatenate([xf, jnp.zeros((1, D_MODEL), xf.dtype)], axis=0)
    xb = x_pad[buf_tok].reshape(n_blocks, MOE_BLOCK, D_MODEL)

    def block_fn(args):
        xblk, e = args
        h = jax.nn.silu(xblk @ w_e_gate[e]) * (xblk @ w_e_up[e])
        return h @ w_e_down[e]

    yb = lax.map(block_fn, (xb, blk_expert)).reshape(P, D_MODEL)
    yb = yb * buf_gate[:, None].astype(yb.dtype)
    y = jax.ops.segment_sum(yb, buf_tok, num_segments=n + 1)[:n]
    return y.reshape(shp)

def _encode(x, meta_tokens, w_in, rpb, conv_w, conv_b, w_att_proj, w_conv_proj, w_out,
            ln1_g, ln1_b, w_router_group, w_router_expert, w_e_gate, w_e_up, w_e_down, ln2_g, ln2_b):
    bsz = x.shape[0]
    meta = jnp.broadcast_to(meta_tokens[None].astype(x.dtype), (bsz, N_META, D_MODEL))
    h = jnp.concatenate([meta, x], axis=1)
    for i in range(DEPTH):
        mix = _mixer(h, w_in[i], rpb[i], conv_w[i], conv_b[i], w_att_proj[i], w_conv_proj[i], w_out[i])
        h = _layer_norm(ALPHA * h + mix, ln1_g[i], ln1_b[i])
        ffn = _hier_moe(h, w_router_group[i], w_router_expert[i], w_e_gate[i], w_e_up[i], w_e_down[i])
        h = _layer_norm(ALPHA * h + ffn, ln2_g[i], ln2_b[i])
    return h[:, N_META:]

def setup_inputs(seed: int = 0) -> dict:
    key = jax.random.key(seed)
    ks = jax.random.split(key, 21)
    f32 = jnp.float32

    def nrm(k, shape, scale):
        return jax.random.normal(k, shape, f32) * scale

    return {
        "x_prompt": nrm(ks[0], (BATCH, SEQ, D_MODEL), 1.0),
        "x_sample": nrm(ks[1], (DEC_BATCH, DEC_SEQ, D_MODEL), 1.0),
        "meta_tokens": nrm(ks[2], (N_META, D_MODEL), 1.0),
        "w_in": nrm(ks[3], (DEPTH, D_MODEL, D_IN_PROJ), D_MODEL ** -0.5),
        "rpb": nrm(ks[4], (DEPTH, N_HEADS_ATT, 2 * WIN_H - 1, 2 * WIN_W - 1), 0.1),
        "conv_w": nrm(ks[5], (DEPTH, CONV_W, D_CONV), CONV_W ** -0.5),
        "conv_b": nrm(ks[6], (DEPTH, D_CONV), 0.02),
        "w_att_proj": nrm(ks[7], (DEPTH, D_ATT, D_MODEL), BETA * D_ATT ** -0.5),
        "w_conv_proj": nrm(ks[8], (DEPTH, D_CONV, D_MODEL), BETA * D_CONV ** -0.5),
        "w_out": nrm(ks[9], (DEPTH, D_MODEL, D_MODEL), BETA * D_MODEL ** -0.5),
        "ln1_g": 1.0 + nrm(ks[10], (DEPTH, D_MODEL), 0.02),
        "ln1_b": nrm(ks[11], (DEPTH, D_MODEL), 0.02),
        "w_router_group": nrm(ks[12], (DEPTH, D_MODEL, N_GROUPS), D_MODEL ** -0.5),
        "w_router_expert": nrm(ks[13], (DEPTH, D_MODEL, N_EXPERTS), D_MODEL ** -0.5),
        "w_e_gate": nrm(ks[14], (DEPTH, N_EXPERTS, D_MODEL, D_EXPERT), D_MODEL ** -0.5),
        "w_e_up": nrm(ks[15], (DEPTH, N_EXPERTS, D_MODEL, D_EXPERT), BETA * D_MODEL ** -0.5),
        "w_e_down": nrm(ks[16], (DEPTH, N_EXPERTS, D_EXPERT, D_MODEL), BETA * D_EXPERT ** -0.5),
        "ln2_g": 1.0 + nrm(ks[17], (DEPTH, D_MODEL), 0.02),
        "ln2_b": nrm(ks[18], (DEPTH, D_MODEL), 0.02),
    }

def reference(x_prompt, x_sample, meta_tokens, w_in, rpb, conv_w, conv_b, w_att_proj, w_conv_proj, w_out,
              ln1_g, ln1_b, w_router_group, w_router_expert, w_e_gate, w_e_up, w_e_down, ln2_g, ln2_b):
    y_prompt = _encode(x_prompt, meta_tokens, w_in, rpb, conv_w, conv_b, w_att_proj, w_conv_proj, w_out,
                       ln1_g, ln1_b, w_router_group, w_router_expert, w_e_gate, w_e_up, w_e_down, ln2_g, ln2_b)
    y_sample = _encode(x_sample, meta_tokens, w_in, rpb, conv_w, conv_b, w_att_proj, w_conv_proj, w_out,
                       ln1_g, ln1_b, w_router_group, w_router_expert, w_e_gate, w_e_up, w_e_down, ln2_g, ln2_b)
    return (y_prompt, y_sample)


_drawn_inputs = setup_inputs


def setup_inputs(seed=0):
    import zlib

    import numpy as np

    out = dict(_drawn_inputs(seed))
    spreads = {}
    factors = {'meta_tokens': 4.985, 'rpb': 8.0, 'conv_b': 8.0, 'ln2_g': 2.875, 'ln2_b': 2.903}
    for name, (base, spread) in spreads.items():
        noise = np.random.default_rng([zlib.crc32(name.encode()), seed]).standard_normal(out[name].shape)
        drawn = base * np.exp(spread * noise) if base else spread * noise
        out[name] = __import__('jax').numpy.asarray(drawn.astype(out[name].dtype))
    for name, factor in factors.items():
        out[name] = (out[name] * factor).astype(out[name].dtype)
    return out
```

```python
from contextlib import ExitStack

import numpy as np

import concourse.bass as bass
from concourse import mybir

F32 = mybir.dt.float32
F32R = mybir.dt.float32r
BF16 = mybir.dt.bfloat16
I32 = mybir.dt.int32
ALU = mybir.AluOpType
ACT = mybir.ActivationFunctionType
AX = mybir.AxisListType

P = 128
D = 1024
KD = D // P
NMETA = 16
PROMPT, SAMPLE = 1024, 512
NTOK = PROMPT + SAMPLE
NCOL = NTOK + NMETA
TILE = 512
NT = NTOK // TILE
GRID, WIN_H, WIN_W = 64, 8, 16
ROWS_T = TILE // GRID
KROWS, KCOLS = 12, 32
NKEY = KROWS * KCOLS
NCB = 4
HEADS, DH = 8, 64
HP = HEADS // 2
FB = D // P
ALPHA = 2.0 ** 0.25
EPS = 1e-5
NEG = -1e30
BP_ROWS = 24
NG, NEXP, EPG = 4, 32, 8
DE = 512
KE = DE // P
NSUB = NTOK // P
SUB_T = TILE // P
NLOG = NG + NEXP
NBLK = (2 * NTOK + NEXP * (P - 1)) // P + 1
NBLK += NBLK % 2
NPLAN = NBLK + 1


NEDGE, RIGHT = 12, 9
N_CXB, N_MERGE, N_OUT = 3 * FB, 4 * FB, FB
N_TILE = N_CXB + N_MERGE + N_OUT


def key_start(cb):
    return min(max(cb * 16 - 8, 0), GRID - KCOLS)


def window_masks():
    m = np.full((NT, P, NCB, KROWS, KCOLS), NEG, np.float32)
    for t in range(NT):
        base = 4 * t + 4 * (t // 2)
        rows, first = (16, 0) if t < 2 else (8, 16)
        for r in range(ROWS_T):
            row = 8 * t + r - first
            rs = min(max(row - WIN_H // 2, 0), rows - WIN_H) + first
            for i in range(16):
                for cb in range(NCB):
                    ws = min(max(cb * 16 + i - WIN_W // 2, 0), GRID - WIN_W)
                    a, c = rs - base, ws - key_start(cb)
                    m[t, r * 16 + i, cb, a:a + WIN_H, c:c + WIN_W] = 0.0
    bits = m.reshape(NT, P, NCB * NKEY).view(np.uint32) >> 16
    return bits.astype(np.uint16)


def project_qkv(nc, a, x_cols, w_qkv, w_cxb, ident, qkv, edges):
    nblk = w_qkv.shape[0]
    nq = HP
    beside = slice(TILE, NCOL, NCOL - 1 - TILE)
    with ExitStack() as ctx:
        sb = lambda n, s, d=F32: ctx.enter_context(nc.sbuf_tensor(n, s, d))
        sem = lambda n: ctx.enter_context(nc.semaphore(n))
        x_hi = sb("qkv_x_hi", [P, KD, NCOL], F32R)
        x_lo = sb("qkv_x_lo", [P, KD, NCOL], F32R)
        x_raw = sb("qkv_x_raw", [P, 2, NCOL])
        w_raw = sb("qkv_w_raw", [P, 2, D])
        w_hi = sb("qkv_w_hi", [P, 2, D], F32R)
        w_lo = sb("qkv_w_lo", [P, 2, D], F32R)
        res = sb("qkv_res", [P, 2, NCOL])
        bank = [[ctx.enter_context(nc.psum_tensor(f"qkv_ps{s}{t}", [P, 512], F32)) for t in range(4)]
                for s in range(2)]
        x_side = sb("qkv_x_side", [P, KD, 2])
        c_row = sb("qkv_c_row", [2, P])
        u_row = sb("qkv_u_row", [2, D])
        side_in = [sem(f"qkv_side_in{s}") for s in range(2)]
        ident_ok = sem("qkv_ident_ok")
        side_used = sem("qkv_side_used")
        x_side_ok = sem("qkv_x_side_ok")
        c_row_ok = sem("qkv_c_row_ok")
        u_row_ok = sem("qkv_u_row_ok")
        u_col_ok = sem("qkv_u_col_ok")
        edge_ok = sem("qkv_edge_ok")
        x_in = [sem(f"qkv_x_in{s}") for s in range(2)]
        x_hi_ok = sem("qkv_x_hi_ok")
        x_lo_ok = sem("qkv_x_lo_ok")
        w_in = [sem(f"qkv_w_in{s}") for s in range(2)]
        w_hi_ok = sem("qkv_w_hi_ok")
        w_lo_ok = sem("qkv_w_lo_ok")
        w_used = sem("qkv_w_used")
        ev_act = sem("qkv_ev_act")
        ev_dve = sem("qkv_ev_dve")
        stored = [sem(f"qkv_stored{s}") for s in range(2)]
        cols = [slice(t * TILE, (t + 1) * TILE) for t in range(NT)] + [slice(NTOK, NCOL)]
        scrap = sb("qkv_scrap", [1, 4])
        block = ctx.enter_context(nc.Block())

        def load_w(eng, n, i, s):
            eng.wait_ge(w_lo_ok, n + 1)
            eng.dma_start(w_raw[:, s, :], w_qkv[bass.ds(n, 1), :, :].rearrange("a p n -> p (a n)"))\
               .then_inc(w_in[s], 16)

        @block.sync
        def _(sp):
            load_w(sp, 0, 0, 0)
            for k in range(KD):
                sp.wait_ge(x_lo_ok, k + 1)
                sp.dma_start(x_raw[:, k % 2, :], x_cols[:, k, :]).then_inc(x_in[k % 2], 16)
            load_w(sp, 1, 0, 1)
            with sp.Fori(1, nblk // 2) as i:
                for s in range(2):
                    load_w(sp, i * 2 + s, i, s)
            for s in range(2):
                sp.wait_ge(w_lo_ok, nblk + 1 + s)
            with sp.Fori(0, FB) as f:
                for s in range(2):
                    sp.wait_ge(side_used, f * 2 + 1)
                    sp.dma_start(w_raw[:, s, :], w_cxb[bass.ds(f * 3 + s, 1), :, :].rearrange("a p n -> p (a n)"))\
                      .then_inc(side_in[s], 16)

        @block.gpsimd
        def _(pool):
            for s in (side_used, u_row_ok):
                pool.sem_inc(s, 1)
            for j, s in enumerate(stored):
                pool.dma_start(scrap[:, j:j + 1], a["ln"][0:1, 0:1]).then_inc(s, 16)
            pool.memset(ident[:, :], 0.0).then_inc(ident_ok, 1)
            pool.wait_ge(ident_ok, 1)
            pool.affine_select(out=ident[:, :], in_=ident[:, :], compare_op=ALU.not_equal, fill=1.0, base=0,
                               pattern=[[-1, P]], channel_multiplier=1).then_inc(ident_ok, 1)
            with pool.Fori(0, nblk // 2) as i:
                for s in range(2):
                    pool.wait_ge(ev_act, i * 2 + s + 3)
                    pool.wait_ge(ev_dve, i * 2 + s + 3)
                    pool.dma_start(qkv[bass.ds(i * 2 + s, 1), :, :].rearrange("a p n -> p (a n)"),
                                   res[:, s, :]).then_inc(stored[s], 16)
            for s in range(2):
                pool.wait_ge(stored[s], 16 * (nblk // 2) + 16)

        @block.scalar
        def _(act):
            act.sem_inc(ev_act, 2)

            def high(n, i, s):
                act.wait_ge(w_in[s], i * 16 + 16)
                act.wait_ge(w_used, n + 1)
                act.activation(w_hi[:, s, :], w_raw[:, s, :], ACT.Copy).then_inc(w_hi_ok, 1)

            def copy_out(n, i, s, scale):
                act.wait_ge(w_used, n + 3)
                act.wait_ge(stored[s], i * 16 + 16)
                for t in range(2):
                    last = act.activation(res[:, s, cols[t]], bank[s][t][:, :], ACT.Copy, scale=scale)
                last.then_inc(ev_act, 1)

            high(0, 0, 0)
            for k in range(KD):
                act.wait_ge(x_in[k % 2], 16 * (k // 2 + 1))
                act.activation(x_hi[:, k, :], x_raw[:, k % 2, :], ACT.Copy).then_inc(x_hi_ok, 1)
            with act.Fori(0, nq // 2) as i:
                high(i * 2 + 1, i, 1)
                copy_out(i * 2, i, 0, DH ** -0.5)
                high(i * 2 + 2, i + 1, 0)
                copy_out(i * 2 + 1, i, 1, DH ** -0.5)
            with act.Fori(nq // 2, nblk // 2 - 1) as i:
                high(i * 2 + 1, i, 1)
                copy_out(i * 2, i, 0, 1.0)
                high(i * 2 + 2, i + 1, 0)
                copy_out(i * 2 + 1, i, 1, 1.0)
            i = nblk // 2 - 1
            high(2 * i + 1, i, 1)
            copy_out(2 * i, i, 0, 1.0)
            copy_out(2 * i + 1, i, 1, 1.0)

        @block.vector
        def _(dve):
            dve.sem_inc(w_lo_ok, 2)
            dve.sem_inc(x_lo_ok, 2)
            dve.sem_inc(ev_dve, 2)

            def low(n, i, s):
                dve.wait_ge(w_hi_ok, n + 1)
                dve.wait_ge(w_used, n + 1)
                dve.tensor_tensor(w_lo[:, s, :], w_raw[:, s, :], w_hi[:, s, :].bitcast(F32), ALU.subtract)\
                   .then_inc(w_lo_ok, 1)

            def copy_out(n, i, s, scale):
                dve.wait_ge(w_used, n + 3)
                dve.wait_ge(stored[s], i * 16 + 16)
                for t in range(2, 4):
                    ps = bank[s][t][:, 0:cols[t].stop - cols[t].start]
                    last = dve.tensor_scalar(res[:, s, cols[t]], ps, scale, None, ALU.mult)
                last.then_inc(ev_dve, 1)

            low(0, 0, 0)
            for k in range(KD):
                dve.wait_ge(x_hi_ok, k + 1)
                dve.tensor_copy(x_side[:, k, :], x_raw[:, k % 2, beside]).then_inc(x_side_ok, 1)
                dve.tensor_tensor(x_lo[:, k, :], x_raw[:, k % 2, :], x_hi[:, k, :].bitcast(F32), ALU.subtract)\
                   .then_inc(x_lo_ok, 1)
            with dve.Fori(0, nq // 2) as i:
                low(i * 2 + 1, i, 1)
                copy_out(i * 2, i, 0, DH ** -0.5)
                low(i * 2 + 2, i + 1, 0)
                copy_out(i * 2 + 1, i, 1, DH ** -0.5)
            with dve.Fori(nq // 2, nblk // 2 - 1) as i:
                low(i * 2 + 1, i, 1)
                copy_out(i * 2, i, 0, 1.0)
                low(i * 2 + 2, i + 1, 0)
                copy_out(i * 2 + 1, i, 1, 1.0)
            i = nblk // 2 - 1
            low(2 * i + 1, i, 1)
            copy_out(2 * i, i, 0, 1.0)
            copy_out(2 * i + 1, i, 1, 1.0)
            with dve.Fori(0, FB) as f:
                dve.wait_ge(side_used, f * 2 + 2)
                dve.wait_ge(u_row_ok, f + 1)
                dve.tensor_copy(c_row[:, :], bank[0][3][0:2, 0:P]).then_inc(c_row_ok, 1)
                dve.wait_ge(side_used, f * 2 + 3)
                dve.wait_ge(c_row_ok, f + 1)
                dve.tensor_tensor(u_row[:, bass.ds(f * P, P)], c_row[:, :], bank[1][3][0:2, 0:P], ALU.mult)\
                   .then_inc(u_row_ok, 1)
            cols_ps = bank[0][0][:, 0:2 * FB].rearrange("p (f c) -> p f c", c=2)
            edge = edges[:, :].rearrange("p (f s) -> p f s", s=NEDGE)
            dve.memset(edges[:, :], 0.0).then_inc(edge_ok, 1)
            dve.wait_ge(edge_ok, 1)
            dve.wait_ge(u_col_ok, 1)
            for slot, col in ((RIGHT, 0), (0, 1), (4, 1)):
                dve.tensor_copy(edge[:, :, slot], cols_ps[:, :, col]).then_inc(edge_ok, 1)

        @block.tensor
        def _(pe):
            pe.sem_inc(w_used, 2)

            def project(n, s, first=False):
                pe.wait_ge(w_lo_ok, n + 3)
                pe.wait_ge(ev_act, n + 1)
                pe.wait_ge(ev_dve, n + 1)
                for k in range(KD):
                    if first:
                        pe.wait_ge(x_lo_ok, k + 3)
                    w = slice(k * P, (k + 1) * P)
                    for t in range(4):
                        ps = bank[s][t][:, 0:cols[t].stop - cols[t].start]
                        pe.matmul(ps, w_hi[:, s, w], x_hi[:, k, cols[t]], start=(k == 0), stop=False)
                        pe.matmul(ps, w_hi[:, s, w], x_lo[:, k, cols[t]], start=False, stop=False)
                        last = pe.matmul(ps, w_lo[:, s, w], x_hi[:, k, cols[t]], start=False, stop=(k == KD - 1))
                last.then_inc(w_used, 1)

            project(0, 0, first=True)
            project(1, 1)
            with pe.Fori(1, nblk // 2) as i:
                for s in range(2):
                    project(i * 2 + s, s)
            pe.wait_ge(ev_dve, nblk + 2)
            pe.wait_ge(ev_act, nblk + 2)
            pe.wait_ge(x_side_ok, KD)
            with pe.Fori(0, FB) as f:
                for s in range(2):
                    pe.wait_ge(side_in[s], f * 16 + 16)
                    pe.wait_ge(u_row_ok, f + 1)
                    for k in range(KD):
                        last = pe.matmul(bank[s][3][0:2, 0:P], x_side[:, k, :], w_raw[:, s, k * P:(k + 1) * P],
                                         start=(k == 0), stop=(k == KD - 1))
                    last.then_inc(side_used, 1)
            pe.wait_ge(ident_ok, 2)
            pe.wait_ge(u_row_ok, FB + 1)
            for f in range(FB):
                last = pe.matmul(bank[0][0][:, 2 * f:2 * f + 2], u_row[:, f * P:(f + 1) * P], ident[0:2, 0:2],
                                 start=True, stop=True)
            last.then_inc(u_col_ok, 1)


def attention_schedule():
    chunk = 0
    for cb in range(NCB):
        for step, gap in (("scores", 5), ("turn0", 3), ("turn1", 3)):
            yield step, cb
            for chunk in range(chunk, chunk + gap):
                yield "chunk", divmod(chunk, KD)
            chunk += 1
    for step in ("drain_values", "drain_turn"):
        yield step, NCB - 1
        for chunk in range(chunk, chunk + 2):
            yield "chunk", divmod(chunk, KD)
        chunk += 1


KB_DMAS = 2 + ROWS_T
NPAIR = N_CXB // HP


def o_block(t, p, cb):
    at = t[:, bass.ds(p * TILE, TILE)].rearrange("p (r c) -> p r c", c=GRID)
    return at[:, :, cb * 16:cb * 16 + 16]


def out_banks(bank, half):
    return bank[3:7] if half == 0 else [bank[0], bank[1], bank[2], bank[7]]


def mixer(nc, a, qkv, edges, ident, logits, h_rows):
    with ExitStack() as ctx:
        sb = lambda n, s, d=F32: ctx.enter_context(nc.sbuf_tensor(n, s, d))
        sem = lambda n: ctx.enter_context(nc.semaphore(n))
        x_raw = sb("x_raw", [P, 2, 2 * TILE])
        x_hi, x_lo = sb("x_hi", [P, KD, TILE], F32R), sb("x_lo", [P, KD, TILE], F32R)
        o_hi, o_lo = sb("o_hi", [P, HP * TILE], F32R), sb("o_lo", [P, HP * TILE], F32R)
        y_hi, y_lo = sb("y_hi", [P, FB * TILE], F32R), sb("y_lo", [P, FB * TILE], F32R)
        w_raw = sb("w_raw", [P, 2, D])
        w_hi, w_lo = sb("w_hi", [P, 2, D], F32R), sb("w_lo", [P, 2, D], F32R)
        conv_wb = sb("conv_wb_sb", [P, 4 * FB])
        w_router = sb("w_router_sb", [P, KD, NLOG])
        ln_g, ln_b = sb("ln1_g", [P, D]), sb("ln1_b", [P, D])
        ident_b = sb("ident_b", [P, P], BF16)
        zeros = sb("zeros", [P, NMETA])
        neg_half = sb("neg_half", [P, SUB_T])
        first = ExitStack()
        sa = lambda n, s, d=F32: first.enter_context(nc.sbuf_tensor(n, s, d))
        q, q_cut = sa("q", [P, TILE]), sa("q_cut", [P, TILE])
        v_cut = sa("v_cut", [P, NCB * NKEY])
        key = sa("key", [P, KROWS * GRID + NMETA])
        val = sa("val", [P, KROWS * GRID + NMETA])
        bias = sa("bias", [P, 2, KROWS * GRID])
        mask = sa("mask", [P, NCB * NKEY], BF16)
        sbias = sa("sbias", [P, 2, NKEY + NMETA])
        prob = sa("prob", [P, 2, 512])
        prob_t = sa("prob_t", [P, 2, 512])
        vkeys = sa("vkeys", [P, 2, NKEY])
        vmeta = sa("vmeta", [NMETA, P])
        o_rows = sa("o_rows", [P, P])
        small = sa("small", [P, 10])
        smeta, smax, nmax, ssum, rsum = (small[:, 2 * j:2 * j + 2] for j in range(5))
        c_sb = sa("c_sb", [P, TILE])
        u = sa("u", [P, TILE + 2])
        y = sa("y", [P, TILE])
        first.close()
        second = ExitStack()
        sa = lambda n, s, d=F32: second.enter_context(nc.sbuf_tensor(n, s, d))
        m_hi, m_lo = sa("m_hi", [P, FB * TILE], F32R), sa("m_lo", [P, FB * TILE], F32R)
        sig_a, sig_c, m_att = sa("sig_a", [P, TILE]), sa("sig_c", [P, TILE]), sa("m_att", [P, TILE])
        rows = sa("rows", [P, SUB_T, D])
        h_t = sa("h_t", [P, D])
        stats = sa("stats", [P, 12])
        mom = sa("mom", [P, SUB_T * 3]).rearrange("p (s m) -> p s m", m=3)
        second.close()
        bank = [ctx.enter_context(nc.psum_tensor(f"bank{j}", [P, 512], F32)) for j in range(8)]
        score, turned, outp = bank[3:5], bank[5], bank[6]

        const_in = sem("const_in")
        const_ok = sem("const_ok")
        x_in = [sem(f"x_in{j}") for j in range(2)]
        x_hi_ok, x_lo_ok = sem("x_hi_ok"), sem("x_lo_ok")
        w_in = [sem(f"w_in{j}") for j in range(2)]
        w_hi_ok, w_lo_ok = sem("w_hi_ok"), sem("w_lo_ok")
        w_used = sem("w_used")
        qv_in = sem("qv_in")
        kb_in = sem("kb_in")
        q_cut_ok = sem("q_cut_ok")
        v_cut_ok = sem("v_cut_ok")
        mask_in = sem("mask_in")
        rows_in = sem("rows_in")
        scores_ok = sem("scores_ok")
        max_step = sem("max_step")
        max_ok = sem("max_ok")
        exp_ok = sem("exp_ok")
        sum_ok = sem("sum_ok")
        turn_ok = sem("turn_ok")
        prob_t_ok = [sem("prob_t0_ok"), sem("prob_t1_ok")]
        vturn_ok, vkeys_ok = sem("vturn_ok"), sem("vkeys_ok")
        pv_ok = sem("pv_ok")
        o_ok = sem("o_ok")
        oturn_ok = sem("oturn_ok")
        o_hi_ok, o_lo_ok = sem("o_hi_ok"), sem("o_lo_ok")
        c_ok = sem("c_ok")
        conv_step = sem("conv_step")
        y_hi_ok, y_lo_ok = sem("y_hi_ok"), sem("y_lo_ok")
        sig_a_ok, sig_c_ok = sem("sig_a_ok"), sem("sig_c_ok")
        m_step = sem("m_step")
        m_hi_ok, m_lo_ok = sem("m_hi_ok"), sem("m_lo_ok")
        res_step = sem("res_step")
        mom_ok = sem("mom_ok")
        var_ok = sem("var_ok")
        rstd_ok = sem("rstd_ok")
        norm_ok = sem("norm_ok")
        aff_step = sem("aff_step")
        hturn_ok = sem("hturn_ok")
        h_t_ok = [sem("h_t0_ok"), sem("h_t1_ok")]
        log_ok = sem("log_ok")
        log_out = sem("log_out")
        stored = sem("h_stored")
        res_bn = sem("res_bn")

        def window(cb, j0=0, j1=KROWS):
            return slice(j0, j1), slice(key_start(cb), key_start(cb) + KCOLS)

        def grid(t):
            return t.rearrange("p (r c) -> p r c", c=GRID)

        scrap = sb("mix_scrap", [1, 4])
        block = ctx.enter_context(nc.Block())

        @block.sync
        def _(sp):
            def load(n, half, src, width=D):
                sp.wait_ge(w_lo_ok, n + 1)
                sp.dma_start(w_raw[:, half % 2, 0:width], src.rearrange("a p n -> p (a n)"))\
                  .then_inc(w_in[half % 2], 16)

            with sp.Fori(0, NT) as t:
                for j in range(4):
                    sp.wait_ge(x_lo_ok, t * 4 + j + 1)
                    sp.dma_start(x_raw[:, j % 2, :].rearrange("p (k n) -> p k n", k=2),
                                 a["x_cols"][:, 2 * j:2 * j + 2, bass.ds(t * TILE, TILE)]).then_inc(x_in[j % 2], 16)
                with sp.Fori(0, HP) as p:
                    for j in range(NPAIR):
                        load(t * N_TILE + p * NPAIR + j, j, a["w_cxb"][bass.ds(p * NPAIR + j, 1), :, :])
                with sp.Fori(0, FB) as f:
                    n = t * N_TILE + N_CXB + f * 4
                    load(n, 0, a["w_gates"][bass.ds(f * 3, 1), :, :])
                    load(n + 1, 1, a["w_att"][bass.ds(f, 1), :, :], HP * P)
                    load(n + 2, 2, a["w_gates"][bass.ds(f * 3 + 1, 1), :, :])
                    load(n + 3, 3, a["w_gates"][bass.ds(f * 3 + 2, 1), :, :])
                for j in range(N_OUT):
                    load(t * N_TILE + N_CXB + N_MERGE + j, j, a["w_out"][j:j + 1, :, :])

        @block.gpsimd
        def _(pool):
            for s in (c_ok, conv_step, *h_t_ok, hturn_ok, log_out, m_hi_ok, m_step, mom_ok, o_lo_ok, oturn_ok, *prob_t_ok, pv_ok, q_cut_ok, scores_ok, sig_a_ok, sig_c_ok, v_cut_ok, vturn_ok, y_lo_ok):
                pool.sem_inc(s, 1)
            for j, s in enumerate((stored,)):
                pool.dma_start(scrap[:, j:j + 1], a["ln"][0:1, 0:1]).then_inc(s, 16)
            pool.tensor_copy(ident_b[:, :], ident[:, :]).then_inc(const_ok, 1)
            pool.memset(zeros[:, :], 0.0).then_inc(const_ok, 1)
            pool.memset(neg_half[:, :], -0.5).then_inc(const_ok, 1)
            pool.dma_start(conv_wb[:, :], a["conv_wb"]).then_inc(const_in, 16)
            pool.dma_start(w_router[:, :, :].rearrange("p k n -> p (k n)"), a["w_router"]).then_inc(const_in, 16)
            pool.dma_start(ln_g[:, :], a["ln"][0:1, :].broadcast_to([P, D])).then_inc(const_in, 16)
            pool.dma_start(ln_b[:, :], a["ln"][1:2, :].broadcast_to([P, D])).then_inc(const_in, 16)
            with pool.Fori(0, NT) as t:
                base = t * 4 + (t // 2) * 4
                out, turned_rows = pool.to_reg(t * SUB_T * 16 + 16), pool.to_reg(t * SUB_T + 1)
                pool.wait_ge(const_ok, 3)
                pool.wait_ge(stored, out)
                pool.wait_ge(hturn_ok, turned_rows)
                pool.wait_ge(log_out, turned_rows)
                pool.memset(prob[:, :, NKEY + NMETA:512], 0.0).then_inc(const_ok, 1)
                pool.dma_start(mask[:, :], a["masks"].bitcast(BF16)[bass.ds(t, 1), :, :].rearrange("a p n -> p (a n)"))\
                    .then_inc(mask_in, 16)
                with pool.Fori(0, HP) as p:
                    g = t * HP + p
                    pool.wait_ge(q_cut_ok, g + 1)
                    pool.dma_start(q[:, :], qkv[bass.ds(p, 1), :, bass.ds(t * TILE, TILE)]
                                   .rearrange("a p n -> p (a n)")).then_inc(qv_in, 16)

                    def load_window(dst, first, landed):
                        pool.dma_start(dst[:, 0:KROWS * GRID],
                                       qkv[bass.ds(p + first, 1), :, bass.ds(base * GRID, KROWS * GRID)]
                                       .rearrange("a p n -> p (a n)")).then_inc(landed, 16)
                        pool.dma_start(dst[:, KROWS * GRID:], qkv[bass.ds(p + first, 1), :, NTOK:NCOL]
                                       .rearrange("a p n -> p (a n)")).then_inc(landed, 16)

                    pool.wait_ge(v_cut_ok, g * NCB + 1)
                    pool.wait_ge(vturn_ok, g * NCB + 1)
                    load_window(val, 2 * HP, qv_in)
                    pool.wait_ge(max_ok, g * 2 * NCB + 2)
                    pool.wait_ge(scores_ok, g * 2 * NCB + 1)
                    load_window(key, HP, kb_in)
                    for r in range(ROWS_T):
                        at = (2 - t) // 2 * (4 * 64) + (ROWS_T - 1 - r) * 64
                        pool.dma_start(bias[r * 16:r * 16 + 16, :, :],
                                       a["bias_planes"][bass.ds(p * 2, 2), :, bass.ds(at, KROWS * GRID)]
                                       .rearrange("h i n -> i h n")).then_inc(kb_in, 16)
                    landed = pool.to_reg(g * 48 + 48)
                    pool.wait_ge(const_ok, 3)
                    pool.wait_ge(qv_in, landed)
                    pool.wait_ge(scores_ok, pool.to_reg(g * 2 * NCB + 1))
                    pool.tensor_copy(q_cut[:, :].rearrange("p (b r i) -> p r b i", b=NCB, r=ROWS_T),
                                     q[:, :].rearrange("p (r b i) -> p r b i", b=NCB, r=ROWS_T)).then_inc(q_cut_ok, 1)
                    for cb in range(NCB):
                        pool.tensor_copy(v_cut[:, cb * NKEY:(cb + 1) * NKEY].rearrange("p (r c) -> p r c", c=KCOLS),
                                         grid(val[:, 0:KROWS * GRID])[:, :, key_start(cb):key_start(cb) + KCOLS])\
                            .then_inc(v_cut_ok, 1)
                pool.wait_ge(y_lo_ok, t * FB + FB + 1)
                pool.wait_ge(o_lo_ok, t * 16 + 17)
                pool.dma_start(rows[:, :, :], a["x_rows"][bass.ds(t * TILE, TILE), :]
                               .rearrange("(s p) n -> p s n", p=P)).then_inc(rows_in, 16)
                known = pool.to_reg(t * SUB_T + SUB_T + 1)
                pool.wait_ge(const_ok, 3)
                pool.wait_ge(mom_ok, known)
                pool.tensor_scalar(mom[:, :, 1], mom[:, :, 1], EPS, None, ALU.add).then_inc(var_ok, 1)
                pool.wait_ge(var_ok, t + 1)
                pool.tensor_tensor(mom[:, :, 2], mom[:, :, 1], neg_half[:, :], ALU.pow).then_inc(rstd_ok, 1)
                for s in range(SUB_T):
                    c = t * SUB_T + s
                    pool.wait_ge(const_in, 64)
                    pool.wait_ge(norm_ok, c + 1)
                    pool.tensor_tensor(rows[:, s, :], rows[:, s, :], ln_g[:, :], ALU.mult).then_inc(aff_step, 1)
                    pool.wait_ge(aff_step, c * 2 + 1)
                    pool.tensor_tensor(rows[:, s, :], rows[:, s, :], ln_b[:, :], ALU.add).then_inc(aff_step, 1)
                    pool.wait_ge(aff_step, c * 2 + 2)
                    pool.dma_start(h_rows[bass.ds(c * P, P), :], rows[:, s, :]).then_inc(stored, 16)
            pool.wait_ge(stored, NSUB * 16 + 16)

        @block.scalar
        def _(act):
            for s in (max_ok, exp_ok, sum_ok, turn_ok, pv_ok, o_ok):
                act.sem_inc(s, 2)

            def high(n, half, width=D):
                act.wait_ge(w_in[half % 2], (n // 2) * 16 + 16)
                act.wait_ge(w_used, n + 1)
                act.activation(w_hi[:, half % 2, 0:width], w_raw[:, half % 2, 0:width], ACT.Copy)\
                   .then_inc(w_hi_ok, 1)

            with act.Fori(0, NT) as t:
                n0 = t * N_TILE
                act.wait_ge(w_used, n0 + 2)
                for j in range(4):
                    act.wait_ge(x_in[j % 2], t * 32 + (j // 2) * 16 + 16)
                    act.activation(x_hi[:, 2 * j:2 * j + 2, :].rearrange("p k n -> p (k n)"),
                                   x_raw[:, j % 2, :], ACT.Copy).then_inc(x_hi_ok, 1)
                high(n0, 0)
                with act.Fori(0, HP) as p:
                    g = t * HP + p

                    def out_rows(cb, h):
                        u2 = (g * NCB + cb) * 2 + h
                        act.wait_ge(pv_ok, u2 + 4)
                        act.wait_ge(sum_ok, u2 + 3)
                        act.wait_ge(oturn_ok, g * NCB + cb + 1)
                        act.activation(o_rows[:, h * DH:(h + 1) * DH], outp[:, h * DH:(h + 1) * DH], ACT.Copy,
                                       scale=rsum[:, h:h + 1]).then_inc(o_ok, 1)

                    def out_high(cb):
                        act.wait_ge(oturn_ok, g * NCB + cb + 2)
                        act.activation(o_block(o_hi, p, cb),
                                       outp[:, P:2 * P].rearrange("p (r c) -> p r c", c=16), ACT.Copy)\
                           .then_inc(o_hi_ok, 1)

                    def y_high(f):
                        act.wait_ge(conv_step, (g * 2 + f) * 8 + 9)
                        act.activation(y_hi[:, bass.ds((p * 2 + f) * TILE, TILE)], y[:, :], ACT.Copy)\
                           .then_inc(y_hi_ok, 1)

                    for step, at in attention_schedule():
                        if step == "scores":
                            unit = g * NCB + at
                            if at:
                                out_rows(at - 1, 1)
                            act.wait_ge(vturn_ok, unit + 2)
                            act.wait_ge(pv_ok, unit * 2 + 1)
                            if at == 0:
                                act.activation(vmeta[:, :], turned[0:NMETA, NKEY:512], ACT.Copy)
                            act.activation(vkeys[:, at % 2, :], turned[:, 0:NKEY], ACT.Copy).then_inc(vkeys_ok, 1)
                            for h in range(2):
                                act.wait_ge(const_ok, t + 4)
                                act.wait_ge(max_ok, unit * 2 + h + 3)
                                act.wait_ge(turn_ok, unit * 2 + h + 1)
                                act.wait_ge(sum_ok, unit * 2 + h + 1)
                                act.activation(prob[:, h, 0:NKEY + NMETA], sbias[:, h, :], ACT.Exp,
                                               bias=nmax[:, h:h + 1], accum_out=ssum[:, h:h + 1])\
                                   .then_inc(exp_ok, 1)
                        elif step == "turn0":
                            if at:
                                out_high(at - 1)
                        elif step == "turn1":
                            unit = g * NCB + at
                            act.wait_ge(turn_ok, unit * 2 + 4)
                            act.wait_ge(pv_ok, unit * 2 + 3)
                            act.activation(prob_t[:, 1, :], turned[:, :], ACT.Copy).then_inc(prob_t_ok[1], 1)
                            out_rows(at, 0)
                        elif step == "drain_values":
                            out_rows(at, 1)
                        elif step == "drain_turn":
                            out_high(at)
                        else:
                            grp, k = at
                            n = n0 + p * NPAIR + grp
                            if k == 0:
                                high(n + 1, grp + 1)
                            if grp == 3 and k == 2:
                                y_high(0)
                            if grp % 3 == 0 and k == KD - 1:
                                f = g * 2 + grp // 3
                                act.wait_ge(w_used, n + 3)
                                act.wait_ge(conv_step, f * 8 + 1)
                                act.activation(c_sb[:, :], bank[0][:, :], ACT.Copy).then_inc(c_ok, 1)
                    y_high(1)
                with act.Fori(0, FB) as f:
                    n, m = n0 + N_CXB + f * 4, t * FB + f
                    high(n + 1, 1, HP * P)
                    act.wait_ge(w_used, n + 3)
                    act.wait_ge(y_lo_ok, t * FB + FB + 1)
                    act.wait_ge(o_lo_ok, t * 16 + 17)
                    act.wait_ge(m_step, m * 3 + 1)
                    act.activation(sig_a[:, :], bank[0][:, :], ACT.Sigmoid).then_inc(sig_a_ok, 1)
                    high(n + 2, 2)
                    high(n + 3, 3)
                    act.wait_ge(w_used, n + 5)
                    act.activation(sig_c[:, :], bank[2][:, :], ACT.Sigmoid).then_inc(sig_c_ok, 1)
                    high(n + 4, 4)
                    act.wait_ge(m_step, m * 3 + 4)
                    act.activation(m_hi[:, bass.ds(f * TILE, TILE)], m_att[:, :], ACT.Copy).then_inc(m_hi_ok, 1)
                for j in range(1, N_OUT):
                    high(n0 + N_CXB + N_MERGE + j, j)
                for s in range(SUB_T):
                    c = t * SUB_T + s
                    act.wait_ge(hturn_ok, c + 2)
                    act.activation(h_t[:, 0:512], bank[3][:, :], ACT.Copy).then_inc(h_t_ok[0], 1)
                    act.wait_ge(log_ok, c + 1)
                    act.activation(logits[:, bass.ds(c * NLOG, NLOG)], bank[5][:, 0:NLOG], ACT.Copy)\
                       .then_inc(log_out, 1)

        @block.vector
        def _(dve):
            dve.sem_inc(w_lo_ok, 2)
            dve.sem_inc(x_lo_ok, 2)
            dve.wait_ge(const_in, 64)

            def low(n, half, width=D):
                dve.wait_ge(w_hi_ok, n + 1)
                dve.wait_ge(w_used, n + 1)
                dve.tensor_tensor(w_lo[:, half % 2, 0:width], w_raw[:, half % 2, 0:width],
                                  w_hi[:, half % 2, 0:width].bitcast(F32), ALU.subtract).then_inc(w_lo_ok, 1)

            with dve.Fori(0, NT) as t:
                n0 = t * N_TILE
                for j in range(4):
                    dve.wait_ge(x_hi_ok, t * 4 + j + 1)
                    dve.wait_ge(w_used, n0 + 2)
                    dve.tensor_tensor(x_lo[:, 2 * j:2 * j + 2, :].rearrange("p k n -> p (k n)"), x_raw[:, j % 2, :],
                                      x_hi[:, 2 * j:2 * j + 2, :].rearrange("p k n -> p (k n)").bitcast(F32),
                                      ALU.subtract).then_inc(x_lo_ok, 1)
                low(n0, 0)
                with dve.Fori(0, HP) as p:
                    g = t * HP + p

                    def one_over_sum(cb, h):
                        u2 = (g * NCB + cb) * 2 + h
                        dve.wait_ge(exp_ok, u2 + 3)
                        dve.wait_ge(o_ok, u2 + 1)
                        dve.reciprocal(rsum[:, h:h + 1], ssum[:, h:h + 1]).then_inc(sum_ok, 1)

                    def out_low(cb):
                        dve.wait_ge(o_hi_ok, g * NCB + cb + 1)
                        dve.tensor_tensor(o_block(o_lo, p, cb),
                                          outp[:, P:2 * P].rearrange("p (r c) -> p r c", c=16),
                                          o_block(o_hi, p, cb).bitcast(F32), ALU.subtract).then_inc(o_lo_ok, 1)

                    def y_low(f):
                        dve.wait_ge(y_hi_ok, g * 2 + f + 1)
                        at = bass.ds((p * 2 + f) * TILE, TILE)
                        dve.tensor_tensor(y_lo[:, at], y[:, :], y_hi[:, at].bitcast(F32), ALU.subtract)\
                           .then_inc(y_lo_ok, 1)

                    for step, at in attention_schedule():
                        if step == "scores":
                            for h in range(2):
                                u2 = (g * NCB + at) * 2 + h
                                here, used = dve.to_reg(u2 + 2), dve.to_reg(u2 + 1)
                                dve.wait_ge(const_ok, 3)
                                dve.wait_ge(scores_ok, here)
                                dve.wait_ge(exp_ok, used)
                                dve.tensor_tensor_reduce(
                                    out=sbias[:, h, NKEY:], in0=score[h][:, NKEY:NKEY + NMETA], in1=zeros[:, :],
                                    scale=1.0, scalar=NEG, op0=ALU.add, op1=ALU.max,
                                    accum_out=smeta[:, h:h + 1]).then_inc(max_step, 1)
                                meta_done, landed = dve.to_reg(u2 * 2 + 1), dve.to_reg((g + 1) * KB_DMAS * 16)
                                dve.wait_ge(const_ok, 3)
                                dve.wait_ge(max_step, meta_done)
                                dve.wait_ge(kb_in, landed)
                                dve.tensor_tensor_reduce(
                                    out=sbias[:, h, 0:NKEY].rearrange("p (r c) -> p r c", c=KCOLS),
                                    in0=score[h][:, 0:NKEY].rearrange("p (r c) -> p r c", c=KCOLS),
                                    in1=bias[:, h, :].rearrange("p (r c) -> p r c", c=64)
                                    [:, :, 16 + key_start(at) - 16 * at:][:, :, 0:KCOLS],
                                    scale=1.0, scalar=smeta[:, h:h + 1], op0=ALU.add, op1=ALU.max,
                                    accum_out=smax[:, h:h + 1]).then_inc(max_step, 1)
                                dve.wait_ge(max_step, u2 * 2 + 2)
                                dve.tensor_scalar(nmax[:, h:h + 1], smax[:, h:h + 1], -1.0, None, ALU.mult)\
                                   .then_inc(max_ok, 1)
                        elif step == "turn0":
                            one_over_sum(at, 0)
                            unit = g * NCB + at
                            dve.wait_ge(turn_ok, unit * 2 + 3)
                            dve.wait_ge(pv_ok, unit * 2 + 2)
                            dve.tensor_copy(prob_t[:, 0, :], turned[:, :]).then_inc(prob_t_ok[0], 1)
                        elif step == "turn1":
                            if at:
                                out_low(at - 1)
                            one_over_sum(at, 1)
                        elif step == "drain_turn":
                            out_low(at)
                        elif step == "chunk":
                            grp, k = at
                            n = n0 + p * NPAIR + grp
                            f = g * 2 + grp // 3
                            wb = lambda j: conv_wb[:, bass.ds(p * 8 + grp // 3 * 4 + j, 1)]
                            edge = lambda e: edges[:, bass.ds((p * 2 + grp // 3) * NEDGE + e, 1)]
                            if k == 0:
                                low(n + 1, grp + 1)
                            if grp == 3 and k == 3:
                                y_low(0)
                            if k == KD - 1 and grp % 3 == 1:
                                dve.wait_ge(w_used, n + 3)
                                dve.wait_ge(c_ok, f + 2)
                                dve.tensor_tensor(u[:, 1:TILE + 1], c_sb[:, :], bank[1][:, :], ALU.mult)\
                                   .then_inc(conv_step, 1)
                                dve.tensor_copy(u[:, 0:1], edge(t * 2)).then_inc(conv_step, 1)
                                dve.tensor_copy(u[:, TILE + 1:], edge(t + RIGHT)).then_inc(conv_step, 1)
                                dve.wait_ge(conv_step, f * 8 + 4)
                                dve.tensor_copy(edge(t * 3 + 2), u[:, TILE:TILE + 1]).then_inc(conv_step, 1)
                                dve.wait_ge(y_lo_ok, f + 1)
                                dve.tensor_scalar(y[:, :], u[:, 0:TILE], wb(0), wb(3), ALU.mult, ALU.add)\
                                   .then_inc(conv_step, 1)
                                for j in (1, 2):
                                    dve.wait_ge(conv_step, f * 8 + 4 + j + 1)
                                    dve.scalar_tensor_tensor(y[:, :], u[:, j:TILE + j], wb(j), y[:, :], ALU.mult, ALU.add)\
                                       .then_inc(conv_step, 1)
                            if k == KD - 1 and grp % 3 == 2:
                                dve.wait_ge(w_used, n + 3)
                                dve.wait_ge(conv_step, f * 8 + 8)
                                dve.tensor_tensor(y[:, :], y[:, :], bank[2][:, :], ALU.mult).then_inc(conv_step, 1)
                    y_low(1)
                with dve.Fori(0, FB) as f:
                    n, m = n0 + N_CXB + f * 4, t * FB + f
                    low(n + 1, 1, HP * P)
                    low(n + 2, 2)
                    dve.wait_ge(w_used, n + 4)
                    dve.wait_ge(sig_a_ok, m + 2)
                    dve.wait_ge(m_hi_ok, m + 1)
                    dve.tensor_tensor(m_att[:, :], sig_a[:, :], bank[1][:, :], ALU.mult).then_inc(m_step, 1)
                    low(n + 3, 3)
                    low(n + 4, 4)
                    dve.wait_ge(w_used, n + 6)
                    dve.wait_ge(sig_c_ok, m + 2)
                    dve.tensor_tensor(sig_c[:, :], sig_c[:, :], bank[7][:, :], ALU.mult).then_inc(m_step, 1)
                    dve.wait_ge(m_step, m * 3 + 3)
                    dve.tensor_tensor(m_att[:, :], m_att[:, :], sig_c[:, :], ALU.add).then_inc(m_step, 1)
                    dve.wait_ge(m_hi_ok, m + 2)
                    at = bass.ds(f * TILE, TILE)
                    dve.tensor_tensor(m_lo[:, at], m_att[:, :], m_hi[:, at].bitcast(F32), ALU.subtract)\
                       .then_inc(m_lo_ok, 1)
                n1 = n0 + N_CXB + N_MERGE
                for half in range(2):
                    for j in range(4 * half, 4 * half + 4):
                        if j + 1 < N_OUT:
                            low(n1 + j + 1, j + 1)
                    dve.wait_ge(w_used, n1 + 4 * half + 6)
                    dve.wait_ge(rows_in, t * 16 + 16)
                    for s in range(SUB_T):
                        r = rows[:, s, half * 512:(half + 1) * 512]
                        dve.scalar_tensor_tensor(r, r, ALPHA, out_banks(bank, half)[s][:, :], ALU.mult, ALU.add)\
                           .then_inc(res_step, 1)
                for s in range(SUB_T):
                    c = t * SUB_T + s
                    dve.wait_ge(res_step, t * 8 + 5 + s)
                    dve.wait_ge(mom_ok, c + 1)
                    for half in range(2):
                        dve.bn_stats(stats[:, half * 6:half * 6 + 6], rows[:, s, half * 512:(half + 1) * 512])\
                           .then_inc(res_bn, 1)
                    taken = dve.to_reg(c * 2 + 2)
                    dve.wait_ge(const_in, 64)
                    dve.wait_ge(res_bn, taken)
                    dve.bn_aggr(mom[:, s, 0:2], stats[:, :]).then_inc(mom_ok, 1)
                for s in range(SUB_T):
                    dve.wait_ge(rstd_ok, t + 1)
                    dve.tensor_scalar(rows[:, s, :], rows[:, s, :], mom[:, s, 0:1], mom[:, s, 2:3],
                                      ALU.subtract, ALU.mult).then_inc(norm_ok, 1)
                for s in range(SUB_T):
                    dve.wait_ge(hturn_ok, t * SUB_T + s + 2)
                    dve.tensor_copy(h_t[:, 512:], bank[4][:, :]).then_inc(h_t_ok[1], 1)

        @block.tensor
        def _(pe):
            pe.sem_inc(w_used, 2)
            pe.wait_ge(const_in, 64)

            def product(ps, half, w, hi, lo, start, stop):
                pe.matmul(ps, w_hi[:, half % 2, w], hi, start=start, stop=False)
                pe.matmul(ps, w_hi[:, half % 2, w], lo, start=False, stop=False)
                return pe.matmul(ps, w_lo[:, half % 2, w], hi, start=False, stop=stop)

            with pe.Fori(0, NT) as t:
                n0 = t * N_TILE
                split, landed, copied = pe.to_reg(t * 4 + 6), pe.to_reg(t * 16 + 16), pe.to_reg(t * SUB_T + 1)
                pe.wait_ge(const_in, 64)
                pe.wait_ge(x_lo_ok, split)
                pe.wait_ge(mask_in, landed)
                pe.wait_ge(log_out, copied)
                with pe.Fori(0, HP) as p:
                    g = t * HP + p

                    def values(cb, h):
                        u2 = (g * NCB + cb) * 2 + h
                        pe.wait_ge(vkeys_ok, g * NCB + cb + 1)
                        pe.wait_ge(prob_t_ok[h], g * NCB + cb + 2)
                        if h == 0:
                            pe.wait_ge(o_lo_ok, g * NCB + cb + 1)
                        else:
                            pe.wait_ge(o_ok, u2 + 2)
                        ps, c = outp[:, h * DH:(h + 1) * DH], slice(h * DH, (h + 1) * DH)
                        for j in range(NKEY // P):
                            pe.matmul(ps, prob_t[:, h, j * P:(j + 1) * P],
                                      vkeys[:, cb % 2, j * P + h * DH:j * P + (h + 1) * DH], start=(j == 0), stop=False)
                        pe.matmul(ps, prob_t[0:NMETA, h, NKEY:512], vmeta[:, c], start=False, stop=True)\
                          .then_inc(pv_ok, 1)

                    def turn_probs(cb, h):
                        pe.wait_ge(exp_ok, (g * NCB + cb) * 2 + h + 3)
                        for j in range(4):
                            last = pe.transpose(turned[:, j * P:(j + 1) * P], prob[:, h, j * P:(j + 1) * P], ident[:, :])
                        last.then_inc(turn_ok, 1)

                    def turn_outputs(cb):
                        pe.wait_ge(o_ok, (g * NCB + cb) * 2 + 4)
                        pe.transpose(outp[:, P:2 * P], o_rows[:, :], ident[:, :]).then_inc(oturn_ok, 1)

                    for step, at in attention_schedule():
                        unit = g * NCB + (at if step != "chunk" else 0)
                        if step == "scores":
                            if at:
                                values(at - 1, 1)
                            pe.wait_ge(kb_in, (g + 1) * KB_DMAS * 16)
                            pe.wait_ge(q_cut_ok, g + 2)
                            pe.wait_ge(v_cut_ok, unit + 2)
                            pe.wait_ge(prob_t_ok[1], unit + 1)
                            for j in range(NKEY // P):
                                last = pe.transpose(turned[:, j * P:(j + 1) * P],
                                                    v_cut[:, at * NKEY + j * P:at * NKEY + (j + 1) * P], ident[:, :])
                            if at == 0:
                                last = pe.matmul(turned[0:NMETA, NKEY:512], val[:, KROWS * GRID:], ident[:, :],
                                                 start=True, stop=True)
                            last.then_inc(vturn_ok, 1)
                            rr, cc = window(at)
                            for h in range(2):
                                hh = slice(h * DH, (h + 1) * DH)
                                qs = q_cut[hh, at * P:(at + 1) * P]
                                pe.wait_ge(max_ok, unit * 2 + h + 1)
                                pe.matmul(score[h][:, 0:NKEY].rearrange("p (r c) -> p r c", c=KCOLS), qs,
                                          grid(key[hh, 0:KROWS * GRID])[:, rr, cc], start=True, stop=False)
                                pe.matmul(score[h][:, 0:NKEY], ident_b[:, :], mask[:, at * NKEY:(at + 1) * NKEY],
                                          start=False, stop=True)
                                pe.matmul(score[h][:, NKEY:NKEY + NMETA], qs, key[hh, KROWS * GRID:],
                                          start=True, stop=True).then_inc(scores_ok, 1)
                        elif step == "turn0":
                            pe.wait_ge(vkeys_ok, unit + 1)
                            turn_probs(at, 0)
                            if at:
                                turn_outputs(at - 1)
                        elif step == "turn1":
                            pe.wait_ge(prob_t_ok[0], unit + 2)
                            turn_probs(at, 1)
                            values(at, 0)
                        elif step == "drain_values":
                            values(at, 1)
                        elif step == "drain_turn":
                            turn_outputs(at)
                        else:
                            grp, k = at
                            n, f = n0 + p * NPAIR + grp, g * 2 + grp // 3
                            if k == 0:
                                pe.wait_ge(w_lo_ok, n + 3)
                                if grp % 3 == 0:
                                    pe.wait_ge(c_ok, f + 1)
                                elif grp % 3 == 1:
                                    pe.wait_ge(conv_step, f * 8 + 1)
                                else:
                                    pe.wait_ge(conv_step, f * 8 + 1)
                            last = product(bank[grp % 3][:, :], grp, slice(k * P, (k + 1) * P), x_hi[:, k, :], x_lo[:, k, :],
                                           k == 0, k == KD - 1)
                            if k == KD - 1:
                                last.then_inc(w_used, 1)
                y_split, o_split = pe.to_reg(t * FB + FB + 1), pe.to_reg(t * 16 + 17)
                pe.wait_ge(const_in, 64)
                pe.wait_ge(y_lo_ok, y_split)
                pe.wait_ge(o_lo_ok, o_split)
                with pe.Fori(0, FB) as f:
                    n, m = n0 + N_CXB + f * 4, t * FB + f

                    def branch(j, ps, nk, hi, lo, free, value):
                        pe.wait_ge(w_lo_ok, n + j + 3)
                        pe.wait_ge(free, value + 1)
                        for k in range(nk):
                            last = product(ps[:, :], j, slice(k * P, (k + 1) * P), hi(k), lo(k), k == 0, k == nk - 1)
                        last.then_inc(w_used, 1)

                    cut = lambda x: lambda k: x[:, k * TILE:(k + 1) * TILE]
                    xc = lambda x: lambda k: x[:, k, :]
                    branch(0, bank[0], KD, xc(x_hi), xc(x_lo), sig_a_ok, m)
                    branch(1, bank[1], HP, cut(o_hi), cut(o_lo), m_step, m * 3)
                    branch(2, bank[2], KD, xc(x_hi), xc(x_lo), sig_c_ok, m)
                    branch(3, bank[7], KD, cut(y_hi), cut(y_lo), m_step, m * 3)
                pe.wait_ge(m_lo_ok, t * FB + FB)
                for j in range(N_OUT):
                    pe.wait_ge(w_lo_ok, n0 + N_CXB + N_MERGE + j + 3)
                    for kk in range(2):
                        k, w = 2 * (j % 4) + kk, slice(kk * 512, (kk + 1) * 512)
                        for s in range(SUB_T):
                            ps, ms = out_banks(bank, j // 4)[s][:, :], slice(k * TILE + s * P, k * TILE + (s + 1) * P)
                            pe.matmul(ps, m_hi[:, ms], w_hi[:, j % 2, w], start=(k == 0), stop=False)
                            pe.matmul(ps, m_hi[:, ms], w_lo[:, j % 2, w], start=False, stop=False)
                            last = pe.matmul(ps, m_lo[:, ms], w_hi[:, j % 2, w], start=False, stop=(k == KD - 1))
                    last.then_inc(w_used, 1)
                pe.wait_ge(res_step, t * 8 + 4)
                for s in range(SUB_T):
                    c = t * SUB_T + s
                    pe.wait_ge(aff_step, c * 2 + 2)
                    pe.wait_ge(h_t_ok[0], c + 1)
                    pe.wait_ge(h_t_ok[1], c + 1)
                    for k in range(KD):
                        last = pe.transpose(bank[3 + k // 4][:, (k % 4) * P:(k % 4 + 1) * P],
                                            rows[:, s, k * P:(k + 1) * P], ident[:, :])
                    last.then_inc(hturn_ok, 1)
                    pe.wait_ge(h_t_ok[0], c + 2)
                    pe.wait_ge(h_t_ok[1], c + 2)
                    pe.wait_ge(log_out, c + 1)
                    for k in range(KD):
                        last = pe.matmul(bank[5][:, 0:NLOG], h_t[:, k * P:(k + 1) * P], w_router[:, k, :],
                                         start=(k == 0), stop=(k == KD - 1))
                    last.then_inc(log_ok, 1)


def route(nc, logits, r):
    NP = 2 * NSUB
    with ExitStack() as ctx:
        sb = lambda n, s, d=F32: ctx.enter_context(nc.sbuf_tensor(n, s, d))
        sem = lambda n: ctx.enter_context(nc.semaphore(n))
        ints = sb("ints", [P, 512], I32)
        lane = sb("lane", [P, P])
        block_no = sb("block_no", [P, NPLAN])
        edge128 = sb("edge128", [P, NSUB])
        token = sb("token", [P, NP])
        spare = sb("spare", [P, 1])
        rank_g, rank_e = sb("rank_g", [P, NG]), sb("rank_e", [P, NEXP])
        ones = sb("ones", [P, NEXP])
        below = sb("below", [P, P], BF16)
        all_one = sb("all_one", [P, P], BF16)
        gdiff, gexp, ghot = (sb(n, [P, NSUB, NG]) for n in ("gdiff", "gexp", "ghot"))
        masked = sb("masked", [P, NSUB, NEXP])
        weight = sb("weight", [P, NSUB, NEXP])
        hot = [sb(f"hot{c}", [P, NSUB, NEXP]) for c in range(2)]
        chosen = sb("chosen", [P, NSUB, NEXP], BF16)
        col = [sb(f"col{j}", [P, NSUB]) for j in range(8)]
        gmax, gsum, best, top1, top2, ediff, e2, den = col
        place = sb("place", [P, NSUB, NEXP])
        count, blocks, pend, pstart = (sb(n, [P, NEXP]) for n in ("count", "blocks", "pend", "pstart"))
        over = sb("over", [P, NEXP, NSUB])
        before = sb("before", [1, NPLAN, NEXP])
        owner_f = sb("owner_f", [1, NPLAN])
        slot_f, slot_i = sb("slot_f", [P, NP]), sb("slot_i", [P, NP], I32)
        code, empty, second = (sb(n, [P, NPLAN]) for n in ("code", "empty", "second"))
        part_i = sb("part_i", [P, 2, NP], I32)
        part_f = sb("part_f", [P, 2, NP])
        at_lane = sb("at_lane", [P, 2, P])
        at_block = sb("at_block", [P, 2, NPLAN])
        ranks_ps = ctx.enter_context(nc.psum_tensor("ranks_ps", [P, 512], F32))
        count_ps = ctx.enter_context(nc.psum_tensor("count_ps", [P, 512], F32))
        table_ps = ctx.enter_context(nc.psum_tensor("table_ps", [P, 512], F32))
        iota_step = sem("iota_step")
        gdiff_ok, gexp_ok = sem("gdiff_ok"), sem("gexp_ok")
        ediff_ok, e2_ok = sem("ediff_ok"), sem("e2_ok")
        chosen_ok = sem("chosen_ok")
        counted = sem("counted")
        hots_ok = sem("hots_ok")
        hots_used = sem("hots_used")
        step = sem("route_step")
        block = ctx.enter_context(nc.Block())

        def spread(t, n):
            return t.unsqueeze(2).broadcast_to([t.shape[0], t.shape[1], n])

        @block.gpsimd
        def _(pool):
            done = [0]

            def link(ins):
                done[0] += 1
                ins.then_inc(iota_step, 1)
                pool.wait_ge(iota_step, done[0])

            for t, pattern, mult, base in ((lane, [[1, P]], 0, 0), (block_no, [[1, NPLAN]], 0, 0),
                                           (edge128, [[P, NSUB]], 0, 0), (token, [[P, NP]], 1, 1),
                                           (spare, [[1, 1]], 1, 2 * NTOK + 1),
                                           (rank_g, [[-1, NG]], 0, NG), (rank_e, [[-1, NEXP]], 0, NEXP)):
                n = pattern[0][1]
                link(pool.iota(ints[:, 0:n], pattern=pattern, base=base, channel_multiplier=mult))
                link(pool.tensor_copy(t[:, :], ints[:, 0:n]))
            link(pool.memset(ones[:, :], 1.0))
            link(pool.memset(all_one[:, :], 1.0))
            link(pool.affine_select(out=below[:, :], in_=all_one[:, :], compare_op=ALU.is_gt, fill=0.0, base=0,
                                    pattern=[[1, P]], channel_multiplier=-1))

        @block.scalar
        def _(act):
            act.wait_ge(gdiff_ok, 1)
            act.activation(gexp[:, :, :].rearrange("p s g -> p (s g)"), gdiff[:, :, :].rearrange("p s g -> p (s g)"),
                           ACT.Exp).then_inc(gexp_ok, 1)
            act.wait_ge(ediff_ok, 1)
            act.activation(e2[:, :], ediff[:, :], ACT.Exp).then_inc(e2_ok, 1)

        @block.vector
        def _(dve):
            done = [0]

            def link(ins):
                done[0] += 1
                ins.then_inc(step, 1)
                dve.wait_ge(step, done[0])

            lg = logits[:, :].rearrange("p (s n) -> p s n", n=NLOG)
            dve.wait_ge(iota_step, 17)
            link(dve.reduce_max(gmax[:, :], lg[:, :, 0:NG], AX.X))
            dve.tensor_tensor(gdiff[:, :, :], lg[:, :, 0:NG], spread(gmax[:, :], NG), ALU.subtract).then_inc(gdiff_ok, 1)
            dve.wait_ge(gdiff_ok, 1)
            link(dve.tensor_scalar(ghot[:, :, :], gdiff[:, :, :], 0.0, None, ALU.is_equal))
            link(dve.tensor_tensor(ghot[:, :, :], ghot[:, :, :],
                                   rank_g[:, :].unsqueeze(1).broadcast_to([P, NSUB, NG]), ALU.mult))
            link(dve.reduce_max(best[:, :], ghot[:, :, :], AX.X))
            link(dve.tensor_tensor(ghot[:, :, :], ghot[:, :, :], spread(best[:, :], NG), ALU.is_equal))
            dve.wait_ge(gexp_ok, 1)
            link(dve.reduce_sum(gsum[:, :], gexp[:, :, :], AX.X))
            link(dve.tensor_scalar(ghot[:, :, :], ghot[:, :, :], -NEG, NEG, ALU.mult, ALU.add))
            link(dve.tensor_tensor(
                masked[:, :, :].rearrange("p s (g e) -> p s g e", g=NG),
                lg[:, :, NG:].rearrange("p s (g e) -> p s g e", g=NG),
                ghot[:, :, :].unsqueeze(3).broadcast_to([P, NSUB, NG, EPG]), ALU.add))
            for c, top in ((0, top1), (1, top2)):
                link(dve.reduce_max(top[:, :], masked[:, :, :], AX.X))
                link(dve.tensor_tensor(weight[:, :, :], masked[:, :, :], spread(top[:, :], NEXP), ALU.is_equal))
                link(dve.tensor_tensor(weight[:, :, :], weight[:, :, :],
                                       rank_e[:, :].unsqueeze(1).broadcast_to([P, NSUB, NEXP]), ALU.mult))
                link(dve.reduce_max(best[:, :], weight[:, :, :], AX.X))
                link(dve.tensor_tensor(hot[c][:, :, :], weight[:, :, :], spread(best[:, :], NEXP), ALU.is_equal))
                if c == 0:
                    link(dve.scalar_tensor_tensor(masked[:, :, :], hot[0][:, :, :], 3 * NEG, masked[:, :, :],
                                                  ALU.mult, ALU.add))
            dve.tensor_tensor(chosen[:, :, :], hot[0][:, :, :], hot[1][:, :, :], ALU.add).then_inc(chosen_ok, 1)
            dve.tensor_tensor(ediff[:, :], top2[:, :], top1[:, :], ALU.subtract).then_inc(ediff_ok, 1)
            dve.wait_ge(e2_ok, 1)
            link(dve.tensor_scalar(den[:, :], e2[:, :], 1.0, None, ALU.add))
            link(dve.tensor_tensor(den[:, :], den[:, :], gsum[:, :], ALU.mult))
            link(dve.reciprocal(r["gates"][:, 0:NSUB], den[:, :]))
            link(dve.tensor_tensor(r["gates"][:, NSUB:], r["gates"][:, 0:NSUB], e2[:, :], ALU.mult))
            dve.wait_ge(counted, 1)
            link(dve.tensor_copy(count[:, :], count_ps[:, 0:NEXP]))
            link(dve.tensor_tensor(over[:, :, :], spread(count[:, :], NSUB),
                                   edge128[:, :].unsqueeze(1).broadcast_to([P, NEXP, NSUB]), ALU.is_gt))
            link(dve.reduce_sum(blocks[:, :], over[:, :, :], AX.X))
            link(dve.tensor_tensor_scan(pend[:, :], ones[:, :], blocks[:, :], 0.0, ALU.mult, ALU.add))
            link(dve.tensor_tensor(pstart[:, :], pend[:, :], blocks[:, :], ALU.subtract))
            link(dve.tensor_scalar(pstart[:, :], pstart[:, :], float(P), None, ALU.mult))
            link(dve.tensor_tensor(place[:, :, :], ranks_ps[:, 0:NSUB * NEXP].rearrange("p (s e) -> p s e", e=NEXP),
                                   pstart[:, :].unsqueeze(1).broadcast_to([P, NSUB, NEXP]), ALU.add))
            for c in range(2):
                link(dve.tensor_tensor(weight[:, :, :], hot[c][:, :, :], place[:, :, :], ALU.mult))
                link(dve.reduce_sum(slot_f[:, c * NSUB:(c + 1) * NSUB], weight[:, :, :], AX.X))
            link(dve.tensor_copy(slot_i[:, :], slot_f[:, :]))
            link(dve.tensor_scalar(part_i[:, 0, :], slot_i[:, :], P - 1, None, ALU.bitwise_and))
            link(dve.tensor_scalar(part_i[:, 1, :], slot_i[:, :], 7, None, ALU.logical_shift_right))
            link(dve.tensor_copy(part_f[:, :, :], part_i[:, :, :]))
            for g in range(NP):
                dve.wait_ge(hots_used, g + 1)
                dve.tensor_scalar(at_lane[:, g % 2, :], lane[:, :], part_f[:, 0, g:g + 1], None, ALU.is_equal)
                dve.tensor_scalar(at_block[:, g % 2, :], block_no[:, :], part_f[:, 1, g:g + 1],
                                  token[:, g:g + 1], ALU.is_equal, ALU.mult).then_inc(hots_ok, 1)
            link(dve.tensor_tensor(before[:, :, :], pend[0:1, :].unsqueeze(1).broadcast_to([1, NPLAN, NEXP]),
                                   spread(block_no[0:1, :], NEXP), ALU.is_le))
            link(dve.reduce_sum(owner_f[:, :], before[:, :, :], AX.X))
            link(dve.tensor_scalar(owner_f[:, :], owner_f[:, :], float(NEXP - 1), None, ALU.min))
            link(dve.tensor_copy(r["owner"][:, :], owner_f[:, :]))
            link(dve.tensor_copy(r["used"][:, :], pend[0:1, NEXP - 1:NEXP]))
            dve.wait_ge(hots_used, NP + 2)
            link(dve.tensor_copy(code[:, :], table_ps[:, 0:NPLAN]))
            link(dve.tensor_scalar(empty[:, :], code[:, :], 0.0, None, ALU.is_equal))
            link(dve.tensor_scalar(second[:, :], code[:, :], NTOK + 0.5, -float(NTOK), ALU.is_gt, ALU.mult))
            link(dve.tensor_scalar(code[:, :], code[:, :], 1.0, None, ALU.subtract))
            link(dve.tensor_tensor(second[:, :], code[:, :], second[:, :], ALU.add))
            link(dve.tensor_scalar(second[:, :], second[:, :], 0.0, None, ALU.max))
            link(dve.tensor_copy(r["table"][:, :], second[:, :]))
            link(dve.scalar_tensor_tensor(code[:, :], empty[:, :], spare[:, 0:1], code[:, :], ALU.mult, ALU.add))
            link(dve.tensor_copy(r["dest"][:, :], code[:, :]))

        @block.tensor
        def _(pe):
            pe.sem_inc(hots_used, 2)
            pe.wait_ge(iota_step, 17)
            pe.wait_ge(chosen_ok, 1)
            for i in range(NSUB):
                ps = ranks_ps[:, i * NEXP:(i + 1) * NEXP]
                for j in range(i):
                    pe.matmul(ps, all_one[:, :], chosen[:, j, :], start=(j == 0), stop=False)
                pe.matmul(ps, below[:, :], chosen[:, i, :], start=(i == 0), stop=True)
            for j in range(NSUB):
                last = pe.matmul(count_ps[:, 0:NEXP], all_one[:, :], chosen[:, j, :], start=(j == 0), stop=(j == NSUB - 1))
            last.then_inc(counted, 1)
            for g in range(NP):
                pe.wait_ge(hots_ok, g + 1)
                pe.matmul(table_ps[:, 0:NPLAN], at_lane[:, g % 2, :], at_block[:, g % 2, :],
                          start=(g == 0), stop=(g == NP - 1)).then_inc(hots_used, 1)


NCHUNK = 6
RAW, CUT = 4, 3


def experts(nc, a, h_rows, y_rows, ident, r):
    with ExitStack() as ctx:
        sb = lambda n, s, d=F32: ctx.enter_context(nc.sbuf_tensor(n, s, d))
        sem = lambda n: ctx.enter_context(nc.semaphore(n))
        raw = sb("e_raw", [P, RAW, 2048])
        hi, lo = sb("e_hi", [P, CUT, 2048], F32R), sb("e_lo", [P, CUT, 2048], F32R)
        xg = sb("e_xg", [P, 2, D])
        index = sb("e_index", [P, 2], I32)
        out_index = sb("e_out_index", [P, 2], I32)
        x_hi, x_lo = sb("e_x_hi", [P, D], F32R), sb("e_x_lo", [P, D], F32R)
        gate, hid = sb("e_gate", [P, DE]), sb("e_hid", [P, DE])
        h_hi, h_lo = sb("e_h_hi", [P, DE], F32R), sb("e_h_lo", [P, DE], F32R)
        y = sb("e_y", [P, 2, D])
        ps = [ctx.enter_context(nc.psum_tensor(f"e_ps{j}", [P, 512], F32)) for j in range(7)]
        gate_ps, up_ps, x_ps, h_ps, y_ps = ps[0], ps[1], ps[2:4], ps[4], ps[5:7]
        raw_in = [sem(f"e_raw_in{s}") for s in range(RAW)]
        hi_ok = sem("e_hi_ok")
        lo_ok = sem("e_lo_ok")
        used = sem("e_used")
        index_ok = sem("e_index_ok")
        dest_ok = sem("e_dest_ok")
        xg_in = [sem(f"e_xg_in{s}") for s in range(2)]
        xt_ok = sem("e_xt_ok")
        x_hi_ok = [sem("e_x_hi0_ok"), sem("e_x_hi1_ok")]
        x_lo_ok = [sem("e_x_lo0_ok"), sem("e_x_lo1_ok")]
        gate_ok = sem("e_gate_ok")
        hid_ok = sem("e_hid_ok")
        ht_ok = sem("e_ht_ok")
        h_hi_ok, h_lo_ok = sem("e_h_hi_ok"), sem("e_h_lo_ok")
        y_ok = [sem("e_y0_ok"), sem("e_y1_ok")]
        y_out = [sem("e_y_out0"), sem("e_y_out1")]
        scrap = sb("e_scrap", [1, 4])
        block = ctx.enter_context(nc.Block())

        def blocks_in_use(eng, body):
            n = eng.value_load(r["used"][0:1, 0:1], min_val=1, max_val=NBLK - 1)
            with eng.Fori(0, NBLK // 2) as i:
                for s in range(2):
                    with eng.If(i * 2 + s < n):
                        body(i * 2 + s, i, s)

        def count_of(i, s, c, slots):
            n = s * NCHUNK + c
            return i * (2 * NCHUNK // slots) + n // slots + 1

        @block.sync
        def _(sp):
            def load(b, i, s, c):
                e = sp.value_load(r["owner"][0:1, bass.ds(b, 1)], min_val=0, max_val=NEXP - 1)
                slot = (s * NCHUNK + c) % RAW
                src = a[("w_e_gate", "w_e_up", "w_e_down")[c // 2]][bass.ds(e, 1), :, :]
                if c < 4:
                    src = src[:, (c % 2) * 512:(c % 2) * 512 + 512, :]
                else:
                    src = src[:, :, (c % 2) * 512:(c % 2) * 512 + 512]
                sp.wait_ge(lo_ok, b * NCHUNK + c + 1)
                sp.dma_start(raw[:, slot, :].rearrange("p (k n) -> p k n", k=4),
                             src.rearrange("a (k p) n -> p (a k) n", p=P)).then_inc(raw_in[slot], 16)

            def body(b, i, s):
                for c in range(2, NCHUNK):
                    load(b, i, s, c)
                for c in range(2):
                    load(b + 1, i + s, 1 - s, c)

            load(0, 0, 0, 0)
            load(0, 0, 0, 1)
            blocks_in_use(sp, body)

        @block.gpsimd
        def _(pool):
            for s in (gate_ok, hid_ok, ht_ok, *x_lo_ok, xt_ok, *y_ok):
                pool.sem_inc(s, 1)
            for j, s in enumerate((*xg_in, *y_out,)):
                pool.dma_start(scrap[:, j:j + 1], a["ln"][0:1, 0:1]).then_inc(s, 16)
            def gather(b, i, s):
                if not isinstance(b, int):
                    pool.wait_ge(xt_ok, b - 1 + 1)
                    pool.wait_ge(xg_in[s], i * 16 + 16)
                pool.tensor_copy(index[:, s:s + 1], r["table"][:, bass.ds(b, 1)]).then_inc(index_ok, 1)
                copied = pool.to_reg(b + 1)
                pool.wait_ge(y_out[0], 16)
                pool.wait_ge(index_ok, copied)
                pool.indirect_dma_start(out=xg[:, s, :], out_offset=None, in_=h_rows,
                                        in_offset=bass.IndirectOffsetOnAxis(ap=index[:, s:s + 1], axis=0))\
                    .then_inc(xg_in[s], 16)

            def body(b, i, s):
                gather(b + 1, i + s, 1 - s)
                halves, copied, last = pool.to_reg(b + 2), pool.to_reg(b + 1), pool.to_reg((i + s) * 16 + 16)
                before = pool.to_reg(i * 16 + 16)
                pool.wait_ge(index_ok, 1)
                pool.wait_ge(y_out[s], before)
                pool.tensor_copy(out_index[:, s:s + 1], r["dest"][:, bass.ds(b, 1)]).then_inc(dest_ok, 1)
                pool.wait_ge(index_ok, 1)
                pool.wait_ge(dest_ok, copied)
                pool.wait_ge(y_ok[0], halves)
                pool.wait_ge(y_ok[1], halves)
                pool.wait_ge(y_out[1 - s], last)
                pool.indirect_dma_start(out=y_rows, in_=y[:, s, :], in_offset=None,
                                        out_offset=bass.IndirectOffsetOnAxis(ap=out_index[:, s:s + 1], axis=0))\
                    .then_inc(y_out[s], 16)

            gather(0, 0, 0)
            blocks_in_use(pool, body)
            n = pool.value_load(r["used"][0:1, 0:1], min_val=1, max_val=NBLK - 1)
            pool.wait_ge(y_out[0], (n + 1) // 2 * 16 + 16)
            pool.wait_ge(y_out[1], n // 2 * 16 + 16)
            pool.wait_ge(xg_in[0], (n + 2) // 2 * 16 + 16)
            pool.wait_ge(xg_in[1], (n + 1) // 2 * 16 + 16)

        @block.scalar
        def _(act):
            def high(b, i, s, c):
                slot, cut = (s * NCHUNK + c) % RAW, (s * NCHUNK + c) % CUT
                act.wait_ge(raw_in[slot], count_of(i, s, c, RAW) * 16)
                act.wait_ge(used, b * NCHUNK + c + 1)
                act.activation(hi[:, cut, :], raw[:, slot, :], ACT.Copy).then_inc(hi_ok, 1)

            def x_high(b):
                for j in range(2):
                    act.wait_ge(xt_ok, b + 2)
                    act.activation(x_hi[:, j * 512:(j + 1) * 512], x_ps[j][:, :], ACT.Copy).then_inc(x_hi_ok[j], 1)

            def body(b, i, s):
                high(b, i, s, 2)
                high(b, i, s, 3)
                high(b, i, s, 4)
                act.wait_ge(used, b * NCHUNK + 2 + CUT)
                act.wait_ge(hid_ok, b + 1)
                act.activation(gate[:, :], gate_ps[:, :], ACT.Silu).then_inc(gate_ok, 1)
                high(b, i, s, 5)
                x_high(b + 1)
                act.wait_ge(ht_ok, b + 2)
                act.activation(h_hi[:, :], h_ps[:, :], ACT.Copy).then_inc(h_hi_ok, 1)
                high(b + 1, i + s, 1 - s, 0)
                high(b + 1, i + s, 1 - s, 1)
                act.wait_ge(used, b * NCHUNK + 5 + CUT)
                act.wait_ge(y_out[s], i * 16 + 16)
                act.activation(y[:, s, 0:512], y_ps[0][:, :], ACT.Copy).then_inc(y_ok[0], 1)

            high(0, 0, 0, 0)
            high(0, 0, 0, 1)
            x_high(0)
            blocks_in_use(act, body)

        @block.vector
        def _(dve):
            dve.sem_inc(lo_ok, RAW)

            def low(b, i, s, c):
                slot, cut = (s * NCHUNK + c) % RAW, (s * NCHUNK + c) % CUT
                dve.wait_ge(hi_ok, b * NCHUNK + c + 1)
                dve.wait_ge(used, b * NCHUNK + c + 1)
                dve.tensor_tensor(lo[:, cut, :], raw[:, slot, :], hi[:, cut, :].bitcast(F32), ALU.subtract)\
                   .then_inc(lo_ok, 1)

            def x_low(b):
                for j in range(2):
                    at = slice(j * 512, (j + 1) * 512)
                    dve.wait_ge(x_hi_ok[j], b + 1)
                    dve.tensor_tensor(x_lo[:, at], x_ps[j][:, :], x_hi[:, at].bitcast(F32), ALU.subtract)\
                       .then_inc(x_lo_ok[j], 1)

            def body(b, i, s):
                for c in range(2, NCHUNK):
                    low(b, i, s, c)
                dve.wait_ge(used, b * NCHUNK + 4 + CUT)
                dve.wait_ge(gate_ok, b + 2)
                dve.wait_ge(ht_ok, b + 1)
                dve.tensor_tensor(hid[:, :], gate[:, :], up_ps[:, :], ALU.mult).then_inc(hid_ok, 1)
                x_low(b + 1)
                dve.wait_ge(h_hi_ok, b + 1)
                dve.tensor_tensor(h_lo[:, :], h_ps[:, :], h_hi[:, :].bitcast(F32), ALU.subtract).then_inc(h_lo_ok, 1)
                low(b + 1, i + s, 1 - s, 0)
                low(b + 1, i + s, 1 - s, 1)
                dve.wait_ge(used, b * NCHUNK + 6 + CUT)
                dve.wait_ge(y_out[s], i * 16 + 16)
                dve.tensor_copy(y[:, s, 512:], y_ps[1][:, :]).then_inc(y_ok[1], 1)

            low(0, 0, 0, 0)
            low(0, 0, 0, 1)
            x_low(0)
            blocks_in_use(dve, body)

        @block.tensor
        def _(pe):
            pe.sem_inc(used, CUT)

            def turn_rows(b, i, s):
                pe.wait_ge(xg_in[s], i * 16 + 32)
                pe.wait_ge(x_lo_ok[1], b + 1)
                for k in range(KD):
                    last = pe.transpose(x_ps[k // 4][:, (k % 4) * P:(k % 4 + 1) * P], xg[:, s, k * P:(k + 1) * P],
                                        ident[:, :])
                last.then_inc(xt_ok, 1)

            def chunk(b, s, c, out, left_hi, left_lo, k0, first, last_k):
                cut = (s * NCHUNK + c) % CUT
                pe.wait_ge(lo_ok, b * NCHUNK + c + RAW + 1)
                for j in range(4):
                    w, t = slice(j * 512, (j + 1) * 512), slice((k0 + j) * P, (k0 + j + 1) * P)
                    pe.matmul(out[:, :], left_hi[:, t], hi[:, cut, w], start=(first and j == 0), stop=False)
                    pe.matmul(out[:, :], left_hi[:, t], lo[:, cut, w], start=False, stop=False)
                    last = pe.matmul(out[:, :], left_lo[:, t], hi[:, cut, w], start=False, stop=(last_k and j == 3))
                last.then_inc(used, 1)

            def body(b, i, s):
                pe.wait_ge(x_lo_ok[0], b + 2)
                pe.wait_ge(x_lo_ok[1], b + 2)
                pe.wait_ge(gate_ok, b + 1)
                pe.wait_ge(hid_ok, b + 1)
                for c in range(4):
                    chunk(b, s, c, (gate_ps, up_ps)[c // 2], x_hi, x_lo, (c % 2) * 4, c % 2 == 0, c % 2 == 1)
                turn_rows(b + 1, i + s, 1 - s)
                pe.wait_ge(hid_ok, b + 2)
                for k in range(KE):
                    last = pe.transpose(h_ps[:, k * P:(k + 1) * P], hid[:, k * P:(k + 1) * P], ident[:, :])
                last.then_inc(ht_ok, 1)
                pe.wait_ge(h_lo_ok, b + 1)
                for c in (4, 5):
                    pe.wait_ge(y_ok[c - 4], b + 1)
                    chunk(b, s, c, y_ps[c - 4], h_hi, h_lo, 0, True, True)

            turn_rows(0, 0, 0)
            blocks_in_use(pe, body)


def combine(nc, a, h_rows, y_rows, r, out):
    with ExitStack() as ctx:
        sb = lambda n, s, d=F32: ctx.enter_context(nc.sbuf_tensor(n, s, d))
        sem = lambda n: ctx.enter_context(nc.semaphore(n))
        S = 2
        ln_g, ln_b = sb("ln2_g", [P, D]), sb("ln2_b", [P, D])
        yc = [sb(f"c_y{c}", [P, S, D]) for c in range(2)]
        h, acc, res = sb("c_h", [P, S, D]), sb("c_acc", [P, S, D]), sb("c_res", [P, S, D])
        stats = sb("c_stats", [P, S, 12])
        mom = sb("c_mom", [P, S, 4])
        neg_half = sb("c_neg_half", [P, 1])
        ln_in = sem("c_ln_in")
        const_ok = sem("c_const_ok")
        y_in = [[sem(f"c_y{c}_in{s}") for s in range(S)] for c in range(2)]
        h_in = [sem(f"c_h_in{s}") for s in range(S)]
        acc_step = sem("c_acc_step")
        sum_step = sem("c_sum_step")
        stat_step = sem("c_stat_step")
        eps_ok, rstd_ok = sem("c_eps_ok"), sem("c_rstd_ok")
        shift_ok = sem("c_shift_ok")
        norm_ok = sem("c_norm_ok")
        gain_ok = sem("c_gain_ok")
        done = sem("c_done")
        stored = [sem(f"c_stored{s}") for s in range(S)]
        block = ctx.enter_context(nc.Block())
        n = NSUB // S

        @block.sync
        def _(sp):
            with sp.Fori(0, n) as i:
                for s in range(S):
                    sp.wait_ge(sum_step, i * S * 2 + 1)
                    sp.dma_start(h[:, s, :], h_rows[bass.ds((i * S + s) * P, P), :]).then_inc(h_in[s], 16)
                    for c in range(2):
                        sp.dma_start(yc[c][:, s, :], y_rows[bass.ds((i * S + s) * P + c * NTOK, P), :])\
                          .then_inc(y_in[c][s], 16)

        @block.gpsimd
        def _(pool):
            for s in (norm_ok, *stored, sum_step):
                pool.sem_inc(s, 1)
            pool.memset(neg_half[:, :], -0.5).then_inc(const_ok, 1)
            pool.dma_start(ln_g[:, :], a["ln"][2:3, :].broadcast_to([P, D])).then_inc(ln_in, 16)
            pool.dma_start(ln_b[:, :], a["ln"][3:4, :].broadcast_to([P, D])).then_inc(ln_in, 16)

            with pool.Fori(0, n) as i:
                for s in range(S):
                    t = i * S + s
                    known = pool.to_reg(t * 3 + 3)
                    pool.wait_ge(const_ok, 1)
                    pool.wait_ge(stat_step, known)
                    pool.tensor_scalar(mom[:, s, 1:2], mom[:, s, 1:2], EPS, None, ALU.add).then_inc(eps_ok, 1)
                    pool.wait_ge(eps_ok, t + 1)
                    pool.tensor_tensor(mom[:, s, 2:3], mom[:, s, 1:2], neg_half[:, :], ALU.pow).then_inc(rstd_ok, 1)
                for s in range(S):
                    t = i * S + s
                    pool.wait_ge(ln_in, 32)
                    pool.wait_ge(norm_ok, t + 2)
                    pool.tensor_tensor(res[:, s, :], res[:, s, :], ln_g[:, :], ALU.mult).then_inc(gain_ok, 1)

        @block.scalar
        def _(act):
            with act.Fori(0, n) as i:
                for s in range(S):
                    t = i * S + s
                    act.wait_ge(y_in[0][s], i * 16 + 16)
                    act.wait_ge(norm_ok, i * S + 1)
                    act.activation(acc[:, s, :], yc[0][:, s, :], ACT.Copy,
                                   scale=r["gates"][:, bass.ds(t, 1)]).then_inc(acc_step, 1)
                for s in range(S):
                    t = i * S + s
                    act.wait_ge(shift_ok, t + 1)
                    act.wait_ge(stored[s], i * 16 + 1)
                    act.activation(res[:, s, :], acc[:, s, :], ACT.Identity, scale=mom[:, s, 2:3],
                                   bias=mom[:, s, 3:4]).then_inc(norm_ok, 1)
                for s in range(S):
                    t = i * S + s
                    act.wait_ge(done, t + 1)
                    act.dma_start(out[bass.ds(t * P, P), :], res[:, s, :]).then_inc(stored[s], 16)
            for s in range(S):
                act.wait_ge(stored[s], n * 16 + 1)

        @block.vector
        def _(dve):
            dve.wait_ge(ln_in, 32)
            with dve.Fori(0, n) as i:
                for s in range(S):
                    t = i * S + s
                    dve.wait_ge(acc_step, t + 1)
                    dve.wait_ge(y_in[1][s], i * 16 + 16)
                    dve.scalar_tensor_tensor(acc[:, s, :], yc[1][:, s, :], r["gates"][:, bass.ds(t + NSUB, 1)],
                                             acc[:, s, :], ALU.mult, ALU.add).then_inc(sum_step, 1)
                    dve.wait_ge(sum_step, t * 2 + 2)
                    dve.wait_ge(h_in[s], i * 16 + 16)
                    dve.scalar_tensor_tensor(acc[:, s, :], h[:, s, :], ALPHA, acc[:, s, :], ALU.mult, ALU.add)\
                       .then_inc(sum_step, 1)
                    dve.wait_ge(sum_step, t * 2 + 3)
                    for half in range(2):
                        dve.bn_stats(stats[:, s, half * 6:half * 6 + 6], acc[:, s, half * 512:(half + 1) * 512])\
                           .then_inc(stat_step, 1)
                    taken = dve.to_reg(t * 3 + 2)
                    dve.wait_ge(ln_in, 32)
                    dve.wait_ge(stat_step, taken)
                    dve.bn_aggr(mom[:, s, 0:2], stats[:, s, :]).then_inc(stat_step, 1)
                for s in range(S):
                    t = i * S + s
                    dve.wait_ge(rstd_ok, t + 1)
                    dve.scalar_tensor_tensor(mom[:, s, 3:4], mom[:, s, 0:1], -1.0, mom[:, s, 2:3], ALU.mult, ALU.mult)\
                       .then_inc(shift_ok, 1)
                for s in range(S):
                    t = i * S + s
                    dve.wait_ge(gain_ok, t + 1)
                    dve.tensor_tensor(res[:, s, :], res[:, s, :], ln_b[:, :], ALU.add).then_inc(done, 1)


def encoder(nc, a, out):
    qkv = nc.dram_tensor("qkv", [3 * HP, P, NCOL], F32, kind="Internal").ap()
    h_rows = nc.dram_tensor("h_rows", [NTOK, D], F32, kind="Internal").ap()
    y_rows = nc.dram_tensor("y_rows", [2 * NTOK + P, D], F32, kind="Internal").ap()
    with ExitStack() as ctx:
        sb = lambda n, s, d=F32: ctx.enter_context(nc.sbuf_tensor(n, s, d))
        ident = sb("ident", [P, P])
        logits = sb("logits", [P, NSUB * NLOG])
        r = {
            "gates": sb("gates", [P, 2 * NSUB]),
            "table": sb("table", [P, NPLAN], I32),
            "dest": sb("dest", [P, NPLAN], I32),
            "owner": sb("owner", [1, NPLAN], I32),
            "used": sb("used", [1, 1], I32),
        }
        edges = sb("edges", [P, FB * NEDGE])
        project_qkv(nc, a, a["x_cols"], a["w_qkv"], a["w_cxb"], ident, qkv, edges)
        mixer(nc, a, qkv, edges, ident, logits, h_rows)
        route(nc, logits, r)
        experts(nc, a, h_rows, y_rows, ident, r)
        combine(nc, a, h_rows, y_rows, r, out)


def layouts(inp):
    a = {k: np.asarray(v) for k, v in inp.items()}
    x = np.concatenate([a["x_prompt"].reshape(PROMPT, D), a["x_sample"].reshape(SAMPLE, D)], 0)
    cols = np.concatenate([x, a["meta_tokens"]], 0).T.reshape(KD, P, NCOL)
    w_in = a["w_in"][0].reshape(KD, P, 52, P).transpose(2, 1, 0, 3).reshape(52, P, D)
    out = {}
    out["x_rows"] = np.ascontiguousarray(x)
    out["x_cols"] = np.ascontiguousarray(cols.transpose(1, 0, 2))
    none = np.zeros((D,), np.float32)
    meta = a["meta_tokens"][NMETA - 1]
    halo = np.stack([np.stack([meta, x[TILE]]), np.stack([x[TILE - 1], none]), np.stack([meta, none])])
    out["x_halo"] = np.ascontiguousarray(halo.reshape(NT, 2, KD, P).transpose(0, 3, 2, 1).reshape(NT, P, KD * 2))
    out["w_qkv"] = np.ascontiguousarray(w_in[0:12])
    b, c, xc, ga, gc = (w_in[12 + 8 * i:20 + 8 * i] for i in range(5))
    out["w_cxb"] = np.ascontiguousarray(np.stack([c, xc, b], 1).reshape(3 * FB, P, D))
    w_conv = a["w_conv_proj"][0].reshape(KD, P, FB, P).transpose(2, 1, 0, 3).reshape(FB, P, D)
    out["w_gates"] = np.ascontiguousarray(np.stack([ga, gc, w_conv], 1).reshape(3 * FB, P, D))
    out["w_att"] = np.ascontiguousarray(
        a["w_att_proj"][0].reshape(HP, P, FB, P).transpose(2, 1, 0, 3).reshape(FB, P, HP * P))
    out["w_out"] = np.ascontiguousarray(
        a["w_out"][0].reshape(KD // 2, 2, P, 2, 512).transpose(3, 0, 2, 1, 4).reshape(KD, P, D))
    cw = np.concatenate([a["conv_w"][0], a["conv_b"]], 0)
    out["conv_wb"] = np.ascontiguousarray(cw.reshape(4, FB, P).transpose(2, 1, 0).reshape(P, 4 * FB))
    plane = np.zeros((HEADS, 16, BP_ROWS * 64 + 64), np.float32)
    rpb = a["rpb"][0]
    for i in range(16):
        for y in range(2 * WIN_H - 1):
            at = (y + 4) * 64 + 16 - (15 - i)
            plane[:, i, at:at + 2 * WIN_W - 1] = rpb[:, y]
    out["bias_planes"] = plane
    out["masks"] = window_masks()
    out["ln"] = np.ascontiguousarray(np.concatenate([a["ln1_g"], a["ln1_b"], a["ln2_g"], a["ln2_b"]], 0))
    wr = np.concatenate([a["w_router_group"][0], a["w_router_expert"][0]], 1)
    out["w_router"] = np.ascontiguousarray(wr.reshape(KD, P, NLOG).transpose(1, 0, 2).reshape(P, KD * NLOG))
    out["w_e_gate"] = a["w_e_gate"][0]
    out["w_e_up"] = a["w_e_up"][0]
    out["w_e_down"] = a["w_e_down"][0]
    return out


def kernel(**inputs):
    import concourse.bacc as bacc
    from concourse.bass_utils import run_bass_kernel_spmd

    arrays = layouts(inputs)
    nc = bacc.Bacc("TRN2", target_bir_lowering=False, num_devices=1)
    a = {n: nc.dram_tensor(f"in_{n}", v.shape, mybir.dt.from_np(v.dtype), kind="ExternalInput").ap()
         for n, v in arrays.items()}
    out = nc.dram_tensor("out", [NTOK, D], F32, kind="ExternalOutput").ap()
    encoder(nc, a, out)
    got = run_bass_kernel_spmd(nc, [{f"in_{n}": v for n, v in arrays.items()}], core_ids=[0]).results[0]["out"]
    return got[:PROMPT].reshape(1, PROMPT, D), got[PROMPT:].reshape(1, SAMPLE, D)
```

```python
from contextlib import ExitStack

import numpy as np

import concourse.bass as bass
from concourse import mybir

F32 = mybir.dt.float32
F32R = mybir.dt.float32r
BF16 = mybir.dt.bfloat16
I32 = mybir.dt.int32
ALU = mybir.AluOpType
ACT = mybir.ActivationFunctionType
AX = mybir.AxisListType

P = 128
D = 1024
KD = D // P
NMETA = 16
PROMPT, SAMPLE = 1024, 512
NTOK = PROMPT + SAMPLE
NCOL = NTOK + NMETA
TILE = 512
NT = NTOK // TILE
GRID, WIN_H, WIN_W = 64, 8, 16
ROWS_T = TILE // GRID
KROWS, KCOLS = 12, 32
NKEY = KROWS * KCOLS
NCB = 4
HEADS, DH = 8, 64
HP = HEADS // 2
FB = D // P
ALPHA = 2.0 ** 0.25
EPS = 1e-5
NEG = -1e30
BP_ROWS = 24
NG, NEXP, EPG = 4, 32, 8
DE = 512
KE = DE // P
NSUB = NTOK // P
SUB_T = TILE // P
NLOG = NG + NEXP
NBLK = (2 * NTOK + NEXP * (P - 1)) // P + 1
NBLK += NBLK % 2
NPLAN = NBLK + 3


NEDGE, RIGHT = 12, 9
N_CXB, N_MERGE, N_OUT = 3 * FB, 4 * FB, FB
N_TILE = N_CXB + N_MERGE + N_OUT


def key_start(cb):
    return min(max(cb * 16 - 8, 0), GRID - KCOLS)


def window_masks():
    m = np.full((NT, P, NCB, KROWS, KCOLS), NEG, np.float32)
    for t in range(NT):
        base = 4 * t + 4 * (t // 2)
        rows, first = (16, 0) if t < 2 else (8, 16)
        for r in range(ROWS_T):
            row = 8 * t + r - first
            rs = min(max(row - WIN_H // 2, 0), rows - WIN_H) + first
            for i in range(16):
                for cb in range(NCB):
                    ws = min(max(cb * 16 + i - WIN_W // 2, 0), GRID - WIN_W)
                    a, c = rs - base, ws - key_start(cb)
                    m[t, r * 16 + i, cb, a:a + WIN_H, c:c + WIN_W] = 0.0
    bits = m.reshape(NT, P, NCB * NKEY).view(np.uint32) >> 16
    return bits.astype(np.uint16)


def project_qkv(nc, a, x_cols, w_qkv, w_cxb, ident, qkv, edges):
    nblk = w_qkv.shape[0]
    nq = HP
    beside = slice(TILE, NCOL, NCOL - 1 - TILE)
    with ExitStack() as ctx:
        sb = lambda n, s, d=F32: ctx.enter_context(nc.sbuf_tensor(n, s, d))
        sem = lambda n: ctx.enter_context(nc.semaphore(n))
        x_hi = sb("qkv_x_hi", [P, KD, NCOL], F32R)
        x_lo = sb("qkv_x_lo", [P, KD, NCOL], F32R)
        x_raw = sb("qkv_x_raw", [P, 2, NCOL])
        w_raw = sb("qkv_w_raw", [P, 2, D])
        w_hi = sb("qkv_w_hi", [P, 2, D], F32R)
        w_lo = sb("qkv_w_lo", [P, 2, D], F32R)
        res = sb("qkv_res", [P, 2, NCOL])
        bank = [[ctx.enter_context(nc.psum_tensor(f"qkv_ps{s}{t}", [P, 512], F32)) for t in range(4)]
                for s in range(2)]
        x_side = sb("qkv_x_side", [P, KD, 2])
        c_row = sb("qkv_c_row", [2, P])
        u_row = sb("qkv_u_row", [2, D])
        side_in = [sem(f"qkv_side_in{s}") for s in range(2)]
        ident_ok = sem("qkv_ident_ok")
        side_used = sem("qkv_side_used")
        x_side_ok = sem("qkv_x_side_ok")
        c_row_ok = sem("qkv_c_row_ok")
        u_row_ok = sem("qkv_u_row_ok")
        u_col_ok = sem("qkv_u_col_ok")
        edge_ok = sem("qkv_edge_ok")
        x_in = [sem(f"qkv_x_in{s}") for s in range(2)]
        x_hi_ok = sem("qkv_x_hi_ok")
        x_lo_ok = sem("qkv_x_lo_ok")
        w_in = [sem(f"qkv_w_in{s}") for s in range(2)]
        w_hi_ok = sem("qkv_w_hi_ok")
        w_lo_ok = sem("qkv_w_lo_ok")
        w_used = sem("qkv_w_used")
        ev_act = sem("qkv_ev_act")
        ev_dve = sem("qkv_ev_dve")
        stored = [sem(f"qkv_stored{s}") for s in range(2)]
        cols = [slice(t * TILE, (t + 1) * TILE) for t in range(NT)] + [slice(NTOK, NCOL)]
        scrap = sb("qkv_scrap", [1, 4])
        block = ctx.enter_context(nc.Block())

        def load_w(eng, n, i, s):
            eng.wait_ge(w_lo_ok, n + 1)
            eng.dma_start(w_raw[:, s, :], w_qkv[bass.ds(n, 1), :, :].rearrange("a p n -> p (a n)"))\
               .then_inc(w_in[s], 16)

        @block.sync
        def _(sp):
            load_w(sp, 0, 0, 0)
            for k in range(KD):
                sp.wait_ge(x_lo_ok, k + 1)
                sp.dma_start(x_raw[:, k % 2, :], x_cols[:, k, :]).then_inc(x_in[k % 2], 16)
            load_w(sp, 1, 0, 1)
            with sp.Fori(1, nblk // 2) as i:
                for s in range(2):
                    load_w(sp, i * 2 + s, i, s)
            for s in range(2):
                sp.wait_ge(w_lo_ok, nblk + 1 + s)
            with sp.Fori(0, FB) as f:
                for s in range(2):
                    sp.wait_ge(side_used, f * 2 + 1)
                    sp.dma_start(w_raw[:, s, :], w_cxb[bass.ds(f * 3 + s, 1), :, :].rearrange("a p n -> p (a n)"))\
                      .then_inc(side_in[s], 16)

        @block.gpsimd
        def _(pool):
            for s in (side_used, u_row_ok):
                pool.sem_inc(s, 1)
            for j, s in enumerate(stored):
                pool.dma_start(scrap[:, j:j + 1], a["ln"][0:1, 0:1]).then_inc(s, 16)
            pool.memset(ident[:, :], 0.0).then_inc(ident_ok, 1)
            pool.wait_ge(ident_ok, 1)
            pool.affine_select(out=ident[:, :], in_=ident[:, :], compare_op=ALU.not_equal, fill=1.0, base=0,
                               pattern=[[-1, P]], channel_multiplier=1).then_inc(ident_ok, 1)
            with pool.Fori(0, nblk // 2) as i:
                for s in range(2):
                    pool.wait_ge(ev_act, i * 2 + s + 3)
                    pool.wait_ge(ev_dve, i * 2 + s + 3)
                    pool.dma_start(qkv[bass.ds(i * 2 + s, 1), :, :].rearrange("a p n -> p (a n)"),
                                   res[:, s, :]).then_inc(stored[s], 16)
            for s in range(2):
                pool.wait_ge(stored[s], 16 * (nblk // 2) + 16)

        @block.scalar
        def _(act):
            act.sem_inc(ev_act, 2)

            def high(n, i, s):
                act.wait_ge(w_in[s], i * 16 + 16)
                act.wait_ge(w_used, n + 1)
                act.activation(w_hi[:, s, :], w_raw[:, s, :], ACT.Copy).then_inc(w_hi_ok, 1)

            def copy_out(n, i, s, scale):
                act.wait_ge(w_used, n + 3)
                act.wait_ge(stored[s], i * 16 + 16)
                for t in range(2):
                    last = act.activation(res[:, s, cols[t]], bank[s][t][:, :], ACT.Copy, scale=scale)
                last.then_inc(ev_act, 1)

            high(0, 0, 0)
            for k in range(KD):
                act.wait_ge(x_in[k % 2], 16 * (k // 2 + 1))
                act.activation(x_hi[:, k, :], x_raw[:, k % 2, :], ACT.Copy).then_inc(x_hi_ok, 1)
            with act.Fori(0, nq // 2) as i:
                high(i * 2 + 1, i, 1)
                copy_out(i * 2, i, 0, DH ** -0.5)
                high(i * 2 + 2, i + 1, 0)
                copy_out(i * 2 + 1, i, 1, DH ** -0.5)
            with act.Fori(nq // 2, nblk // 2 - 1) as i:
                high(i * 2 + 1, i, 1)
                copy_out(i * 2, i, 0, 1.0)
                high(i * 2 + 2, i + 1, 0)
                copy_out(i * 2 + 1, i, 1, 1.0)
            i = nblk // 2 - 1
            high(2 * i + 1, i, 1)
            copy_out(2 * i, i, 0, 1.0)
            copy_out(2 * i + 1, i, 1, 1.0)

        @block.vector
        def _(dve):
            dve.sem_inc(w_lo_ok, 2)
            dve.sem_inc(x_lo_ok, 2)
            dve.sem_inc(ev_dve, 2)

            def low(n, i, s):
                dve.wait_ge(w_hi_ok, n + 1)
                dve.wait_ge(w_used, n + 1)
                dve.tensor_tensor(w_lo[:, s, :], w_raw[:, s, :], w_hi[:, s, :].bitcast(F32), ALU.subtract)\
                   .then_inc(w_lo_ok, 1)

            def copy_out(n, i, s, scale):
                dve.wait_ge(w_used, n + 3)
                dve.wait_ge(stored[s], i * 16 + 16)
                for t in range(2, 4):
                    ps = bank[s][t][:, 0:cols[t].stop - cols[t].start]
                    last = dve.tensor_scalar(res[:, s, cols[t]], ps, scale, None, ALU.mult)
                last.then_inc(ev_dve, 1)

            low(0, 0, 0)
            for k in range(KD):
                dve.wait_ge(x_hi_ok, k + 1)
                dve.tensor_copy(x_side[:, k, :], x_raw[:, k % 2, beside]).then_inc(x_side_ok, 1)
                dve.tensor_tensor(x_lo[:, k, :], x_raw[:, k % 2, :], x_hi[:, k, :].bitcast(F32), ALU.subtract)\
                   .then_inc(x_lo_ok, 1)
            with dve.Fori(0, nq // 2) as i:
                low(i * 2 + 1, i, 1)
                copy_out(i * 2, i, 0, DH ** -0.5)
                low(i * 2 + 2, i + 1, 0)
                copy_out(i * 2 + 1, i, 1, DH ** -0.5)
            with dve.Fori(nq // 2, nblk // 2 - 1) as i:
                low(i * 2 + 1, i, 1)
                copy_out(i * 2, i, 0, 1.0)
                low(i * 2 + 2, i + 1, 0)
                copy_out(i * 2 + 1, i, 1, 1.0)
            i = nblk // 2 - 1
            low(2 * i + 1, i, 1)
            copy_out(2 * i, i, 0, 1.0)
            copy_out(2 * i + 1, i, 1, 1.0)
            with dve.Fori(0, FB) as f:
                dve.wait_ge(side_used, f * 2 + 2)
                dve.wait_ge(u_row_ok, f + 1)
                dve.tensor_copy(c_row[:, :], bank[0][3][0:2, 0:P]).then_inc(c_row_ok, 1)
                dve.wait_ge(side_used, f * 2 + 3)
                dve.wait_ge(c_row_ok, f + 1)
                dve.tensor_tensor(u_row[:, bass.ds(f * P, P)], c_row[:, :], bank[1][3][0:2, 0:P], ALU.mult)\
                   .then_inc(u_row_ok, 1)
            cols_ps = bank[0][0][:, 0:2 * FB].rearrange("p (f c) -> p f c", c=2)
            edge = edges[:, :].rearrange("p (f s) -> p f s", s=NEDGE)
            dve.memset(edges[:, :], 0.0).then_inc(edge_ok, 1)
            dve.wait_ge(edge_ok, 1)
            dve.wait_ge(u_col_ok, 1)
            for slot, col in ((RIGHT, 0), (0, 1), (4, 1)):
                dve.tensor_copy(edge[:, :, slot], cols_ps[:, :, col]).then_inc(edge_ok, 1)

        @block.tensor
        def _(pe):
            pe.sem_inc(w_used, 2)

            def project(n, s, first=False):
                pe.wait_ge(w_lo_ok, n + 3)
                pe.wait_ge(ev_act, n + 1)
                pe.wait_ge(ev_dve, n + 1)
                for k in range(KD):
                    if first:
                        pe.wait_ge(x_lo_ok, k + 3)
                    w = slice(k * P, (k + 1) * P)
                    for t in range(4):
                        ps = bank[s][t][:, 0:cols[t].stop - cols[t].start]
                        pe.matmul(ps, w_hi[:, s, w], x_hi[:, k, cols[t]], start=(k == 0), stop=False)
                        pe.matmul(ps, w_hi[:, s, w], x_lo[:, k, cols[t]], start=False, stop=False)
                        last = pe.matmul(ps, w_lo[:, s, w], x_hi[:, k, cols[t]], start=False, stop=(k == KD - 1))
                last.then_inc(w_used, 1)

            project(0, 0, first=True)
            project(1, 1)
            with pe.Fori(1, nblk // 2) as i:
                for s in range(2):
                    project(i * 2 + s, s)
            pe.wait_ge(ev_dve, nblk + 2)
            pe.wait_ge(ev_act, nblk + 2)
            pe.wait_ge(x_side_ok, KD)
            with pe.Fori(0, FB) as f:
                for s in range(2):
                    pe.wait_ge(side_in[s], f * 16 + 16)
                    pe.wait_ge(u_row_ok, f + 1)
                    for k in range(KD):
                        last = pe.matmul(bank[s][3][0:2, 0:P], x_side[:, k, :], w_raw[:, s, k * P:(k + 1) * P],
                                         start=(k == 0), stop=(k == KD - 1))
                    last.then_inc(side_used, 1)
            pe.wait_ge(ident_ok, 2)
            pe.wait_ge(u_row_ok, FB + 1)
            for f in range(FB):
                last = pe.matmul(bank[0][0][:, 2 * f:2 * f + 2], u_row[:, f * P:(f + 1) * P], ident[0:2, 0:2],
                                 start=True, stop=True)
            last.then_inc(u_col_ok, 1)


def attention_schedule():
    chunk = 0
    for cb in range(NCB):
        for step, gap in (("scores", 5), ("turn0", 3), ("turn1", 3)):
            yield step, cb
            for chunk in range(chunk, chunk + gap):
                yield "chunk", divmod(chunk, KD)
            chunk += 1
    for step in ("drain_values", "drain_turn"):
        yield step, NCB - 1
        for chunk in range(chunk, chunk + 2):
            yield "chunk", divmod(chunk, KD)
        chunk += 1


KB_DMAS = 2 + ROWS_T
NPAIR = N_CXB // HP


def o_block(t, p, cb):
    at = t[:, bass.ds(p * TILE, TILE)].rearrange("p (r c) -> p r c", c=GRID)
    return at[:, :, cb * 16:cb * 16 + 16]


OUT_BANK = [(3, 4), (5, 6), (0, 1), (2, 7)]


def mixer(nc, a, qkv, edges, ident, logits, h_rows):
    with ExitStack() as ctx:
        sb = lambda n, s, d=F32: ctx.enter_context(nc.sbuf_tensor(n, s, d))
        sem = lambda n: ctx.enter_context(nc.semaphore(n))
        x_raw = sb("x_raw", [P, 2, 2 * TILE])
        x_hi, x_lo = sb("x_hi", [P, KD, TILE], F32R), sb("x_lo", [P, KD, TILE], F32R)
        o_hi, o_lo = sb("o_hi", [P, HP * TILE], F32R), sb("o_lo", [P, HP * TILE], F32R)
        y_hi, y_lo = sb("y_hi", [P, FB * TILE], F32R), sb("y_lo", [P, FB * TILE], F32R)
        w_raw = sb("w_raw", [P, 2, D])
        w_hi, w_lo = sb("w_hi", [P, 2, D], F32R), sb("w_lo", [P, 2, D], F32R)
        conv_wb = sb("conv_wb_sb", [P, 4 * FB])
        w_router = sb("w_router_sb", [P, KD, NLOG])
        ln_g, ln_b = sb("ln1_g", [P, D]), sb("ln1_b", [P, D])
        ident_b = sb("ident_b", [P, P], BF16)
        zeros = sb("zeros", [P, NMETA])
        neg_half = sb("neg_half", [P, SUB_T])
        q, q_cut = sb("q", [P, TILE]), sb("q_cut", [P, TILE])
        v_cut = sb("v_cut", [P, NCB * NKEY])
        key = sb("key", [P, KROWS * GRID + NMETA])
        val = sb("val", [P, KROWS * GRID + NMETA])
        bias = sb("bias", [P, 2, KROWS * GRID])
        mask = sb("mask", [P, NCB * NKEY], BF16)
        rows = sb("rows", [P, SUB_T, D])
        stats = sb("stats", [P, 12])
        mom = sb("mom", [P, SUB_T * 3]).rearrange("p (s m) -> p s m", m=3)
        first = ExitStack()
        sa = lambda n, s, d=F32: first.enter_context(nc.sbuf_tensor(n, s, d))
        prob = sa("prob", [P, 2, 512])
        prob_t = sa("prob_t", [P, 2, 512])
        sbias = sa("sbias", [P, 2, NKEY + NMETA])
        vkeys = sa("vkeys", [P, 2, NKEY])
        vmeta = sa("vmeta", [NMETA, P])
        o_rows = sa("o_rows", [P, P])
        small = sa("small", [P, 10])
        smeta, smax, nmax, ssum, rsum = (small[:, 2 * j:2 * j + 2] for j in range(5))
        c_sb = sa("c_sb", [P, TILE])
        u = sa("u", [P, TILE + 2])
        y = sa("y", [P, TILE])
        first.close()
        m_hi, m_lo = sb("m_hi", [P, FB * TILE], F32R), sb("m_lo", [P, FB * TILE], F32R)
        m_att = sb("m_att", [P, TILE])
        third = ExitStack()
        sa = lambda n, s, d=F32: third.enter_context(nc.sbuf_tensor(n, s, d))
        sig_a, sig_c = sa("sig_a", [P, TILE]), sa("sig_c", [P, TILE])
        third.close()
        h_t = sb("h_t", [P, D])
        out_hi = [w_hi[:, 0, :], w_hi[:, 1, :]] + [o_hi[:, j * D:(j + 1) * D] for j in range(2)] \
            + [y_hi[:, j * D:(j + 1) * D] for j in range(4)]
        out_lo = [w_lo[:, 0, :], w_lo[:, 1, :]] + [o_lo[:, j * D:(j + 1) * D] for j in range(2)] \
            + [y_lo[:, j * D:(j + 1) * D] for j in range(4)]
        bank = [ctx.enter_context(nc.psum_tensor(f"bank{j}", [P, 512], F32)) for j in range(8)]
        score, turned, outp = bank[3:5], bank[5], bank[6]

        const_in = sem("const_in")
        const_ok = sem("const_ok")
        x_in = [sem(f"x_in{j}") for j in range(2)]
        x_hi_ok, x_lo_ok = sem("x_hi_ok"), sem("x_lo_ok")
        w_in = [sem(f"w_in{j}") for j in range(2)]
        w_hi_ok, w_lo_ok = sem("w_hi_ok"), sem("w_lo_ok")
        w_used = sem("w_used")
        qv_in = sem("qv_in")
        kb_in = sem("kb_in")
        q_cut_ok = sem("q_cut_ok")
        v_cut_ok = sem("v_cut_ok")
        mask_in = sem("mask_in")
        rows_in = sem("rows_in")
        scores_ok = sem("scores_ok")
        max_step = sem("max_step")
        max_ok = sem("max_ok")
        exp_ok = sem("exp_ok")
        sum_ok = sem("sum_ok")
        turn_ok = sem("turn_ok")
        prob_t_ok = [sem("prob_t0_ok"), sem("prob_t1_ok")]
        vturn_ok, vkeys_ok = sem("vturn_ok"), sem("vkeys_ok")
        pv_ok = sem("pv_ok")
        o_ok = sem("o_ok")
        oturn_ok = sem("oturn_ok")
        o_hi_ok, o_lo_ok = sem("o_hi_ok"), sem("o_lo_ok")
        c_ok = sem("c_ok")
        conv_step = sem("conv_step")
        y_hi_ok, y_lo_ok = sem("y_hi_ok"), sem("y_lo_ok")
        sig_a_ok, sig_c_ok = sem("sig_a_ok"), sem("sig_c_ok")
        m_step = sem("m_step")
        m_hi_ok, m_lo_ok = sem("m_hi_ok"), sem("m_lo_ok")
        res_step = sem("res_step")
        mom_ok = sem("mom_ok")
        var_ok = sem("var_ok")
        rstd_ok = sem("rstd_ok")
        norm_ok = sem("norm_ok")
        gain_ok = sem("gain_ok")
        h_ok = sem("h_ok")
        hturn_ok = sem("hturn_ok")
        h_t_ok = [sem("h_t0_ok"), sem("h_t1_ok")]
        log_ok = sem("log_ok")
        log_out = sem("log_out")
        h_stored = sem("h_stored")
        made = sem("made")
        res_bn = sem("res_bn")

        def window(cb, j0=0, j1=KROWS):
            return slice(j0, j1), slice(key_start(cb), key_start(cb) + KCOLS)

        def grid(t):
            return t.rearrange("p (r c) -> p r c", c=GRID)

        def next_tile(t):
            return nc.s_assert_within(t + 1, 1, NT - 1, skip_runtime_bounds_check_because="only where t < NT - 1")

        block = ctx.enter_context(nc.Block())

        @block.sync
        def _(sp):
            def load(n, half, src, width=D):
                sp.wait_ge(w_lo_ok, n + 1)
                sp.dma_start(w_raw[:, half % 2, 0:width], src.rearrange("a p n -> p (a n)"))\
                  .then_inc(w_in[half % 2], 16)

            def load_x(t):
                for j in range(4):
                    sp.wait_ge(x_lo_ok, t * 4 + j + 1)
                    sp.dma_start(x_raw[:, j % 2, :].rearrange("p (k n) -> p k n", k=2),
                                 a["x_cols"][:, 2 * j:2 * j + 2, bass.ds(t * TILE, TILE)]).then_inc(x_in[j % 2], 16)

            load_x(0)
            with sp.Fori(0, NT) as t:
                with sp.Fori(0, HP) as p:
                    for j in range(NPAIR):
                        load(t * N_TILE + p * NPAIR + j, j, a["w_cxb"][bass.ds(p * NPAIR + j, 1), :, :])
                with sp.Fori(0, FB) as f:
                    n = t * N_TILE + N_CXB + f * 4
                    load(n, 0, a["w_gates"][bass.ds(f * 3, 1), :, :])
                    load(n + 1, 1, a["w_att"][bass.ds(f, 1), :, :], HP * P)
                    load(n + 2, 2, a["w_gates"][bass.ds(f * 3 + 1, 1), :, :])
                    load(n + 3, 3, a["w_gates"][bass.ds(f * 3 + 2, 1), :, :])
                for j in range(N_OUT):
                    load(t * N_TILE + N_CXB + N_MERGE + j, j, a["w_out"][j:j + 1, :, :])
                with sp.If(t < NT - 1):
                    load_x(next_tile(t))

        @block.gpsimd
        def _(pool):
            for s in (c_ok, conv_step, h_stored, *h_t_ok, hturn_ok, log_out, m_hi_ok, m_step, mom_ok, o_lo_ok, oturn_ok, *prob_t_ok, pv_ok, q_cut_ok, scores_ok, sig_a_ok, sig_c_ok, v_cut_ok, vturn_ok, y_lo_ok):
                pool.sem_inc(s, 1)
            pool.tensor_copy(ident_b[:, :], ident[:, :]).then_inc(const_ok, 1)
            pool.memset(zeros[:, :], 0.0).then_inc(const_ok, 1)
            pool.memset(neg_half[:, :], -0.5).then_inc(const_ok, 1)
            pool.dma_start(conv_wb[:, :], a["conv_wb"]).then_inc(const_in, 16)
            pool.dma_start(w_router[:, :, :].rearrange("p k n -> p (k n)"), a["w_router"]).then_inc(const_in, 16)
            pool.dma_start(ln_g[:, :], a["ln"][0:1, :].broadcast_to([P, D])).then_inc(const_in, 16)
            pool.dma_start(ln_b[:, :], a["ln"][1:2, :].broadcast_to([P, D])).then_inc(const_in, 16)
            def load_mask(t):
                scored = pool.to_reg(t * HP * 2 * NCB + 1)
                pool.wait_ge(const_ok, 3)
                pool.wait_ge(scores_ok, scored)
                pool.dma_start(mask[:, :], a["masks"].bitcast(BF16)[bass.ds(t, 1), :, :].rearrange("a p n -> p (a n)"))\
                    .then_inc(mask_in, 16)

            def load_pair(t, p):
                base = t * 4 + (t // 2) * 4
                g = t * HP + p
                pool.wait_ge(q_cut_ok, g + 1)
                pool.dma_start(q[:, :], qkv[bass.ds(p, 1), :, bass.ds(t * TILE, TILE)]
                               .rearrange("a p n -> p (a n)")).then_inc(qv_in, 16)

                def load_window(dst, first, landed):
                    pool.dma_start(dst[:, 0:KROWS * GRID],
                                   qkv[bass.ds(p + first, 1), :, bass.ds(base * GRID, KROWS * GRID)]
                                   .rearrange("a p n -> p (a n)")).then_inc(landed, 16)
                    pool.dma_start(dst[:, KROWS * GRID:], qkv[bass.ds(p + first, 1), :, NTOK:NCOL]
                                   .rearrange("a p n -> p (a n)")).then_inc(landed, 16)

                pool.wait_ge(v_cut_ok, g * NCB + 1)
                pool.wait_ge(vturn_ok, g * NCB + 1)
                load_window(val, 2 * HP, qv_in)
                pool.wait_ge(max_ok, g * 2 * NCB + 2)
                pool.wait_ge(scores_ok, g * 2 * NCB + 1)
                load_window(key, HP, kb_in)
                for r in range(ROWS_T):
                    at = (2 - t) // 2 * (4 * 64) + (ROWS_T - 1 - r) * 64
                    pool.dma_start(bias[r * 16:r * 16 + 16, :, :],
                                   a["bias_planes"][bass.ds(p * 2, 2), :, bass.ds(at, KROWS * GRID)]
                                   .rearrange("h i n -> i h n")).then_inc(kb_in, 16)
                landed, scored = pool.to_reg(g * 48 + 48), pool.to_reg(g * 2 * NCB + 1)
                pool.wait_ge(const_ok, 3)
                pool.wait_ge(qv_in, landed)
                pool.wait_ge(scores_ok, scored)
                pool.tensor_copy(q_cut[:, :].rearrange("p (b r i) -> p r b i", b=NCB, r=ROWS_T),
                                 q[:, :].rearrange("p (r b i) -> p r b i", b=NCB, r=ROWS_T)).then_inc(q_cut_ok, 1)
                for cb in range(NCB):
                    pool.tensor_copy(v_cut[:, cb * NKEY:(cb + 1) * NKEY].rearrange("p (r c) -> p r c", c=KCOLS),
                                     grid(val[:, 0:KROWS * GRID])[:, :, key_start(cb):key_start(cb) + KCOLS])\
                        .then_inc(v_cut_ok, 1)

            load_mask(0)
            load_pair(0, 0)
            with pool.Fori(0, NT) as t:
                made, read = pool.to_reg(t * N_TILE + 2), pool.to_reg(t * SUB_T + 1)
                pool.wait_ge(const_ok, 3)
                pool.wait_ge(w_used, made)
                pool.memset(prob[:, :, NKEY + NMETA:512], 0.0).then_inc(const_ok, 1)
                with pool.Fori(1, HP) as p:
                    load_pair(t, p)
                pool.wait_ge(h_stored, t * SUB_T * 16 + 1)
                pool.wait_ge(hturn_ok, t * SUB_T + 1)
                pool.dma_start(rows[:, :, :], a["x_rows"][bass.ds(t * TILE, TILE), :]
                               .rearrange("(s p) n -> p s n", p=P)).then_inc(rows_in, 16)
                with pool.If(t < NT - 1):
                    load_mask(next_tile(t))
                    load_pair(next_tile(t), 0)
                for s in range(SUB_T):
                    c = t * SUB_T + s
                    known = pool.to_reg(c + 2)
                    pool.wait_ge(const_ok, 3)
                    pool.wait_ge(mom_ok, known)
                    pool.tensor_scalar(mom[:, s, 1:2], mom[:, s, 1:2], EPS, None, ALU.add).then_inc(var_ok, 1)
                    pool.wait_ge(var_ok, c + 1)
                    pool.tensor_tensor(mom[:, s, 2:3], mom[:, s, 1:2], neg_half[:, 0:1], ALU.pow).then_inc(rstd_ok, 1)
                    pool.wait_ge(const_in, 64)
                    pool.wait_ge(norm_ok, c + 1)
                    pool.tensor_tensor(rows[:, s, :], rows[:, s, :], ln_g[:, :], ALU.mult).then_inc(gain_ok, 1)

        @block.scalar
        def _(act):
            for s in (max_ok, exp_ok, sum_ok, turn_ok, pv_ok, o_ok):
                act.sem_inc(s, 2)

            def high(n, half, width=D):
                act.wait_ge(w_in[half % 2], (n // 2) * 16 + 16)
                act.wait_ge(w_used, n + 1)
                act.activation(w_hi[:, half % 2, 0:width], w_raw[:, half % 2, 0:width], ACT.Copy)\
                   .then_inc(w_hi_ok, 1)

            def x_high(t):
                for j in range(4):
                    act.wait_ge(x_in[j % 2], t * 32 + (j // 2) * 16 + 16)
                    act.activation(x_hi[:, 2 * j:2 * j + 2, :].rearrange("p k n -> p (k n)"),
                                   x_raw[:, j % 2, :], ACT.Copy).then_inc(x_hi_ok, 1)

            x_high(0)
            high(0, 0)
            with act.Fori(0, NT) as t:
                n0 = t * N_TILE
                with act.Fori(0, HP) as p:
                    g = t * HP + p

                    def out_rows(cb, h):
                        u2 = (g * NCB + cb) * 2 + h
                        act.wait_ge(pv_ok, u2 + 4)
                        act.wait_ge(sum_ok, u2 + 3)
                        act.wait_ge(oturn_ok, g * NCB + cb + 1)
                        act.activation(o_rows[:, h * DH:(h + 1) * DH], outp[:, h * DH:(h + 1) * DH], ACT.Copy,
                                       scale=rsum[:, h:h + 1]).then_inc(o_ok, 1)

                    def out_high(cb):
                        act.wait_ge(oturn_ok, g * NCB + cb + 2)
                        act.activation(o_block(o_hi, p, cb),
                                       outp[:, P:2 * P].rearrange("p (r c) -> p r c", c=16), ACT.Copy)\
                           .then_inc(o_hi_ok, 1)

                    def y_high(f):
                        act.wait_ge(conv_step, (g * 2 + f) * 8 + 9)
                        act.activation(y_hi[:, bass.ds((p * 2 + f) * TILE, TILE)], y[:, :], ACT.Copy)\
                           .then_inc(y_hi_ok, 1)

                    for step, at in attention_schedule():
                        if step == "scores":
                            unit = g * NCB + at
                            if at:
                                out_rows(at - 1, 1)
                            act.wait_ge(vturn_ok, unit + 2)
                            act.wait_ge(pv_ok, unit * 2 + 1)
                            if at == 0:
                                act.activation(vmeta[:, :], turned[0:NMETA, NKEY:512], ACT.Copy)
                            act.activation(vkeys[:, at % 2, :], turned[:, 0:NKEY], ACT.Copy).then_inc(vkeys_ok, 1)
                            for h in range(2):
                                act.wait_ge(const_ok, t + 4)
                                act.wait_ge(max_ok, unit * 2 + h + 3)
                                act.wait_ge(turn_ok, unit * 2 + h + 1)
                                act.wait_ge(sum_ok, unit * 2 + h + 1)
                                act.activation(prob[:, h, 0:NKEY + NMETA], sbias[:, h, :], ACT.Exp,
                                               bias=nmax[:, h:h + 1], accum_out=ssum[:, h:h + 1])\
                                   .then_inc(exp_ok, 1)
                        elif step == "turn0":
                            if at:
                                out_high(at - 1)
                        elif step == "turn1":
                            unit = g * NCB + at
                            act.wait_ge(turn_ok, unit * 2 + 4)
                            act.wait_ge(pv_ok, unit * 2 + 3)
                            act.activation(prob_t[:, 1, :], turned[:, :], ACT.Copy).then_inc(prob_t_ok[1], 1)
                            out_rows(at, 0)
                        elif step == "drain_values":
                            out_rows(at, 1)
                        elif step == "drain_turn":
                            out_high(at)
                        else:
                            grp, k = at
                            n = n0 + p * NPAIR + grp
                            if k == 0:
                                high(n + 1, grp + 1)
                            if grp == 3 and k == 2:
                                y_high(0)
                            if grp % 3 == 0 and k == KD - 1:
                                f = g * 2 + grp // 3
                                act.wait_ge(w_used, n + 3)
                                act.wait_ge(conv_step, f * 8 + 1)
                                act.activation(c_sb[:, :], bank[0][:, :], ACT.Copy).then_inc(c_ok, 1)
                    y_high(1)
                with act.Fori(0, FB) as f:
                    n, m = n0 + N_CXB + f * 4, t * FB + f
                    high(n + 1, 1, HP * P)
                    high(n + 2, 2)
                    act.wait_ge(w_used, n + 3)
                    act.wait_ge(y_lo_ok, t * FB + FB + 1)
                    act.wait_ge(o_lo_ok, t * 16 + 17)
                    act.wait_ge(m_step, m * 3 + 1)
                    act.activation(sig_a[:, :], bank[0][:, :], ACT.Sigmoid).then_inc(sig_a_ok, 1)
                    high(n + 3, 3)
                    act.wait_ge(w_used, n + 5)
                    act.activation(sig_c[:, :], bank[2][:, :], ACT.Sigmoid).then_inc(sig_c_ok, 1)
                    high(n + 4, 4)
                    act.wait_ge(m_step, m * 3 + 4)
                    act.activation(m_hi[:, bass.ds(f * TILE, TILE)], m_att[:, :], ACT.Copy).then_inc(m_hi_ok, 1)
                n1 = n0 + N_CXB + N_MERGE
                act.wait_ge(w_used, n1 + 2)
                for j in range(1, N_OUT):
                    act.wait_ge(w_in[j % 2], ((n1 + j) // 2) * 16 + 16)
                    act.activation(out_hi[j], w_raw[:, j % 2, :], ACT.Copy).then_inc(w_hi_ok, 1)
                with act.If(t < NT - 1):
                    x_high(t + 1)

                def store(s):
                    c = t * SUB_T + s
                    act.wait_ge(h_ok, c + 1)
                    act.dma_start(h_rows[bass.ds(c * P, P), :], rows[:, s, :]).then_inc(h_stored, 16)

                def copy_turned(s):
                    act.wait_ge(hturn_ok, t * SUB_T + s + 2)
                    act.activation(h_t[:, 0:512], bank[3][:, :], ACT.Copy).then_inc(h_t_ok[0], 1)

                def copy_logits(s):
                    c = t * SUB_T + s
                    act.wait_ge(log_ok, c + 1)
                    act.activation(logits[:, bass.ds(c * NLOG, NLOG)], bank[5][:, 0:NLOG], ACT.Copy)\
                       .then_inc(log_out, 1)

                store(0)
                store(1)
                with act.If(t < NT - 1):
                    act.wait_ge(w_in[0], (n0 + N_TILE) // 2 * 16 + 16)
                    act.wait_ge(w_used, n1 + 3)
                    act.activation(w_hi[:, 0, :], w_raw[:, 0, :], ACT.Copy).then_inc(w_hi_ok, 1)
                copy_turned(0)
                store(2)
                for s in range(SUB_T):
                    copy_logits(s)
                    if s == SUB_T - 2:
                        store(SUB_T - 1)
                    if s < SUB_T - 1:
                        copy_turned(s + 1)
            act.wait_ge(h_stored, NSUB * 16 + 1)

        @block.vector
        def _(dve):
            dve.sem_inc(w_lo_ok, 2)
            dve.sem_inc(x_lo_ok, 2)
            dve.wait_ge(const_in, 64)

            def low(n, half, width=D):
                dve.wait_ge(w_hi_ok, n + 1)
                dve.wait_ge(w_used, n + 1)
                dve.tensor_tensor(w_lo[:, half % 2, 0:width], w_raw[:, half % 2, 0:width],
                                  w_hi[:, half % 2, 0:width].bitcast(F32), ALU.subtract).then_inc(w_lo_ok, 1)

            def x_low(t):
                for j in range(4):
                    dve.wait_ge(x_hi_ok, t * 4 + j + 1)
                    dve.tensor_tensor(x_lo[:, 2 * j:2 * j + 2, :].rearrange("p k n -> p (k n)"), x_raw[:, j % 2, :],
                                      x_hi[:, 2 * j:2 * j + 2, :].rearrange("p k n -> p (k n)").bitcast(F32),
                                      ALU.subtract).then_inc(x_lo_ok, 1)

            x_low(0)
            low(0, 0)
            with dve.Fori(0, NT) as t:
                n0 = t * N_TILE
                with dve.Fori(0, HP) as p:
                    g = t * HP + p

                    def one_over_sum(cb, h):
                        u2 = (g * NCB + cb) * 2 + h
                        dve.wait_ge(exp_ok, u2 + 3)
                        dve.wait_ge(o_ok, u2 + 1)
                        dve.reciprocal(rsum[:, h:h + 1], ssum[:, h:h + 1]).then_inc(sum_ok, 1)

                    def out_low(cb):
                        dve.wait_ge(o_hi_ok, g * NCB + cb + 1)
                        dve.tensor_tensor(o_block(o_lo, p, cb),
                                          outp[:, P:2 * P].rearrange("p (r c) -> p r c", c=16),
                                          o_block(o_hi, p, cb).bitcast(F32), ALU.subtract).then_inc(o_lo_ok, 1)

                    def y_low(f):
                        dve.wait_ge(y_hi_ok, g * 2 + f + 1)
                        at = bass.ds((p * 2 + f) * TILE, TILE)
                        dve.tensor_tensor(y_lo[:, at], y[:, :], y_hi[:, at].bitcast(F32), ALU.subtract)\
                           .then_inc(y_lo_ok, 1)

                    for step, at in attention_schedule():
                        if step == "scores":
                            for h in range(2):
                                u2 = (g * NCB + at) * 2 + h
                                here, used = dve.to_reg(u2 + 2), dve.to_reg(u2 + 1)
                                dve.wait_ge(const_ok, 3)
                                dve.wait_ge(scores_ok, here)
                                dve.wait_ge(exp_ok, used)
                                dve.tensor_tensor_reduce(
                                    out=sbias[:, h, NKEY:], in0=score[h][:, NKEY:NKEY + NMETA], in1=zeros[:, :],
                                    scale=1.0, scalar=NEG, op0=ALU.add, op1=ALU.max,
                                    accum_out=smeta[:, h:h + 1]).then_inc(max_step, 1)
                                meta_done, landed = dve.to_reg(u2 * 2 + 1), dve.to_reg((g + 1) * KB_DMAS * 16)
                                dve.wait_ge(const_ok, 3)
                                dve.wait_ge(max_step, meta_done)
                                dve.wait_ge(kb_in, landed)
                                dve.tensor_tensor_reduce(
                                    out=sbias[:, h, 0:NKEY].rearrange("p (r c) -> p r c", c=KCOLS),
                                    in0=score[h][:, 0:NKEY].rearrange("p (r c) -> p r c", c=KCOLS),
                                    in1=bias[:, h, :].rearrange("p (r c) -> p r c", c=64)
                                    [:, :, 16 + key_start(at) - 16 * at:][:, :, 0:KCOLS],
                                    scale=1.0, scalar=smeta[:, h:h + 1], op0=ALU.add, op1=ALU.max,
                                    accum_out=smax[:, h:h + 1]).then_inc(max_step, 1)
                                dve.wait_ge(max_step, u2 * 2 + 2)
                                dve.tensor_scalar(nmax[:, h:h + 1], smax[:, h:h + 1], -1.0, None, ALU.mult)\
                                   .then_inc(max_ok, 1)
                        elif step == "turn0":
                            one_over_sum(at, 0)
                            unit = g * NCB + at
                            dve.wait_ge(turn_ok, unit * 2 + 3)
                            dve.wait_ge(pv_ok, unit * 2 + 2)
                            dve.tensor_copy(prob_t[:, 0, :], turned[:, :]).then_inc(prob_t_ok[0], 1)
                            one_over_sum(at, 1)
                            if at:
                                out_low(at - 1)
                        elif step == "drain_turn":
                            out_low(at)
                        elif step == "chunk":
                            grp, k = at
                            n = n0 + p * NPAIR + grp
                            f = g * 2 + grp // 3
                            wb = lambda j: conv_wb[:, bass.ds(p * 8 + grp // 3 * 4 + j, 1)]
                            edge = lambda e: edges[:, bass.ds((p * 2 + grp // 3) * NEDGE + e, 1)]
                            if k == 0:
                                low(n + 1, grp + 1)
                            if grp == 3 and k == 3:
                                y_low(0)
                            if k == 1 and grp % 3 == 2:
                                dve.wait_ge(w_used, n + 2)
                                dve.wait_ge(c_ok, f + 2)
                                dve.tensor_tensor(u[:, 1:TILE + 1], c_sb[:, :], bank[1][:, :], ALU.mult)\
                                   .then_inc(conv_step, 1)
                                dve.tensor_copy(u[:, 0:1], edge(t * 2)).then_inc(conv_step, 1)
                                dve.tensor_copy(u[:, TILE + 1:], edge(t + RIGHT)).then_inc(conv_step, 1)
                                dve.wait_ge(conv_step, f * 8 + 4)
                                dve.tensor_copy(edge(t * 3 + 2), u[:, TILE:TILE + 1]).then_inc(conv_step, 1)
                                dve.wait_ge(y_lo_ok, f + 1)
                                dve.tensor_scalar(y[:, :], u[:, 0:TILE], wb(0), wb(3), ALU.mult, ALU.add)\
                                   .then_inc(conv_step, 1)
                                for j in (1, 2):
                                    dve.wait_ge(conv_step, f * 8 + 4 + j + 1)
                                    dve.scalar_tensor_tensor(y[:, :], u[:, j:TILE + j], wb(j), y[:, :], ALU.mult, ALU.add)\
                                       .then_inc(conv_step, 1)
                            if k == KD - 1 and grp % 3 == 2:
                                dve.wait_ge(w_used, n + 3)
                                dve.wait_ge(conv_step, f * 8 + 8)
                                dve.tensor_tensor(y[:, :], y[:, :], bank[2][:, :], ALU.mult).then_inc(conv_step, 1)
                    y_low(1)
                with dve.Fori(0, FB) as f:
                    n, m = n0 + N_CXB + f * 4, t * FB + f
                    low(n + 1, 1, HP * P)
                    low(n + 2, 2)
                    dve.wait_ge(w_used, n + 4)
                    dve.wait_ge(sig_a_ok, m + 2)
                    dve.wait_ge(m_hi_ok, m + 1)
                    dve.tensor_tensor(m_att[:, :], sig_a[:, :], bank[1][:, :], ALU.mult).then_inc(m_step, 1)
                    low(n + 3, 3)
                    low(n + 4, 4)
                    dve.wait_ge(w_used, n + 6)
                    dve.wait_ge(sig_c_ok, m + 2)
                    dve.tensor_tensor(sig_c[:, :], sig_c[:, :], bank[7][:, :], ALU.mult).then_inc(m_step, 1)
                    dve.wait_ge(m_step, m * 3 + 3)
                    dve.tensor_tensor(m_att[:, :], m_att[:, :], sig_c[:, :], ALU.add).then_inc(m_step, 1)
                    dve.wait_ge(m_hi_ok, m + 2)
                    at = bass.ds(f * TILE, TILE)
                    dve.tensor_tensor(m_lo[:, at], m_att[:, :], m_hi[:, at].bitcast(F32), ALU.subtract)\
                       .then_inc(m_lo_ok, 1)
                n1 = n0 + N_CXB + N_MERGE
                dve.wait_ge(w_used, n1 + 2)
                for j in range(1, N_OUT):
                    dve.wait_ge(w_hi_ok, n1 + j + 1)
                    dve.tensor_tensor(out_lo[j], w_raw[:, j % 2, :], out_hi[j].bitcast(F32), ALU.subtract)\
                       .then_inc(w_lo_ok, 1)
                with dve.If(t < NT - 1):
                    x_low(t + 1)
                dve.wait_ge(rows_in, t * 16 + 16)

                def residual(s, half, step=None):
                    if s < SUB_T - 1:
                        dve.wait_ge(made, t * 4 + step)
                    else:
                        dve.wait_ge(w_used, n1 + 4 * half + 6)
                    part = rows[:, s, half * 512:(half + 1) * 512]
                    dve.scalar_tensor_tensor(part, part, ALPHA, bank[OUT_BANK[s][half]][:, :], ALU.mult, ALU.add)\
                       .then_inc(res_step, 1)

                def moments(s):
                    c = t * SUB_T + s
                    dve.wait_ge(res_step, c * 2 + 2)
                    dve.wait_ge(mom_ok, c + 1)
                    for half in range(2):
                        dve.bn_stats(stats[:, half * 6:half * 6 + 6], rows[:, s, half * 512:(half + 1) * 512])\
                           .then_inc(res_bn, 1)
                    taken = dve.to_reg(c * 2 + 2)
                    dve.wait_ge(const_in, 64)
                    dve.wait_ge(res_bn, taken)
                    dve.bn_aggr(mom[:, s, 0:2], stats[:, :]).then_inc(mom_ok, 1)

                def norm(s):
                    dve.wait_ge(rstd_ok, t * SUB_T + s + 1)
                    dve.tensor_scalar(rows[:, s, :], rows[:, s, :], mom[:, s, 0:1], mom[:, s, 2:3],
                                      ALU.subtract, ALU.mult).then_inc(norm_ok, 1)

                def offset(s):
                    dve.wait_ge(gain_ok, t * SUB_T + s + 1)
                    dve.tensor_tensor(rows[:, s, :], rows[:, s, :], ln_b[:, :], ALU.add).then_inc(h_ok, 1)

                def copy_turned(s):
                    dve.wait_ge(hturn_ok, t * SUB_T + s + 2)
                    dve.tensor_copy(h_t[:, 512:], bank[4][:, :]).then_inc(h_t_ok[1], 1)

                for s in range(2):
                    for half in range(2):
                        residual(s, half, half + 1)
                    moments(s)
                    norm(s)
                offset(0)
                residual(2, 0, 3)
                offset(1)
                residual(2, 1, 4)
                moments(2)
                norm(2)
                with dve.If(t < NT - 1):
                    dve.wait_ge(w_hi_ok, n0 + N_TILE + 1)
                    dve.tensor_tensor(w_lo[:, 0, :], w_raw[:, 0, :], w_hi[:, 0, :].bitcast(F32), ALU.subtract)\
                       .then_inc(w_lo_ok, 1)
                copy_turned(0)
                residual(3, 0)
                offset(2)
                residual(3, 1)
                moments(3)
                copy_turned(1)
                norm(3)
                copy_turned(2)
                offset(3)
                copy_turned(3)

        @block.tensor
        def _(pe):
            pe.sem_inc(w_used, 2)
            pe.wait_ge(const_in, 64)

            def product(ps, half, w, hi, lo, start, stop):
                pe.matmul(ps, w_hi[:, half % 2, w], hi, start=start, stop=False)
                pe.matmul(ps, w_hi[:, half % 2, w], lo, start=False, stop=False)
                return pe.matmul(ps, w_lo[:, half % 2, w], hi, start=False, stop=stop)

            with pe.Fori(0, NT) as t:
                n0 = t * N_TILE
                split, landed, copied = pe.to_reg(t * 4 + 6), pe.to_reg(t * 16 + 16), pe.to_reg(t * SUB_T + 1)
                pe.wait_ge(const_in, 64)
                pe.wait_ge(x_lo_ok, split)
                pe.wait_ge(mask_in, landed)
                pe.wait_ge(log_out, copied)
                with pe.Fori(0, HP) as p:
                    g = t * HP + p

                    def values(cb, h):
                        u2 = (g * NCB + cb) * 2 + h
                        pe.wait_ge(vkeys_ok, g * NCB + cb + 1)
                        pe.wait_ge(prob_t_ok[h], g * NCB + cb + 2)
                        if h == 0:
                            pe.wait_ge(o_lo_ok, g * NCB + cb + 1)
                        else:
                            pe.wait_ge(o_ok, u2 + 2)
                        ps, c = outp[:, h * DH:(h + 1) * DH], slice(h * DH, (h + 1) * DH)
                        for j in range(NKEY // P):
                            pe.matmul(ps, prob_t[:, h, j * P:(j + 1) * P],
                                      vkeys[:, cb % 2, j * P + h * DH:j * P + (h + 1) * DH], start=(j == 0), stop=False)
                        pe.matmul(ps, prob_t[0:NMETA, h, NKEY:512], vmeta[:, c], start=False, stop=True)\
                          .then_inc(pv_ok, 1)

                    def turn_probs(cb, h):
                        pe.wait_ge(exp_ok, (g * NCB + cb) * 2 + h + 3)
                        for j in range(4):
                            last = pe.transpose(turned[:, j * P:(j + 1) * P], prob[:, h, j * P:(j + 1) * P], ident[:, :])
                        last.then_inc(turn_ok, 1)

                    def turn_outputs(cb):
                        pe.wait_ge(o_ok, (g * NCB + cb) * 2 + 4)
                        pe.transpose(outp[:, P:2 * P], o_rows[:, :], ident[:, :]).then_inc(oturn_ok, 1)

                    for step, at in attention_schedule():
                        unit = g * NCB + (at if step != "chunk" else 0)
                        if step == "scores":
                            if at:
                                values(at - 1, 1)
                            pe.wait_ge(kb_in, (g + 1) * KB_DMAS * 16)
                            pe.wait_ge(q_cut_ok, g + 2)
                            pe.wait_ge(v_cut_ok, unit + 2)
                            pe.wait_ge(prob_t_ok[1], unit + 1)
                            for j in range(NKEY // P):
                                last = pe.transpose(turned[:, j * P:(j + 1) * P],
                                                    v_cut[:, at * NKEY + j * P:at * NKEY + (j + 1) * P], ident[:, :])
                            if at == 0:
                                last = pe.matmul(turned[0:NMETA, NKEY:512], val[:, KROWS * GRID:], ident[:, :],
                                                 start=True, stop=True)
                            last.then_inc(vturn_ok, 1)
                            rr, cc = window(at)
                            for h in range(2):
                                hh = slice(h * DH, (h + 1) * DH)
                                qs = q_cut[hh, at * P:(at + 1) * P]
                                pe.wait_ge(max_ok, unit * 2 + h + 1)
                                pe.matmul(score[h][:, 0:NKEY].rearrange("p (r c) -> p r c", c=KCOLS), qs,
                                          grid(key[hh, 0:KROWS * GRID])[:, rr, cc], start=True, stop=False)
                                pe.matmul(score[h][:, 0:NKEY], ident_b[:, :], mask[:, at * NKEY:(at + 1) * NKEY],
                                          start=False, stop=True)
                                pe.matmul(score[h][:, NKEY:NKEY + NMETA], qs, key[hh, KROWS * GRID:],
                                          start=True, stop=True).then_inc(scores_ok, 1)
                        elif step == "turn0":
                            pe.wait_ge(vkeys_ok, unit + 1)
                            turn_probs(at, 0)
                            if at:
                                turn_outputs(at - 1)
                        elif step == "turn1":
                            pe.wait_ge(prob_t_ok[0], unit + 2)
                            turn_probs(at, 1)
                            values(at, 0)
                        elif step == "drain_values":
                            values(at, 1)
                        elif step == "drain_turn":
                            turn_outputs(at)
                        else:
                            grp, k = at
                            n, f = n0 + p * NPAIR + grp, g * 2 + grp // 3
                            if k == 0:
                                pe.wait_ge(w_lo_ok, n + 3)
                                if grp % 3 == 0:
                                    pe.wait_ge(c_ok, f + 1)
                                elif grp % 3 == 1:
                                    pe.wait_ge(conv_step, f * 8 + 1)
                                else:
                                    pe.wait_ge(conv_step, f * 8 + 1)
                            last = product(bank[grp % 3][:, :], grp, slice(k * P, (k + 1) * P), x_hi[:, k, :], x_lo[:, k, :],
                                           k == 0, k == KD - 1)
                            if k == KD - 1:
                                last.then_inc(w_used, 1)
                y_split, o_split = pe.to_reg(t * FB + FB + 1), pe.to_reg(t * 16 + 17)
                pe.wait_ge(const_in, 64)
                pe.wait_ge(y_lo_ok, y_split)
                pe.wait_ge(o_lo_ok, o_split)
                with pe.Fori(0, FB) as f:
                    n, m = n0 + N_CXB + f * 4, t * FB + f

                    def branch(j, ps, nk, hi, lo, free, value):
                        pe.wait_ge(w_lo_ok, n + j + 3)
                        pe.wait_ge(free, value + 1)
                        for k in range(nk):
                            last = product(ps[:, :], j, slice(k * P, (k + 1) * P), hi(k), lo(k), k == 0, k == nk - 1)
                        last.then_inc(w_used, 1)

                    cut = lambda x: lambda k: x[:, k * TILE:(k + 1) * TILE]
                    xc = lambda x: lambda k: x[:, k, :]
                    branch(0, bank[0], KD, xc(x_hi), xc(x_lo), sig_a_ok, m)
                    branch(1, bank[1], HP, cut(o_hi), cut(o_lo), m_step, m * 3)
                    branch(2, bank[2], KD, xc(x_hi), xc(x_lo), sig_c_ok, m)
                    branch(3, bank[7], KD, cut(y_hi), cut(y_lo), m_step, m * 3)
                pe.wait_ge(m_lo_ok, t * FB + FB)
                n1 = n0 + N_CXB + N_MERGE

                def out_product(subtiles, half):
                    for j in range(4 * half, 4 * half + 4):
                        if subtiles[0] == 0:
                            pe.wait_ge(w_lo_ok, n1 + j + 3)
                        for kk in range(2):
                            k, w = 2 * (j % 4) + kk, slice(kk * 512, (kk + 1) * 512)
                            for s in subtiles:
                                ps = bank[OUT_BANK[s][half]][:, :]
                                ms = slice(k * TILE + s * P, k * TILE + (s + 1) * P)
                                pe.matmul(ps, m_hi[:, ms], out_hi[j][:, w], start=(k == 0), stop=False)
                                pe.matmul(ps, m_hi[:, ms], out_lo[j][:, w], start=False, stop=False)
                                last = pe.matmul(ps, m_lo[:, ms], out_hi[j][:, w], start=False, stop=(k == KD - 1))
                        if subtiles[-1] == SUB_T - 1:
                            last.then_inc(w_used, 1)
                    if subtiles[-1] < SUB_T - 1:
                        last.then_inc(made, 1)

                def turn(s):
                    c = t * SUB_T + s
                    pe.wait_ge(h_ok, c + 1)
                    pe.wait_ge(h_t_ok[0], c + 1)
                    pe.wait_ge(h_t_ok[1], c + 1)
                    for k in range(KD):
                        last = pe.transpose(bank[3 + k // 4][:, (k % 4) * P:(k % 4 + 1) * P],
                                            rows[:, s, k * P:(k + 1) * P], ident[:, :])
                    last.then_inc(hturn_ok, 1)

                def route_logits(s):
                    c = t * SUB_T + s
                    pe.wait_ge(h_t_ok[0], c + 2)
                    pe.wait_ge(h_t_ok[1], c + 2)
                    pe.wait_ge(log_out, c + 1)
                    if s == 0:
                        pe.wait_ge(res_step, t * 8 + 4)
                    for k in range(KD):
                        last = pe.matmul(bank[5][:, 0:NLOG], h_t[:, k * P:(k + 1) * P], w_router[:, k, :],
                                         start=(k == 0), stop=(k == KD - 1))
                    last.then_inc(log_ok, 1)

                out_product((0, 1), 0)
                out_product((0, 1), 1)
                out_product((2,), 0)
                out_product((2,), 1)
                out_product((3,), 0)
                turn(0)
                out_product((3,), 1)
                for s in range(SUB_T):
                    route_logits(s)
                    if s < SUB_T - 1:
                        turn(s + 1)


def route(nc, logits, ident, r):
    NP = 2 * NSUB
    MARKS = 4
    with ExitStack() as ctx:
        sb = lambda n, s, d=F32: ctx.enter_context(nc.sbuf_tensor(n, s, d))
        sem = lambda n: ctx.enter_context(nc.semaphore(n))
        ints = sb("ints", [P, 512], I32)
        lane = sb("lane", [P, P])
        block_no = sb("block_no", [P, NPLAN])
        edge128 = sb("edge128", [P, NSUB])
        token = sb("token", [P, NP])
        spare = sb("spare", [P, 1])
        rank_g, rank_e = sb("rank_g", [P, NG]), sb("rank_e", [P, NEXP])
        ones = sb("ones", [P, NEXP])
        below = sb("below", [P, P], BF16)
        all_one = sb("all_one", [P, P], BF16)
        gdiff, gexp, ghot = (sb(n, [P, NSUB, NG]) for n in ("gdiff", "gexp", "ghot"))
        masked = sb("masked", [P, NSUB, NEXP])
        weight = sb("weight", [P, NSUB, NEXP])
        hot = [sb(f"hot{c}", [P, NSUB, NEXP]) for c in range(2)]
        chosen = sb("chosen", [P, NSUB, NEXP], BF16)
        col = [sb(f"col{j}", [P, NSUB]) for j in range(8)]
        gmax, gsum, best, top1, top2, ediff, e2, den = col
        place = sb("place", [P, NSUB, NEXP])
        count, blocks, pend, pstart = (sb(n, [P, NEXP]) for n in ("count", "blocks", "pend", "pstart"))
        over = sb("over", [P, NEXP, NSUB])
        under, begins = sb("under", [P, NEXP]), sb("begins", [P, NEXP])
        plan_col = sb("plan_col", [P, 2])
        one_row = sb("one_row", [1, NPLAN])
        fresh_f, visit_f = sb("fresh_f", [1, NPLAN]), sb("visit_f", [1, NPLAN])
        slot_f, slot_i = sb("slot_f", [P, NP]), sb("slot_i", [P, NP], I32)
        code, empty, second = (sb(n, [P, NPLAN]) for n in ("code", "empty", "second"))
        part_i = sb("part_i", [P, 2, NP], I32)
        part_f = sb("part_f", [P, 2, NP])
        at_lane = sb("at_lane", [P, MARKS, P])
        at_block = sb("at_block", [P, MARKS, NPLAN])
        ranks_ps = ctx.enter_context(nc.psum_tensor("ranks_ps", [P, 512], F32))
        count_ps = ctx.enter_context(nc.psum_tensor("count_ps", [P, 512], F32))
        table_ps = ctx.enter_context(nc.psum_tensor("table_ps", [P, 512], F32))
        plan_ps = ctx.enter_context(nc.psum_tensor("plan_ps", [P, 512], F32))
        iota_step = sem("iota_step")
        gdiff_ok, gexp_ok = sem("gdiff_ok"), sem("gexp_ok")
        ediff_ok, e2_ok = sem("ediff_ok"), sem("e2_ok")
        chosen_ok = sem("chosen_ok")
        counted = sem("counted")
        plan_ok = sem("plan_ok")
        plan_rows = sem("plan_rows")
        hots_ok = sem("hots_ok")
        hots_used = sem("hots_used")
        step = sem("route_step")
        block = ctx.enter_context(nc.Block())

        def spread(t, n):
            return t.unsqueeze(2).broadcast_to([t.shape[0], t.shape[1], n])

        @block.gpsimd
        def _(pool):
            done = [0]

            def link(ins):
                done[0] += 1
                ins.then_inc(iota_step, 1)
                pool.wait_ge(iota_step, done[0])

            for t, pattern, mult, base in ((lane, [[1, P]], 0, 0), (block_no, [[1, NPLAN]], 0, 0),
                                           (edge128, [[P, NSUB]], 0, 0), (token, [[P, NP]], 1, 1),
                                           (spare, [[1, 1]], 1, 2 * NTOK + 1),
                                           (rank_g, [[-1, NG]], 0, NG), (rank_e, [[-1, NEXP]], 0, NEXP)):
                n = pattern[0][1]
                link(pool.iota(ints[:, 0:n], pattern=pattern, base=base, channel_multiplier=mult))
                link(pool.tensor_copy(t[:, :], ints[:, 0:n]))
            link(pool.memset(ones[:, :], 1.0))
            link(pool.memset(all_one[:, :], 1.0))
            link(pool.affine_select(out=below[:, :], in_=all_one[:, :], compare_op=ALU.is_gt, fill=0.0, base=0,
                                    pattern=[[1, P]], channel_multiplier=-1))

        @block.scalar
        def _(act):
            act.wait_ge(gdiff_ok, 1)
            act.activation(gexp[:, :, :].rearrange("p s g -> p (s g)"), gdiff[:, :, :].rearrange("p s g -> p (s g)"),
                           ACT.Exp).then_inc(gexp_ok, 1)
            act.wait_ge(ediff_ok, 1)
            act.activation(e2[:, :], ediff[:, :], ACT.Exp).then_inc(e2_ok, 1)

        @block.vector
        def _(dve):
            done = [0]

            def link(ins):
                done[0] += 1
                ins.then_inc(step, 1)
                dve.wait_ge(step, done[0])

            lg = logits[:, :].rearrange("p (s n) -> p s n", n=NLOG)
            dve.wait_ge(iota_step, 17)
            link(dve.reduce_max(gmax[:, :], lg[:, :, 0:NG], AX.X))
            dve.tensor_tensor(gdiff[:, :, :], lg[:, :, 0:NG], spread(gmax[:, :], NG), ALU.subtract).then_inc(gdiff_ok, 1)
            dve.wait_ge(gdiff_ok, 1)
            link(dve.tensor_scalar(ghot[:, :, :], gdiff[:, :, :], 0.0, None, ALU.is_equal))
            link(dve.tensor_tensor(ghot[:, :, :], ghot[:, :, :],
                                   rank_g[:, :].unsqueeze(1).broadcast_to([P, NSUB, NG]), ALU.mult))
            link(dve.reduce_max(best[:, :], ghot[:, :, :], AX.X))
            link(dve.tensor_tensor(ghot[:, :, :], ghot[:, :, :], spread(best[:, :], NG), ALU.is_equal))
            dve.wait_ge(gexp_ok, 1)
            link(dve.reduce_sum(gsum[:, :], gexp[:, :, :], AX.X))
            link(dve.tensor_scalar(ghot[:, :, :], ghot[:, :, :], -NEG, NEG, ALU.mult, ALU.add))
            link(dve.tensor_tensor(
                masked[:, :, :].rearrange("p s (g e) -> p s g e", g=NG),
                lg[:, :, NG:].rearrange("p s (g e) -> p s g e", g=NG),
                ghot[:, :, :].unsqueeze(3).broadcast_to([P, NSUB, NG, EPG]), ALU.add))
            for c, top in ((0, top1), (1, top2)):
                link(dve.reduce_max(top[:, :], masked[:, :, :], AX.X))
                link(dve.tensor_tensor(weight[:, :, :], masked[:, :, :], spread(top[:, :], NEXP), ALU.is_equal))
                link(dve.tensor_tensor(weight[:, :, :], weight[:, :, :],
                                       rank_e[:, :].unsqueeze(1).broadcast_to([P, NSUB, NEXP]), ALU.mult))
                link(dve.reduce_max(best[:, :], weight[:, :, :], AX.X))
                link(dve.tensor_tensor(hot[c][:, :, :], weight[:, :, :], spread(best[:, :], NEXP), ALU.is_equal))
                if c == 0:
                    link(dve.scalar_tensor_tensor(masked[:, :, :], hot[0][:, :, :], 3 * NEG, masked[:, :, :],
                                                  ALU.mult, ALU.add))
            dve.tensor_tensor(chosen[:, :, :], hot[0][:, :, :], hot[1][:, :, :], ALU.add).then_inc(chosen_ok, 1)
            dve.tensor_tensor(ediff[:, :], top2[:, :], top1[:, :], ALU.subtract).then_inc(ediff_ok, 1)
            dve.wait_ge(e2_ok, 1)
            link(dve.tensor_scalar(den[:, :], e2[:, :], 1.0, None, ALU.add))
            link(dve.tensor_tensor(den[:, :], den[:, :], gsum[:, :], ALU.mult))
            link(dve.reciprocal(r["gates"][:, 0:NSUB], den[:, :]))
            link(dve.tensor_tensor(r["gates"][:, NSUB:], r["gates"][:, 0:NSUB], e2[:, :], ALU.mult))
            dve.wait_ge(counted, 1)
            link(dve.tensor_copy(count[:, :], count_ps[:, 0:NEXP]))
            link(dve.tensor_tensor(over[:, :, :], spread(count[:, :], NSUB),
                                   edge128[:, :].unsqueeze(1).broadcast_to([P, NEXP, NSUB]), ALU.is_gt))
            link(dve.reduce_sum(blocks[:, :], over[:, :, :], AX.X))
            link(dve.tensor_tensor_scan(pend[:, :], ones[:, :], blocks[:, :], 0.0, ALU.mult, ALU.add))
            link(dve.tensor_tensor(pstart[:, :], pend[:, :], blocks[:, :], ALU.subtract))
            link(dve.tensor_scalar(under[:, :], pend[:, :], token[:, 0:1], None, ALU.is_lt))
            link(dve.reduce_sum(plan_col[:, 0:1], under[:, :], AX.X))
            link(dve.tensor_scalar(plan_col[:, 0:1], plan_col[:, 0:1], float(NEXP - 1), None, ALU.min))
            link(dve.tensor_scalar(under[:, :], blocks[:, :], 0.0, None, ALU.is_gt))
            link(dve.tensor_scalar(begins[:, :], pstart[:, :], 1.0, token[:, 0:1], ALU.add, ALU.is_equal))
            link(dve.tensor_tensor(under[:, :], begins[:, :], under[:, :], ALU.mult))
            dve.reduce_sum(plan_col[:, 1:2], under[:, :], AX.X).then_inc(plan_ok, 1)
            link(dve.tensor_copy(r["used"][:, :], pend[0:1, NEXP - 1:NEXP]))
            link(dve.memset(one_row[:, :], 1.0))
            link(dve.tensor_scalar(pstart[:, :], pstart[:, :], float(P), None, ALU.mult))
            link(dve.tensor_tensor(place[:, :, :], ranks_ps[:, 0:NSUB * NEXP].rearrange("p (s e) -> p s e", e=NEXP),
                                   pstart[:, :].unsqueeze(1).broadcast_to([P, NSUB, NEXP]), ALU.add))
            for c in range(2):
                link(dve.tensor_tensor(weight[:, :, :], hot[c][:, :, :], place[:, :, :], ALU.mult))
                link(dve.reduce_sum(slot_f[:, c * NSUB:(c + 1) * NSUB], weight[:, :, :], AX.X))
            link(dve.tensor_copy(slot_i[:, :], slot_f[:, :]))
            link(dve.tensor_scalar(part_i[:, 0, :], slot_i[:, :], P - 1, None, ALU.bitwise_and))
            link(dve.tensor_scalar(part_i[:, 1, :], slot_i[:, :], 7, None, ALU.logical_shift_right))
            link(dve.tensor_copy(part_f[:, :, :], part_i[:, :, :]))
            for g in range(NP):
                dve.wait_ge(hots_used, g + 1)
                dve.tensor_scalar(at_lane[:, g % MARKS, :], lane[:, :], part_f[:, 0, g:g + 1], None, ALU.is_equal)
                dve.tensor_scalar(at_block[:, g % MARKS, :], block_no[:, :], part_f[:, 1, g:g + 1],
                                  token[:, g:g + 1], ALU.is_equal, ALU.mult).then_inc(hots_ok, 1)
            dve.wait_ge(plan_rows, 1)
            link(dve.tensor_copy(r["owner"][:, :], plan_ps[0:1, 0:NPLAN]))
            link(dve.tensor_copy(fresh_f[:, :], plan_ps[0:1, P:P + NPLAN]))
            link(dve.tensor_tensor_scan(visit_f[:, :], one_row[:, :], fresh_f[:, :], -1.0, ALU.mult, ALU.add))
            link(dve.tensor_copy(r["fresh"][:, :], fresh_f[:, :]))
            link(dve.tensor_copy(r["visit"][:, :], visit_f[:, :]))
            dve.wait_ge(hots_used, NP + MARKS)
            link(dve.tensor_copy(code[:, :], table_ps[:, 0:NPLAN]))
            link(dve.tensor_scalar(empty[:, :], code[:, :], 0.0, None, ALU.is_equal))
            link(dve.tensor_scalar(second[:, :], code[:, :], NTOK + 0.5, -float(NTOK), ALU.is_gt, ALU.mult))
            link(dve.tensor_scalar(code[:, :], code[:, :], 1.0, None, ALU.subtract))
            link(dve.tensor_tensor(second[:, :], code[:, :], second[:, :], ALU.add))
            link(dve.tensor_scalar(second[:, :], second[:, :], 0.0, None, ALU.max))
            link(dve.tensor_copy(r["table"][:, :], second[:, :]))
            link(dve.scalar_tensor_tensor(code[:, :], empty[:, :], spare[:, 0:1], code[:, :], ALU.mult, ALU.add))
            link(dve.tensor_copy(r["dest"][:, :], code[:, :]))

        @block.tensor
        def _(pe):
            pe.sem_inc(hots_used, MARKS)
            pe.wait_ge(iota_step, 17)
            pe.wait_ge(chosen_ok, 1)
            for i in range(NSUB):
                ps = ranks_ps[:, i * NEXP:(i + 1) * NEXP]
                for j in range(i):
                    pe.matmul(ps, all_one[:, :], chosen[:, j, :], start=(j == 0), stop=False)
                pe.matmul(ps, below[:, :], chosen[:, i, :], start=(i == 0), stop=True)
            for j in range(NSUB):
                last = pe.matmul(count_ps[:, 0:NEXP], all_one[:, :], chosen[:, j, :], start=(j == 0), stop=(j == NSUB - 1))
            last.then_inc(counted, 1)
            pe.wait_ge(plan_ok, 1)
            for j in range(2):
                last = pe.matmul(plan_ps[0:1, j * P:(j + 1) * P], plan_col[:, j:j + 1], ident[:, :], start=True, stop=True)
            last.then_inc(plan_rows, 1)
            for g in range(NP):
                pe.wait_ge(hots_ok, g + 1)
                pe.matmul(table_ps[:, 0:NPLAN], at_lane[:, g % MARKS, :], at_block[:, g % MARKS, :],
                          start=(g == 0), stop=(g == NP - 1)).then_inc(hots_used, 1)


GU, DN = 4, 2


def experts(nc, a, h_rows, y_rows, ident, r):
    with ExitStack() as ctx:
        sb = lambda n, s, d=F32: ctx.enter_context(nc.sbuf_tensor(n, s, d))
        sem = lambda n: ctx.enter_context(nc.semaphore(n))
        raw = sb("e_raw", [P, GU + DN, 2048])
        hi, lo = sb("e_hi", [P, GU + DN, 2048], F32R), sb("e_lo", [P, GU + DN, 2048], F32R)
        xg = sb("e_xg", [P, 2, D])
        index = sb("e_index", [P, 2], I32)
        out_index = sb("e_out_index", [P, 2], I32)
        x_hi, x_lo = sb("e_x_hi", [P, D], F32R), sb("e_x_lo", [P, D], F32R)
        gate, hid = sb("e_gate", [P, DE]), sb("e_hid", [P, DE])
        h_hi, h_lo = sb("e_h_hi", [P, DE], F32R), sb("e_h_lo", [P, DE], F32R)
        y = sb("e_y", [P, 2, D])
        ps = [ctx.enter_context(nc.psum_tensor(f"e_ps{j}", [P, 512], F32)) for j in range(7)]
        gate_ps, up_ps, x_ps, h_ps, y_ps = ps[0], ps[1], ps[2:4], ps[4], ps[5:7]
        raw_in = [sem(f"e_raw_in{c}") for c in range(GU + DN)]
        hi_ok = [sem("e_gu_hi_ok"), sem("e_dn_hi_ok")]
        lo_ok = [sem("e_gu_lo_ok"), sem("e_dn_lo_ok")]
        used = [sem("e_gu_used"), sem("e_dn_used")]
        index_ok = sem("e_index_ok")
        dest_ok = sem("e_dest_ok")
        xg_in = [sem(f"e_xg_in{s}") for s in range(2)]
        xt_ok = sem("e_xt_ok")
        x_hi_ok = [sem("e_x_hi0_ok"), sem("e_x_hi1_ok")]
        x_lo_ok = [sem("e_x_lo0_ok"), sem("e_x_lo1_ok")]
        gate_ok = sem("e_gate_ok")
        hid_ok = sem("e_hid_ok")
        ht_ok = sem("e_ht_ok")
        h_hi_ok, h_lo_ok = sem("e_h_hi_ok"), sem("e_h_lo_ok")
        y_ok = [sem("e_y0_ok"), sem("e_y1_ok")]
        y_out = [sem("e_y_out0"), sem("e_y_out1")]
        scrap = sb("e_scrap", [1, 4])
        block = ctx.enter_context(nc.Block())

        def plan(eng, name, b, top=NEXP - 1):
            return eng.value_load(r[name][0:1, bass.ds(b, 1)], min_val=0, max_val=top)

        def rounds(eng, body):
            n = eng.value_load(r["used"][0:1, 0:1], min_val=1, max_val=NBLK - 1)
            with eng.Fori(0, NBLK // 2) as i:
                for s in range(2):
                    with eng.If(i * 2 + s < n):
                        body(i * 2 + s, i, s)

        def chunks(part):
            return [(c, part * GU + c) for c in range((GU, DN)[part])]

        @block.sync
        def _(sp):
            def load(b, part):
                with sp.If(plan(sp, "fresh", b, 1) > 0):
                    e, v = plan(sp, "owner", b), plan(sp, "visit", b)
                    for c, slot in chunks(part):
                        src = a[("w_e_gate", "w_e_up", "w_e_down")[slot // 2]][bass.ds(e, 1), :, :]
                        half = slice((c % 2) * 512, (c % 2) * 512 + 512)
                        src = src[:, half, :] if part == 0 else src[:, :, half]
                        sp.wait_ge(lo_ok[part], v * (GU, DN)[part] + c + 1)
                        sp.dma_start(raw[:, slot, :].rearrange("p (k n) -> p k n", k=4),
                                     src.rearrange("a (k p) n -> p (a k) n", p=P)).then_inc(raw_in[slot], 16)

            def body(b, i, s):
                load(b + 1, 1)
                load(b + 3, 0)

            load(0, 0)
            load(0, 1)
            load(1, 0)
            load(2, 0)
            rounds(sp, body)

        @block.gpsimd
        def _(pool):
            for s in (gate_ok, hid_ok, ht_ok, *x_lo_ok, xt_ok, h_lo_ok, *y_ok):
                pool.sem_inc(s, 1)
            for j, s in enumerate((*xg_in, *y_out)):
                pool.dma_start(scrap[:, j:j + 1], a["ln"][0:1, 0:1]).then_inc(s, 16)

            def gather(b, i, s):
                copied, turned, last = pool.to_reg(b + 1), pool.to_reg(b), pool.to_reg(i * 16 + 16)
                pool.wait_ge(x_lo_ok[0], 1)
                if not isinstance(b, int) or b >= 2:
                    pool.wait_ge(xt_ok, turned)
                    pool.wait_ge(xg_in[s], last)
                pool.tensor_copy(index[:, s:s + 1], r["table"][:, bass.ds(b, 1)]).then_inc(index_ok, 1)
                pool.wait_ge(x_lo_ok[0], 1)
                pool.wait_ge(index_ok, copied)
                pool.indirect_dma_start(out=xg[:, s, :], out_offset=None, in_=h_rows,
                                        in_offset=bass.IndirectOffsetOnAxis(ap=index[:, s:s + 1], axis=0))\
                    .then_inc(xg_in[s], 16)

            def body(b, i, s):
                gather(b + 3, i + 1 + s, 1 - s)
                halves, copied = pool.to_reg(b + 2), pool.to_reg(b + 1)
                before, last = pool.to_reg(i * 16 + 16), pool.to_reg((i + s) * 16 + 16)
                pool.wait_ge(index_ok, 1)
                pool.wait_ge(y_out[s], before)
                pool.tensor_copy(out_index[:, s:s + 1], r["dest"][:, bass.ds(b, 1)]).then_inc(dest_ok, 1)
                pool.wait_ge(index_ok, 1)
                pool.wait_ge(dest_ok, copied)
                pool.wait_ge(y_ok[0], halves)
                pool.wait_ge(y_ok[1], halves)
                pool.wait_ge(y_out[1 - s], last)
                pool.indirect_dma_start(out=y_rows, in_=y[:, s, :], in_offset=None,
                                        out_offset=bass.IndirectOffsetOnAxis(ap=out_index[:, s:s + 1], axis=0))\
                    .then_inc(y_out[s], 16)

            gather(0, 0, 0)
            gather(1, 0, 1)
            gather(2, 1, 0)
            rounds(pool, body)
            n = pool.value_load(r["used"][0:1, 0:1], min_val=1, max_val=NBLK - 1)
            pool.wait_ge(y_out[0], (n + 1) // 2 * 16 + 16)
            pool.wait_ge(y_out[1], n // 2 * 16 + 16)
            pool.wait_ge(xg_in[0], (n + 4) // 2 * 16 + 16)
            pool.wait_ge(xg_in[1], (n + 3) // 2 * 16 + 16)

        @block.scalar
        def _(act):
            def high(b, v, part, c, slot):
                act.wait_ge(raw_in[slot], v * 16 + 16)
                act.wait_ge(used[part], b * (GU, DN)[part] + c + 1)
                act.activation(hi[:, slot, :], raw[:, slot, :], ACT.Copy).then_inc(hi_ok[part], 1)

            def x_high(b):
                for j in range(2):
                    act.wait_ge(xt_ok, b + 2)
                    act.activation(x_hi[:, j * 512:(j + 1) * 512], x_ps[j][:, :], ACT.Copy).then_inc(x_hi_ok[j], 1)

            def gate_up(b):
                with act.If(plan(act, "fresh", b, 1) > 0):
                    v = plan(act, "visit", b)
                    for c, slot in chunks(0)[:3]:
                        high(b, v, 0, c, slot)
                    x_high(b)
                    high(b, v, 0, *chunks(0)[3])
                with act.Else():
                    x_high(b)

            def silu(b):
                act.wait_ge(used[0], b * GU + 2 + GU)
                act.wait_ge(hid_ok, b + 1)
                act.activation(gate[:, :], gate_ps[:, :], ACT.Silu).then_inc(gate_ok, 1)

            def body(b, i, s):
                with act.If(plan(act, "fresh", b, 1) > 0):
                    v = plan(act, "visit", b)
                    for c, slot in chunks(1):
                        high(b, v, 1, c, slot)
                act.wait_ge(ht_ok, b + 2)
                act.activation(h_hi[:, :], h_ps[:, :], ACT.Copy).then_inc(h_hi_ok, 1)
                silu(b + 1)
                gate_up(b + 2)
                act.wait_ge(used[1], b * DN + 1 + DN)
                act.wait_ge(y_out[s], i * 16 + 16)
                act.activation(y[:, s, 0:512], y_ps[0][:, :], ACT.Copy).then_inc(y_ok[0], 1)

            gate_up(0)
            silu(0)
            gate_up(1)
            rounds(act, body)

        @block.vector
        def _(dve):
            dve.sem_inc(lo_ok[0], GU)
            dve.sem_inc(lo_ok[1], DN)

            def low(b, v, part, c, slot):
                dve.wait_ge(hi_ok[part], v * (GU, DN)[part] + c + 1)
                dve.wait_ge(used[part], b * (GU, DN)[part] + c + 1)
                dve.tensor_tensor(lo[:, slot, :], raw[:, slot, :], hi[:, slot, :].bitcast(F32), ALU.subtract)\
                   .then_inc(lo_ok[part], 1)

            def x_low(b):
                for j in range(2):
                    at = slice(j * 512, (j + 1) * 512)
                    dve.wait_ge(x_hi_ok[j], b + 1)
                    dve.tensor_tensor(x_lo[:, at], x_ps[j][:, :], x_hi[:, at].bitcast(F32), ALU.subtract)\
                       .then_inc(x_lo_ok[j], 1)

            def hidden(b):
                dve.wait_ge(used[0], b * GU + 4 + GU)
                dve.wait_ge(gate_ok, b + 2)
                dve.wait_ge(ht_ok, b + 1)
                dve.tensor_tensor(hid[:, :], gate[:, :], up_ps[:, :], ALU.mult).then_inc(hid_ok, 1)

            def gate_up(b):
                with dve.If(plan(dve, "fresh", b, 1) > 0):
                    v = plan(dve, "visit", b)
                    for c, slot in chunks(0)[:3]:
                        low(b, v, 0, c, slot)
                    if not isinstance(b, int) or b > 0:
                        hidden(b - 1)
                    x_low(b)
                    low(b, v, 0, *chunks(0)[3])
                with dve.Else():
                    if not isinstance(b, int) or b > 0:
                        hidden(b - 1)
                    x_low(b)

            def body(b, i, s):
                with dve.If(plan(dve, "fresh", b, 1) > 0):
                    v = plan(dve, "visit", b)
                    for c, slot in chunks(1):
                        low(b, v, 1, c, slot)
                dve.wait_ge(h_hi_ok, b + 1)
                dve.tensor_tensor(h_lo[:, :], h_ps[:, :], h_hi[:, :].bitcast(F32), ALU.subtract).then_inc(h_lo_ok, 1)
                gate_up(b + 2)
                dve.wait_ge(used[1], b * DN + 2 + DN)
                dve.wait_ge(y_out[s], i * 16 + 16)
                dve.tensor_copy(y[:, s, 512:], y_ps[1][:, :]).then_inc(y_ok[1], 1)

            gate_up(0)
            gate_up(1)
            rounds(dve, body)

        @block.tensor
        def _(pe):
            pe.sem_inc(used[0], GU)
            pe.sem_inc(used[1], DN)

            def turn_rows(b, i, s):
                pe.wait_ge(xg_in[s], i * 16 + 32)
                pe.wait_ge(x_lo_ok[1], b + 1)
                for k in range(KD):
                    last = pe.transpose(x_ps[k // 4][:, (k % 4) * P:(k % 4 + 1) * P], xg[:, s, k * P:(k + 1) * P],
                                        ident[:, :])
                last.then_inc(xt_ok, 1)

            def chunk(v, part, c, slot, out, left_hi, left_lo, k0, first, last_k):
                pe.wait_ge(lo_ok[part], v * (GU, DN)[part] + c + 1 + (GU, DN)[part])
                for j in range(4):
                    w, t = slice(j * 512, (j + 1) * 512), slice((k0 + j) * P, (k0 + j + 1) * P)
                    pe.matmul(out[:, :], left_hi[:, t], hi[:, slot, w], start=(first and j == 0), stop=False)
                    pe.matmul(out[:, :], left_hi[:, t], lo[:, slot, w], start=False, stop=False)
                    last = pe.matmul(out[:, :], left_lo[:, t], hi[:, slot, w], start=False, stop=(last_k and j == 3))
                last.then_inc(used[part], 1)

            def gate_up(b):
                v = plan(pe, "visit", b)
                pe.wait_ge(x_lo_ok[0], b + 2)
                pe.wait_ge(x_lo_ok[1], b + 2)
                pe.wait_ge(gate_ok, b + 1)
                pe.wait_ge(hid_ok, b + 1)
                for c, slot in chunks(0):
                    chunk(v, 0, c, slot, (gate_ps, up_ps)[c // 2], x_hi, x_lo, (c % 2) * 4, c % 2 == 0, c % 2 == 1)

            def turn_hidden(b):
                pe.wait_ge(hid_ok, b + 2)
                pe.wait_ge(h_lo_ok, b + 1)
                for k in range(KE):
                    last = pe.transpose(h_ps[:, k * P:(k + 1) * P], hid[:, k * P:(k + 1) * P], ident[:, :])
                last.then_inc(ht_ok, 1)

            def body(b, i, s):
                gate_up(b + 1)
                turn_rows(b + 2, i + 1, s)
                v = plan(pe, "visit", b)
                pe.wait_ge(h_lo_ok, b + 2)
                for c, slot in chunks(1):
                    pe.wait_ge(y_ok[c], b + 1)
                    chunk(v, 1, c, slot, y_ps[c], h_hi, h_lo, 0, True, True)
                turn_hidden(b + 1)

            turn_rows(0, 0, 0)
            gate_up(0)
            turn_rows(1, 0, 1)
            turn_hidden(0)
            rounds(pe, body)


def combine(nc, a, h_rows, y_rows, r, out):
    with ExitStack() as ctx:
        sb = lambda n, s, d=F32: ctx.enter_context(nc.sbuf_tensor(n, s, d))
        sem = lambda n: ctx.enter_context(nc.semaphore(n))
        S = 6
        ln_g, ln_b = sb("ln2_g", [P, D]), sb("ln2_b", [P, D])
        yc = [sb(f"c_y{c}", [P, S, D]) for c in range(2)]
        h, acc, res = sb("c_h", [P, S, D]), sb("c_acc", [P, S, D]), sb("c_res", [P, S, D])
        stats = sb("c_stats", [P, S, 12])
        mom = sb("c_mom", [P, S, 4])
        neg_half = sb("c_neg_half", [P, 1])
        ln_in = sem("c_ln_in")
        const_ok = sem("c_const_ok")
        y_in = [[sem(f"c_y{c}_in{s}") for s in range(S)] for c in range(2)]
        h_in = [sem(f"c_h_in{s}") for s in range(S)]
        acc_step = sem("c_acc_step")
        sum_step = sem("c_sum_step")
        stat_step = sem("c_stat_step")
        eps_ok, rstd_ok = sem("c_eps_ok"), sem("c_rstd_ok")
        shift_ok = sem("c_shift_ok")
        norm_ok = sem("c_norm_ok")
        gain_ok = sem("c_gain_ok")
        done = sem("c_done")
        stored = [sem(f"c_stored{s}") for s in range(S)]
        block = ctx.enter_context(nc.Block())
        n = NSUB // S

        def subtiles(i):
            return [(s, i * S + s) for s in range(S)]

        @block.sync
        def _(sp):
            with sp.Fori(0, n) as i:
                for s, t in subtiles(i):
                    sp.wait_ge(sum_step, t * 2 + 2)
                    for c in range(2):
                        sp.dma_start(yc[c][:, s, :], y_rows[bass.ds(t * P + c * NTOK, P), :]).then_inc(y_in[c][s], 16)
                    sp.dma_start(h[:, s, :], h_rows[bass.ds(t * P, P), :]).then_inc(h_in[s], 16)

        @block.gpsimd
        def _(pool):
            pool.sem_inc(norm_ok, S)
            pool.sem_inc(sum_step, 2 * S)
            for s in stored:
                pool.sem_inc(s, 1)
            pool.memset(neg_half[:, :], -0.5).then_inc(const_ok, 1)
            pool.dma_start(ln_g[:, :], a["ln"][2:3, :].broadcast_to([P, D])).then_inc(ln_in, 16)
            pool.dma_start(ln_b[:, :], a["ln"][3:4, :].broadcast_to([P, D])).then_inc(ln_in, 16)

            def gain(s, t):
                pool.wait_ge(ln_in, 32)
                pool.wait_ge(norm_ok, t + 1 + S)
                pool.tensor_tensor(res[:, s, :], res[:, s, :], ln_g[:, :], ALU.mult).then_inc(gain_ok, 1)

            with pool.Fori(0, n) as i:
                for s, t in subtiles(i):
                    known = pool.to_reg(t * 3 + 3)
                    pool.wait_ge(const_ok, 1)
                    pool.wait_ge(stat_step, known)
                    pool.tensor_scalar(mom[:, s, 1:2], mom[:, s, 1:2], EPS, None, ALU.add).then_inc(eps_ok, 1)
                    pool.wait_ge(eps_ok, t + 1)
                    pool.tensor_tensor(mom[:, s, 2:3], mom[:, s, 1:2], neg_half[:, :], ALU.pow).then_inc(rstd_ok, 1)
                    if s:
                        gain(s - 1, t - 1)
                gain(S - 1, i * S + S - 1)

        @block.scalar
        def _(act):
            def norm(s, t, i):
                act.wait_ge(shift_ok, t + 1)
                act.wait_ge(stored[s], i * 16 + 1)
                act.activation(res[:, s, :], acc[:, s, :], ACT.Identity, scale=mom[:, s, 2:3],
                               bias=mom[:, s, 3:4]).then_inc(norm_ok, 1)

            def store(s, t):
                act.wait_ge(done, t + 1)
                act.dma_start(out[bass.ds(t * P, P), :], res[:, s, :]).then_inc(stored[s], 16)

            with act.Fori(0, n) as i:
                for s, t in subtiles(i):
                    act.wait_ge(y_in[0][s], i * 16 + 16)
                    act.wait_ge(norm_ok, t + 1)
                    act.activation(acc[:, s, :], yc[0][:, s, :], ACT.Copy,
                                   scale=r["gates"][:, bass.ds(t, 1)]).then_inc(acc_step, 1)
                    if s > 0:
                        norm(s - 1, t - 1, i)
                    if s > 2:
                        store(s - 3, t - 3)
                norm(S - 1, i * S + S - 1, i)
                for s in range(S - 3, S):
                    store(s, i * S + s)
            for s in range(S):
                act.wait_ge(stored[s], n * 16 + 1)

        @block.vector
        def _(dve):
            dve.wait_ge(ln_in, 32)

            def offset(s, t):
                dve.wait_ge(gain_ok, t + 1)
                dve.tensor_tensor(res[:, s, :], res[:, s, :], ln_b[:, :], ALU.add).then_inc(done, 1)

            with dve.Fori(0, n) as i:
                for s, t in subtiles(i):
                    dve.wait_ge(acc_step, t + 1)
                    dve.wait_ge(y_in[1][s], i * 16 + 16)
                    dve.scalar_tensor_tensor(acc[:, s, :], yc[1][:, s, :], r["gates"][:, bass.ds(t + NSUB, 1)],
                                             acc[:, s, :], ALU.mult, ALU.add).then_inc(sum_step, 1)
                    dve.wait_ge(sum_step, t * 2 + 1 + 2 * S)
                    dve.wait_ge(h_in[s], i * 16 + 16)
                    dve.scalar_tensor_tensor(acc[:, s, :], h[:, s, :], ALPHA, acc[:, s, :], ALU.mult, ALU.add)\
                       .then_inc(sum_step, 1)
                    dve.wait_ge(sum_step, t * 2 + 2 + 2 * S)
                    for half in range(2):
                        dve.bn_stats(stats[:, s, half * 6:half * 6 + 6], acc[:, s, half * 512:(half + 1) * 512])\
                           .then_inc(stat_step, 1)
                    taken = dve.to_reg(t * 3 + 2)
                    dve.wait_ge(ln_in, 32)
                    dve.wait_ge(stat_step, taken)
                    dve.bn_aggr(mom[:, s, 0:2], stats[:, s, :]).then_inc(stat_step, 1)
                    if s > 1:
                        offset(s - 2, t - 2)
                    dve.wait_ge(rstd_ok, t + 1)
                    dve.scalar_tensor_tensor(mom[:, s, 3:4], mom[:, s, 0:1], -1.0, mom[:, s, 2:3], ALU.mult, ALU.mult)\
                       .then_inc(shift_ok, 1)
                for s in (S - 2, S - 1):
                    offset(s, i * S + s)


def encoder(nc, a, out):
    qkv = nc.dram_tensor("qkv", [3 * HP, P, NCOL], F32, kind="Internal").ap()
    h_rows = nc.dram_tensor("h_rows", [NTOK, D], F32, kind="Internal").ap()
    y_rows = nc.dram_tensor("y_rows", [2 * NTOK + P, D], F32, kind="Internal").ap()
    with ExitStack() as ctx:
        sb = lambda n, s, d=F32: ctx.enter_context(nc.sbuf_tensor(n, s, d))
        ident = sb("ident", [P, P])
        logits = sb("logits", [P, NSUB * NLOG])
        r = {
            "gates": sb("gates", [P, 2 * NSUB]),
            "table": sb("table", [P, NPLAN], I32),
            "dest": sb("dest", [P, NPLAN], I32),
            "owner": sb("owner", [1, NPLAN], I32),
            "fresh": sb("fresh", [1, NPLAN], I32),
            "visit": sb("visit", [1, NPLAN], I32),
            "used": sb("used", [1, 1], I32),
        }
        edges = sb("edges", [P, FB * NEDGE])
        project_qkv(nc, a, a["x_cols"], a["w_qkv"], a["w_cxb"], ident, qkv, edges)
        mixer(nc, a, qkv, edges, ident, logits, h_rows)
        route(nc, logits, ident, r)
        experts(nc, a, h_rows, y_rows, ident, r)
        combine(nc, a, h_rows, y_rows, r, out)


def layouts(inp):
    a = {k: np.asarray(v) for k, v in inp.items()}
    x = np.concatenate([a["x_prompt"].reshape(PROMPT, D), a["x_sample"].reshape(SAMPLE, D)], 0)
    cols = np.concatenate([x, a["meta_tokens"]], 0).T.reshape(KD, P, NCOL)
    w_in = a["w_in"][0].reshape(KD, P, 52, P).transpose(2, 1, 0, 3).reshape(52, P, D)
    out = {}
    out["x_rows"] = np.ascontiguousarray(x)
    out["x_cols"] = np.ascontiguousarray(cols.transpose(1, 0, 2))
    none = np.zeros((D,), np.float32)
    meta = a["meta_tokens"][NMETA - 1]
    halo = np.stack([np.stack([meta, x[TILE]]), np.stack([x[TILE - 1], none]), np.stack([meta, none])])
    out["x_halo"] = np.ascontiguousarray(halo.reshape(NT, 2, KD, P).transpose(0, 3, 2, 1).reshape(NT, P, KD * 2))
    out["w_qkv"] = np.ascontiguousarray(w_in[0:12])
    b, c, xc, ga, gc = (w_in[12 + 8 * i:20 + 8 * i] for i in range(5))
    out["w_cxb"] = np.ascontiguousarray(np.stack([c, xc, b], 1).reshape(3 * FB, P, D))
    w_conv = a["w_conv_proj"][0].reshape(KD, P, FB, P).transpose(2, 1, 0, 3).reshape(FB, P, D)
    out["w_gates"] = np.ascontiguousarray(np.stack([ga, gc, w_conv], 1).reshape(3 * FB, P, D))
    out["w_att"] = np.ascontiguousarray(
        a["w_att_proj"][0].reshape(HP, P, FB, P).transpose(2, 1, 0, 3).reshape(FB, P, HP * P))
    out["w_out"] = np.ascontiguousarray(
        a["w_out"][0].reshape(KD // 2, 2, P, 2, 512).transpose(3, 0, 2, 1, 4).reshape(KD, P, D))
    cw = np.concatenate([a["conv_w"][0], a["conv_b"]], 0)
    out["conv_wb"] = np.ascontiguousarray(cw.reshape(4, FB, P).transpose(2, 1, 0).reshape(P, 4 * FB))
    plane = np.zeros((HEADS, 16, BP_ROWS * 64 + 64), np.float32)
    rpb = a["rpb"][0]
    for i in range(16):
        for y in range(2 * WIN_H - 1):
            at = (y + 4) * 64 + 16 - (15 - i)
            plane[:, i, at:at + 2 * WIN_W - 1] = rpb[:, y]
    out["bias_planes"] = plane
    out["masks"] = window_masks()
    out["ln"] = np.ascontiguousarray(np.concatenate([a["ln1_g"], a["ln1_b"], a["ln2_g"], a["ln2_b"]], 0))
    wr = np.concatenate([a["w_router_group"][0], a["w_router_expert"][0]], 1)
    out["w_router"] = np.ascontiguousarray(wr.reshape(KD, P, NLOG).transpose(1, 0, 2).reshape(P, KD * NLOG))
    out["w_e_gate"] = a["w_e_gate"][0]
    out["w_e_up"] = a["w_e_up"][0]
    out["w_e_down"] = a["w_e_down"][0]
    return out


def kernel(**inputs):
    import concourse.bacc as bacc
    from concourse.bass_utils import run_bass_kernel_spmd

    arrays = layouts(inputs)
    nc = bacc.Bacc("TRN2", target_bir_lowering=False, num_devices=1)
    a = {n: nc.dram_tensor(f"in_{n}", v.shape, mybir.dt.from_np(v.dtype), kind="ExternalInput").ap()
         for n, v in arrays.items()}
    out = nc.dram_tensor("out", [NTOK, D], F32, kind="ExternalOutput").ap()
    encoder(nc, a, out)
    got = run_bass_kernel_spmd(nc, [{f"in_{n}": v for n, v in arrays.items()}], core_ids=[0]).results[0]["out"]
    return got[:PROMPT].reshape(1, PROMPT, D), got[PROMPT:].reshape(1, SAMPLE, D)
```

```python
from contextlib import ExitStack

import numpy as np

import concourse.bass as bass
from concourse import mybir

F32 = mybir.dt.float32
F32R = mybir.dt.float32r
BF16 = mybir.dt.bfloat16
I32 = mybir.dt.int32
ALU = mybir.AluOpType
ACT = mybir.ActivationFunctionType
AX = mybir.AxisListType

P = 128
D = 1024
KD = D // P
NMETA = 16
PROMPT, SAMPLE = 1024, 512
NTOK = PROMPT + SAMPLE
NCOL = NTOK + NMETA
TILE = 512
NT = NTOK // TILE
GRID, WIN_H, WIN_W = 64, 8, 16
ROWS_T = TILE // GRID
KROWS, KCOLS = 12, 32
NKEY = KROWS * KCOLS
NCB = 4
HEADS, DH = 8, 64
HP = HEADS // 2
FB = D // P
ALPHA = 2.0 ** 0.25
EPS = 1e-5
NEG = -1e30
BP_ROWS = 24
NG, NEXP, EPG = 4, 32, 8
DE = 512
KE = DE // P
NSUB = NTOK // P
SUB_T = TILE // P
NLOG = NG + NEXP
NBLK = (2 * NTOK + NEXP * (P - 1)) // P + 1
NBLK += NBLK % 2
NPLAN = NBLK + 3


NEDGE, RIGHT = 12, 9
N_CXB, N_MERGE, N_OUT = 3 * FB, 4 * FB, FB
N_TILE = N_CXB + N_MERGE + N_OUT
W_IN_TILE = (N_TILE - N_OUT // 2) // 2


def key_start(cb):
    return min(max(cb * 16 - 8, 0), GRID - KCOLS)


def window_masks():
    m = np.full((NT, P, NCB, KROWS, KCOLS), NEG, np.float32)
    for t in range(NT):
        base = 4 * t + 4 * (t // 2)
        rows, first = (16, 0) if t < 2 else (8, 16)
        for r in range(ROWS_T):
            row = 8 * t + r - first
            rs = min(max(row - WIN_H // 2, 0), rows - WIN_H) + first
            for i in range(16):
                for cb in range(NCB):
                    ws = min(max(cb * 16 + i - WIN_W // 2, 0), GRID - WIN_W)
                    a, c = rs - base, ws - key_start(cb)
                    m[t, r * 16 + i, cb, a:a + WIN_H, c:c + WIN_W] = 0.0
    bits = m.reshape(NT, P, NCB * NKEY).view(np.uint32) >> 16
    return bits.astype(np.uint16)


SIDE = 4


def project_qkv(nc, a, x_hi, x_lo, ident, qkv, edges, stored):
    x_cols, w_qkv, w_cxb = a["x_cols"], a["w_qkv"], a["w_cxb"]
    nblk = w_qkv.shape[0]
    nq = HP
    beside = slice(TILE, NCOL, NCOL - 1 - TILE)
    with ExitStack() as ctx:
        sb = lambda n, s, d=F32: ctx.enter_context(nc.sbuf_tensor(n, s, d))
        sem = lambda n: ctx.enter_context(nc.semaphore(n))
        rest_hi = sb("rest_hi", [P, KD, NCOL - TILE], F32R)
        rest_lo = sb("rest_lo", [P, KD, NCOL - TILE], F32R)
        x_raw = sb("qkv_x_raw", [P, 2, NCOL])
        w_raw = sb("qkv_w_raw", [P, 2, D])
        w_hi = sb("qkv_w_hi", [P, 2, D], F32R)
        w_lo = sb("qkv_w_lo", [P, 2, D], F32R)
        res = sb("qkv_res", [P, 2, NCOL])
        bank = [[ctx.enter_context(nc.psum_tensor(f"qkv_ps{s}{t}", [P, 512], F32)) for t in range(4)]
                for s in range(2)]
        x_side = sb("qkv_x_side", [P, KD, 2])
        side_w = sb("qkv_side_w", [P, 3, SIDE, D])
        c_row, u_row = sb("qkv_c_row", [2, D]), sb("qkv_u_row", [2, D])
        side_in = [sem(f"qkv_side_in{s}") for s in range(3)]
        ident_ok = sem("qkv_ident_ok")
        side_used = sem("qkv_side_used")
        x_side_ok = sem("qkv_x_side_ok")
        c_row_ok = sem("qkv_c_row_ok")
        u_row_ok = sem("qkv_u_row_ok")
        u_col_ok = sem("qkv_u_col_ok")
        edge_ok = sem("qkv_edge_ok")
        x_in = [sem(f"qkv_x_in{s}") for s in range(2)]
        x_hi_ok = sem("qkv_x_hi_ok")
        x_lo_ok = sem("qkv_x_lo_ok")
        w_in = [sem(f"qkv_w_in{s}") for s in range(2)]
        w_hi_ok = sem("qkv_w_hi_ok")
        w_lo_ok = sem("qkv_w_lo_ok")
        w_used = sem("qkv_w_used")
        ev_act = sem("qkv_ev_act")
        ev_dve = sem("qkv_ev_dve")
        ends = [0, TILE, TILE + 352, TILE + 352 + 344, NCOL]
        cols = [slice(ends[j], ends[j + 1]) for j in range(4)]

        def part(tile, rest, k, t):
            return tile[:, k, :] if t == 0 else rest[:, k, ends[t] - TILE:ends[t + 1] - TILE]

        scrap = sb("qkv_scrap", [1, 4])
        block = ctx.enter_context(nc.Block())

        def load_w(eng, n, i, s):
            eng.wait_ge(w_lo_ok, n + 1)
            eng.dma_start(w_raw[:, s, :], w_qkv[bass.ds(n, 1), :, :].rearrange("a p n -> p (a n)"))\
               .then_inc(w_in[s], 16)

        def load_side(eng, n):
            i, j = divmod(n, 2)
            blocks = w_cxb.rearrange("(f c) p n -> c p f n", c=3)[j][:, i * SIDE:(i + 1) * SIDE, :]
            eng.dma_start(side_w[:, n % 3, :, :], blocks)\
               .then_inc(side_in[n % 3], 16)

        @block.sync
        def _(sp):
            load_w(sp, 0, 0, 0)
            for k in range(KD):
                sp.wait_ge(x_lo_ok, k + 1)
                sp.dma_start(x_raw[:, k % 2, :], x_cols[:, k, :]).then_inc(x_in[k % 2], 16)
            load_w(sp, 1, 0, 1)
            for n in range(3):
                load_side(sp, n)
            with sp.Fori(1, nblk // 2) as i:
                for s in range(2):
                    load_w(sp, i * 2 + s, i, s)
            sp.wait_ge(side_used, 1)
            load_side(sp, 3)

        @block.gpsimd
        def _(pool):
            for j, s in enumerate(stored):
                pool.dma_start(scrap[:, j:j + 1], a["ln"][0:1, 0:1]).then_inc(s, 16)
            pool.memset(ident[:, :], 0.0).then_inc(ident_ok, 1)
            pool.wait_ge(ident_ok, 1)
            pool.affine_select(out=ident[:, :], in_=ident[:, :], compare_op=ALU.not_equal, fill=1.0, base=0,
                               pattern=[[-1, P]], channel_multiplier=1).then_inc(ident_ok, 1)
            with pool.Fori(0, nblk // 2) as i:
                for s in range(2):
                    pool.wait_ge(ev_act, i * 2 + s + 3)
                    pool.wait_ge(ev_dve, i * 2 + s + 3)
                    pool.dma_start(qkv[bass.ds(i * 2 + s, 1), :, :].rearrange("a p n -> p (a n)"),
                                   res[:, s, :]).then_inc(stored[s], 16)
            for s in range(2):
                pool.wait_ge(stored[s], 16 * (nblk // 2) + 16)

        @block.scalar
        def _(act):
            act.sem_inc(ev_act, 2)

            def high(n, i, s):
                act.wait_ge(w_in[s], i * 16 + 16)
                act.wait_ge(w_used, n + 1)
                act.activation(w_hi[:, s, :], w_raw[:, s, :], ACT.Copy).then_inc(w_hi_ok, 1)

            def copy_out(n, i, s, scale):
                act.wait_ge(w_used, n + 3)
                act.wait_ge(stored[s], i * 16 + 16)
                for t in range(2):
                    last = act.activation(res[:, s, cols[t]], bank[s][t][:, 0:cols[t].stop - cols[t].start],
                                          ACT.Copy, scale=scale)
                last.then_inc(ev_act, 1)

            high(0, 0, 0)
            for k in range(KD):
                act.wait_ge(x_in[k % 2], 16 * (k // 2 + 1))
                act.activation(x_hi[:, k, :], x_raw[:, k % 2, 0:TILE], ACT.Copy).then_inc(x_hi_ok, 1)
                act.activation(rest_hi[:, k, :], x_raw[:, k % 2, TILE:], ACT.Copy).then_inc(x_hi_ok, 1)
            with act.Fori(0, nq // 2) as i:
                high(i * 2 + 1, i, 1)
                copy_out(i * 2, i, 0, DH ** -0.5)
                high(i * 2 + 2, i + 1, 0)
                copy_out(i * 2 + 1, i, 1, DH ** -0.5)
            with act.Fori(nq // 2, nblk // 2 - 1) as i:
                high(i * 2 + 1, i, 1)
                copy_out(i * 2, i, 0, 1.0)
                high(i * 2 + 2, i + 1, 0)
                copy_out(i * 2 + 1, i, 1, 1.0)
            i = nblk // 2 - 1
            high(2 * i + 1, i, 1)
            copy_out(2 * i, i, 0, 1.0)
            copy_out(2 * i + 1, i, 1, 1.0)

        @block.vector
        def _(dve):
            dve.sem_inc(w_lo_ok, 2)
            dve.sem_inc(x_lo_ok, 2)
            dve.sem_inc(ev_dve, 2)

            def low(n, i, s):
                dve.wait_ge(w_hi_ok, n + 1)
                dve.wait_ge(w_used, n + 1)
                dve.tensor_tensor(w_lo[:, s, :], w_raw[:, s, :], w_hi[:, s, :].bitcast(F32), ALU.subtract)\
                   .then_inc(w_lo_ok, 1)

            def copy_out(n, i, s, scale):
                dve.wait_ge(w_used, n + 3)
                dve.wait_ge(stored[s], i * 16 + 16)
                for t in range(2, 4):
                    ps = bank[s][t][:, 0:cols[t].stop - cols[t].start]
                    last = dve.tensor_scalar(res[:, s, cols[t]], ps, scale, None, ALU.mult)
                last.then_inc(ev_dve, 1)

            low(0, 0, 0)
            for k in range(KD):
                dve.wait_ge(x_hi_ok, 2 * k + 1)
                dve.tensor_copy(x_side[:, k, :], x_raw[:, k % 2, beside]).then_inc(x_side_ok, 1)
                dve.tensor_tensor(x_lo[:, k, :], x_raw[:, k % 2, 0:TILE], x_hi[:, k, :].bitcast(F32), ALU.subtract)
                dve.wait_ge(x_hi_ok, 2 * k + 2)
                dve.tensor_tensor(rest_lo[:, k, :], x_raw[:, k % 2, TILE:], rest_hi[:, k, :].bitcast(F32),
                                  ALU.subtract).then_inc(x_lo_ok, 1)
            with dve.Fori(0, nq // 2) as i:
                low(i * 2 + 1, i, 1)
                copy_out(i * 2, i, 0, DH ** -0.5)
                low(i * 2 + 2, i + 1, 0)
                copy_out(i * 2 + 1, i, 1, DH ** -0.5)
            with dve.Fori(nq // 2, nblk // 2 - 1) as i:
                low(i * 2 + 1, i, 1)
                copy_out(i * 2, i, 0, 1.0)
                low(i * 2 + 2, i + 1, 0)
                copy_out(i * 2 + 1, i, 1, 1.0)
            i = nblk // 2 - 1
            low(2 * i + 1, i, 1)
            copy_out(2 * i, i, 0, 1.0)
            copy_out(2 * i + 1, i, 1, 1.0)
            half = FB // SIDE
            for i in range(half):
                at = slice(i * SIDE * P, (i + 1) * SIDE * P)
                dve.wait_ge(side_used, 2 * i + 1)
                dve.tensor_copy(c_row[:, at], bank[0][i][0:2, :]).then_inc(c_row_ok, 1)
                dve.wait_ge(side_used, 2 * i + 2)
                dve.wait_ge(c_row_ok, i + 1)
                dve.tensor_tensor(u_row[:, at], c_row[:, at], bank[1][i][0:2, :], ALU.mult).then_inc(u_row_ok, 1)
            edge = edges[:, :].rearrange("p (f s) -> p f s", s=NEDGE)
            cols_ps = bank[0][2][:, 0:2 * FB].rearrange("p (f c) -> p f c", c=2)
            dve.memset(edges[:, :], 0.0).then_inc(edge_ok, 1)
            dve.wait_ge(edge_ok, 1)
            dve.wait_ge(u_col_ok, 1)
            for slot, col in ((RIGHT, 0), (0, 1), (4, 1)):
                dve.tensor_copy(edge[:, :, slot], cols_ps[:, :, col]).then_inc(edge_ok, 1)

        @block.tensor
        def _(pe):
            pe.sem_inc(w_used, 2)

            def project(n, s, first=False):
                pe.wait_ge(w_lo_ok, n + 3)
                pe.wait_ge(ev_act, n + 1)
                pe.wait_ge(ev_dve, n + 1)
                for k in range(KD):
                    if first:
                        pe.wait_ge(x_lo_ok, k + 3)
                    w = slice(k * P, (k + 1) * P)
                    for t in range(4):
                        ps = bank[s][t][:, 0:cols[t].stop - cols[t].start]
                        high, low = part(x_hi, rest_hi, k, t), part(x_lo, rest_lo, k, t)
                        pe.matmul(ps, w_hi[:, s, w], high, start=(k == 0), stop=False)
                        pe.matmul(ps, w_hi[:, s, w], low, start=False, stop=False)
                        last = pe.matmul(ps, w_lo[:, s, w], high, start=False, stop=(k == KD - 1))
                last.then_inc(w_used, 1)

            project(0, 0, first=True)
            project(1, 1)
            with pe.Fori(1, nblk // 2) as i:
                for s in range(2):
                    project(i * 2 + s, s)
            pe.wait_ge(ev_dve, nblk + 2)
            pe.wait_ge(ev_act, nblk + 2)
            pe.wait_ge(x_side_ok, KD)
            for n in range(2 * FB // SIDE):
                i, j = divmod(n, 2)
                pe.wait_ge(side_in[n % 3], n // 3 * 16 + 16)
                for k in range(KD):
                    last = pe.matmul(bank[j][i][0:2, :], x_side[:, k, :], side_w[:, n % 3, :, k * P:(k + 1) * P],
                                     start=(k == 0), stop=(k == KD - 1))
                last.then_inc(side_used, 1)
            pe.wait_ge(ident_ok, 2)
            pe.wait_ge(u_row_ok, FB // SIDE)
            for f in range(FB):
                last = pe.matmul(bank[0][2][:, 2 * f:2 * f + 2], u_row[:, f * P:(f + 1) * P], ident[0:2, 0:2],
                                 start=True, stop=True)
            last.then_inc(u_col_ok, 1)


def attention_schedule():
    chunk = 0
    for cb in range(NCB):
        for step, gap in (("scores", 5), ("turn0", 3), ("turn1", 3)):
            yield step, cb
            for chunk in range(chunk, chunk + gap):
                yield "chunk", divmod(chunk, KD)
            chunk += 1
    for step in ("drain_values", "drain_turn"):
        yield step, NCB - 1
        for chunk in range(chunk, chunk + 2):
            yield "chunk", divmod(chunk, KD)
        chunk += 1


NPAIR = N_CXB // HP


def o_block(t, p, cb):
    at = t[:, bass.ds(p * TILE, TILE)].rearrange("p (r c) -> p r c", c=GRID)
    return at[:, :, cb * 16:cb * 16 + 16]


OUT_BANK = [(3, 4), (5, 6), (0, 1), (2, 7)]


def mixer(nc, a, x_hi, x_lo, qkv, edges, ident, logits, h_rows):
    with ExitStack() as ctx:
        sb = lambda n, s, d=F32: ctx.enter_context(nc.sbuf_tensor(n, s, d))
        sem = lambda n: ctx.enter_context(nc.semaphore(n))
        x_raw = sb("x_raw", [P, 2, 2 * TILE])
        o_hi, o_lo = sb("o_hi", [P, HP * TILE], F32R), sb("o_lo", [P, HP * TILE], F32R)
        y_hi, y_lo = sb("y_hi", [P, FB * TILE], F32R), sb("y_lo", [P, FB * TILE], F32R)
        w_raw = sb("w_raw", [P, 2, D])
        w_hi, w_lo = sb("w_hi", [P, 2, D], F32R), sb("w_lo", [P, 2, D], F32R)
        conv_wb = sb("conv_wb_sb", [P, 4 * FB])
        w_router = sb("w_router_sb", [P, KD, NLOG])
        ln_g, ln_b = sb("ln1_g", [P, D]), sb("ln1_b", [P, D])
        ident_b = sb("ident_b", [P, P], BF16)
        zeros = sb("zeros", [P, NMETA])
        neg_half = sb("neg_half", [P, SUB_T])
        q, q_cut = sb("q", [P, TILE]), sb("q_cut", [P, TILE])
        v_cut = sb("v_cut", [P, NCB * NKEY])
        key = sb("key", [P, KROWS * GRID + NMETA])
        val = sb("val", [P, KROWS * GRID + NMETA])
        bias = sb("bias", [P, 2, KROWS * GRID])
        mask = sb("mask", [P, NCB * NKEY], BF16)
        rows = sb("rows", [P, SUB_T, D])
        stats = sb("stats", [P, 12])
        mom = sb("mom", [P, SUB_T * 3]).rearrange("p (s m) -> p s m", m=3)
        first = ExitStack()
        sa = lambda n, s, d=F32: first.enter_context(nc.sbuf_tensor(n, s, d))
        prob = sa("prob", [P, 2, 512])
        prob_t = sa("prob_t", [P, 2, 512])
        sbias = sa("sbias", [P, 2, NKEY + NMETA])
        vkeys = sa("vkeys", [P, 2, NKEY])
        vmeta = sa("vmeta", [NMETA, P])
        o_rows = sa("o_rows", [P, P])
        small = sa("small", [P, 10])
        smeta, smax, nmax, ssum, rsum = (small[:, 2 * j:2 * j + 2] for j in range(5))
        c_sb = sa("c_sb", [P, TILE])
        u = sa("u", [P, TILE + 2])
        y = sa("y", [P, TILE])
        first.close()
        m_hi, m_lo = sb("m_hi", [P, FB * TILE], F32R), sb("m_lo", [P, FB * TILE], F32R)
        m_att = sb("m_att", [P, TILE])
        third = ExitStack()
        sa = lambda n, s, d=F32: third.enter_context(nc.sbuf_tensor(n, s, d))
        sig_a, sig_c = sa("sig_a", [P, TILE]), sa("sig_c", [P, TILE])
        third.close()
        h_t = sb("h_t", [P, D])
        out_hi = [w_hi[:, 0, :], w_hi[:, 1, :]] + [o_hi[:, j * D:(j + 1) * D] for j in range(2)] \
            + [y_hi[:, j * D:(j + 1) * D] for j in range(4)]
        out_lo = [w_lo[:, 0, :], w_lo[:, 1, :]] + [o_lo[:, j * D:(j + 1) * D] for j in range(2)] \
            + [y_lo[:, j * D:(j + 1) * D] for j in range(4)]
        bank = [ctx.enter_context(nc.psum_tensor(f"bank{j}", [P, 512], F32)) for j in range(8)]
        score, turned, outp = bank[3:5], bank[5], bank[6]

        const_in = sem("const_in")
        const_ok = sem("const_ok")
        x_in = [sem(f"x_in{j}") for j in range(2)]
        x_hi_ok, x_lo_ok = sem("x_hi_ok"), sem("x_lo_ok")
        w_in = [sem(f"w_in{j}") for j in range(2)]
        out_in = [sem(f"out_in{j}") for j in range(2)]
        w_hi_ok, w_lo_ok = sem("w_hi_ok"), sem("w_lo_ok")
        w_used = sem("w_used")
        qv_in = sem("qv_in")
        key_in = sem("key_in")
        bias_in = sem("bias_in")
        q_cut_ok = sem("q_cut_ok")
        v_cut_ok = sem("v_cut_ok")
        mask_in = sem("mask_in")
        rows_in = sem("rows_in")
        scores_ok = sem("scores_ok")
        max_step = sem("max_step")
        max_ok = sem("max_ok")
        exp_ok = sem("exp_ok")
        sum_ok = sem("sum_ok")
        turn_ok = sem("turn_ok")
        prob_t_ok = [sem("prob_t0_ok"), sem("prob_t1_ok")]
        vturn_ok, vkeys_ok = sem("vturn_ok"), sem("vkeys_ok")
        pv_ok = sem("pv_ok")
        o_ok = sem("o_ok")
        oturn_ok = sem("oturn_ok")
        o_hi_ok, o_lo_ok = sem("o_hi_ok"), sem("o_lo_ok")
        c_ok = sem("c_ok")
        conv_step = sem("conv_step")
        y_hi_ok, y_lo_ok = sem("y_hi_ok"), sem("y_lo_ok")
        sig_a_ok, sig_c_ok = sem("sig_a_ok"), sem("sig_c_ok")
        m_step = sem("m_step")
        m_hi_ok, m_lo_ok = sem("m_hi_ok"), sem("m_lo_ok")
        res_step = sem("res_step")
        mom_ok = sem("mom_ok")
        var_ok = sem("var_ok")
        rstd_ok = sem("rstd_ok")
        norm_ok = sem("norm_ok")
        gain_ok = sem("gain_ok")
        h_ok = sem("h_ok")
        hturn_ok = sem("hturn_ok")
        h_t_ok = [sem("h_t0_ok"), sem("h_t1_ok")]
        log_ok = sem("log_ok")
        log_out = sem("log_out")
        h_stored = sem("h_stored")
        made = sem("made")
        res_bn = sem("res_bn")

        def window(cb, j0=0, j1=KROWS):
            return slice(j0, j1), slice(key_start(cb), key_start(cb) + KCOLS)

        def grid(t):
            return t.rearrange("p (r c) -> p r c", c=GRID)

        def raw_out(j):
            if j % 4 < 2:
                return w_raw[:, j % 2, :], w_in[j % 2]
            return x_raw[:, j % 2, :], out_in[j % 2]

        def load_window(eng, dst, first, t, p, landed):
            base = t * 4 + (t // 2) * 4
            eng.dma_start(dst[:, 0:KROWS * GRID], qkv[bass.ds(p + first, 1), :, bass.ds(base * GRID, KROWS * GRID)]
                          .rearrange("a p n -> p (a n)")).then_inc(landed, 16)
            eng.dma_start(dst[:, KROWS * GRID:], qkv[bass.ds(p + first, 1), :, NTOK:NCOL]
                          .rearrange("a p n -> p (a n)")).then_inc(landed, 16)

        def next_tile(t):
            return nc.s_assert_within(t + 1, 1, NT - 1, skip_runtime_bounds_check_because="only where t < NT - 1")

        block = ctx.enter_context(nc.Block())

        @block.sync
        def _(sp):
            def load(n, half, src, width=D):
                sp.wait_ge(w_lo_ok, n + 1)
                sp.dma_start(w_raw[:, half % 2, 0:width], src.rearrange("a p n -> p (a n)"))\
                  .then_inc(w_in[half % 2], 16)

            def load_x(t):
                out_split = sp.to_reg((t + 1) * N_TILE + 2)
                for j in range(4):
                    chunk_split = sp.to_reg(t * 4 + j + 1)
                    sp.wait_ge(w_lo_ok, out_split)
                    sp.wait_ge(x_lo_ok, chunk_split)
                    sp.dma_start(x_raw[:, j % 2, :].rearrange("p (k n) -> p k n", k=2),
                                 a["x_cols"][:, 2 * j:2 * j + 2, bass.ds(next_tile(t) * TILE, TILE)]).then_inc(x_in[j % 2], 16)

            def load_keys(t, p):
                sp.wait_ge(scores_ok, (t * HP + p) * 2 * NCB + 1)
                load_window(sp, key, HP, t, p, key_in)
                sp.wait_ge(max_ok, (t * HP + p) * 2 * NCB + 2)
                for r in range(ROWS_T):
                    at = (2 - t) // 2 * (4 * 64) + (ROWS_T - 1 - r) * 64
                    sp.dma_start(bias[r * 16:r * 16 + 16, :, :],
                                 a["bias_planes"][bass.ds(p * 2, 2), :, bass.ds(at, KROWS * GRID)]
                                 .rearrange("h i n -> i h n")).then_inc(bias_in, 16)

            with sp.Fori(0, NT) as t:
                sp.wait_ge(scores_ok, t * HP * 2 * NCB + 1)
                sp.dma_start(mask[:, :], a["masks"].bitcast(BF16)[bass.ds(t, 1), :, :].rearrange("a p n -> p (a n)"))\
                  .then_inc(mask_in, 16)
                with sp.Fori(0, HP) as p:
                    for j in range(NPAIR):
                        load(t * N_TILE + p * NPAIR + j, j, a["w_cxb"][bass.ds(p * NPAIR + j, 1), :, :])
                        if j == 0:
                            load_keys(t, p)
                with sp.Fori(0, FB) as f:
                    n = t * N_TILE + N_CXB + f * 4
                    load(n, 0, a["w_gates"][bass.ds(f * 3, 1), :, :])
                    load(n + 1, 1, a["w_att"][bass.ds(f, 1), :, :], HP * P)
                    load(n + 2, 2, a["w_gates"][bass.ds(f * 3 + 1, 1), :, :])
                    load(n + 3, 3, a["w_gates"][bass.ds(f * 3 + 2, 1), :, :])
                n1 = t * N_TILE + N_CXB + N_MERGE
                for j in range(N_OUT):
                    if j < 2:
                        load(n1 + j, j, a["w_out"][j:j + 1, :, :])
                        continue
                    dst, landed = raw_out(j)
                    if j >= 4:
                        sp.wait_ge(w_lo_ok, n1 + j - 1)
                    else:
                        sp.wait_ge(x_lo_ok, t * 4 + 2)
                    sp.dma_start(dst, a["w_out"][j:j + 1, :, :].rearrange("a p n -> p (a n)")).then_inc(landed, 16)
                with sp.If(t < NT - 1):
                    load_x(t)

        @block.gpsimd
        def _(pool):
            for s in (c_ok, conv_step, h_stored, *h_t_ok, hturn_ok, log_out, m_hi_ok, m_step, mom_ok, o_lo_ok,
                      oturn_ok, *prob_t_ok, pv_ok, q_cut_ok, scores_ok, sig_a_ok, sig_c_ok, v_cut_ok, vturn_ok,
                      y_lo_ok):
                pool.sem_inc(s, 1)
            pool.tensor_copy(ident_b[:, :], ident[:, :]).then_inc(const_ok, 1)
            pool.memset(zeros[:, :], 0.0).then_inc(const_ok, 1)
            pool.memset(neg_half[:, :], -0.5).then_inc(const_ok, 1)
            def load_pair(t, p):
                g = t * HP + p
                pool.wait_ge(q_cut_ok, g + 1)
                pool.dma_start(q[:, :], qkv[bass.ds(p, 1), :, bass.ds(t * TILE, TILE)]
                               .rearrange("a p n -> p (a n)")).then_inc(qv_in, 16)

                pool.wait_ge(v_cut_ok, g * NCB + 1)
                pool.wait_ge(vturn_ok, g * NCB + 1)
                load_window(pool, val, 2 * HP, t, p, qv_in)
                landed, scored = pool.to_reg(g * 48 + 48), pool.to_reg(g * 2 * NCB + 1)
                pool.wait_ge(const_ok, 3)
                pool.wait_ge(qv_in, landed)
                pool.wait_ge(scores_ok, scored)
                pool.tensor_copy(q_cut[:, :].rearrange("p (b r i) -> p r b i", b=NCB, r=ROWS_T),
                                 q[:, :].rearrange("p (r b i) -> p r b i", b=NCB, r=ROWS_T)).then_inc(q_cut_ok, 1)
                for cb in range(NCB):
                    pool.tensor_copy(v_cut[:, cb * NKEY:(cb + 1) * NKEY].rearrange("p (r c) -> p r c", c=KCOLS),
                                     grid(val[:, 0:KROWS * GRID])[:, :, key_start(cb):key_start(cb) + KCOLS])\
                        .then_inc(v_cut_ok, 1)

            load_pair(0, 0)
            with pool.Fori(0, NT) as t:
                last_made = pool.to_reg(t * N_TILE + 2)
                pool.wait_ge(const_ok, 3)
                pool.wait_ge(w_used, last_made)
                pool.memset(prob[:, :, NKEY + NMETA:512], 0.0).then_inc(const_ok, 1)
                with pool.Fori(1, HP) as p:
                    load_pair(t, p)
                pool.wait_ge(h_stored, t * SUB_T * 16 + 1)
                pool.wait_ge(hturn_ok, t * SUB_T + 1)
                pool.dma_start(rows[:, :, :], a["x_rows"][bass.ds(t * TILE, TILE), :]
                               .rearrange("(s p) n -> p s n", p=P)).then_inc(rows_in, 16)
                with pool.If(t < NT - 1):
                    load_pair(next_tile(t), 0)
                for s in range(SUB_T):
                    c = t * SUB_T + s
                    known = pool.to_reg(c + 2)
                    pool.wait_ge(const_ok, 3)
                    pool.wait_ge(mom_ok, known)
                    pool.tensor_scalar(mom[:, s, 1:2], mom[:, s, 1:2], EPS, None, ALU.add).then_inc(var_ok, 1)
                    pool.wait_ge(var_ok, c + 1)
                    pool.tensor_tensor(mom[:, s, 2:3], mom[:, s, 1:2], neg_half[:, 0:1], ALU.pow).then_inc(rstd_ok, 1)
                    pool.wait_ge(const_in, 64)
                    pool.wait_ge(norm_ok, c + 1)
                    pool.tensor_tensor(rows[:, s, :], rows[:, s, :], ln_g[:, :], ALU.mult).then_inc(gain_ok, 1)

        @block.scalar
        def _(act):
            for s in (max_ok, exp_ok, sum_ok, turn_ok, pv_ok, o_ok):
                act.sem_inc(s, 2)

            def high(t, at, half, width=D):
                n = t * N_TILE + at
                act.wait_ge(w_in[half % 2], t * W_IN_TILE * 16 + (at // 2) * 16 + 16)
                act.wait_ge(w_used, n + 1)
                act.activation(w_hi[:, half % 2, 0:width], w_raw[:, half % 2, 0:width], ACT.Copy)\
                   .then_inc(w_hi_ok, 1)

            def x_high(t):
                for j in range(4):
                    act.wait_ge(x_in[j % 2], t * 32 + (j // 2) * 16 + 16)
                    act.activation(x_hi[:, 2 * j:2 * j + 2, :].rearrange("p k n -> p (k n)"),
                                   x_raw[:, j % 2, :], ACT.Copy).then_inc(x_hi_ok, 1)

            high(0, 0, 0)
            act.dma_start(conv_wb[:, :], a["conv_wb"]).then_inc(const_in, 16)
            act.dma_start(w_router[:, :, :].rearrange("p k n -> p (k n)"), a["w_router"]).then_inc(const_in, 16)
            act.dma_start(ln_g[:, :], a["ln"][0:1, :].broadcast_to([P, D])).then_inc(const_in, 16)
            act.dma_start(ln_b[:, :], a["ln"][1:2, :].broadcast_to([P, D])).then_inc(const_in, 16)
            with act.Fori(0, NT) as t:
                n0 = t * N_TILE
                with act.Fori(0, HP) as p:
                    g = t * HP + p

                    def out_rows(cb, h):
                        u2 = (g * NCB + cb) * 2 + h
                        act.wait_ge(pv_ok, u2 + 4)
                        act.wait_ge(sum_ok, u2 + 3)
                        act.wait_ge(oturn_ok, g * NCB + cb + 1)
                        act.activation(o_rows[:, h * DH:(h + 1) * DH], outp[:, h * DH:(h + 1) * DH], ACT.Copy,
                                       scale=rsum[:, h:h + 1]).then_inc(o_ok, 1)

                    def out_high(cb):
                        act.wait_ge(oturn_ok, g * NCB + cb + 2)
                        act.activation(o_block(o_hi, p, cb),
                                       outp[:, P:2 * P].rearrange("p (r c) -> p r c", c=16), ACT.Copy)\
                           .then_inc(o_hi_ok, 1)

                    def y_high(f):
                        act.wait_ge(conv_step, (g * 2 + f) * 8 + 9)
                        act.activation(y_hi[:, bass.ds((p * 2 + f) * TILE, TILE)], y[:, :], ACT.Copy)\
                           .then_inc(y_hi_ok, 1)

                    for step, at in attention_schedule():
                        if step == "scores":
                            unit = g * NCB + at
                            if at:
                                out_rows(at - 1, 1)
                            act.wait_ge(vturn_ok, unit + 2)
                            act.wait_ge(pv_ok, unit * 2 + 1)
                            if at == 0:
                                act.activation(vmeta[:, :], turned[0:NMETA, NKEY:512], ACT.Copy)
                            act.activation(vkeys[:, at % 2, :], turned[:, 0:NKEY], ACT.Copy).then_inc(vkeys_ok, 1)
                            for h in range(2):
                                act.wait_ge(const_ok, t + 4)
                                act.wait_ge(max_ok, unit * 2 + h + 3)
                                act.wait_ge(turn_ok, unit * 2 + h + 1)
                                act.wait_ge(sum_ok, unit * 2 + h + 1)
                                act.activation(prob[:, h, 0:NKEY + NMETA], sbias[:, h, :], ACT.Exp,
                                               bias=nmax[:, h:h + 1], accum_out=ssum[:, h:h + 1])\
                                   .then_inc(exp_ok, 1)
                        elif step == "turn0":
                            if at:
                                out_high(at - 1)
                        elif step == "turn1":
                            unit = g * NCB + at
                            act.wait_ge(turn_ok, unit * 2 + 4)
                            act.wait_ge(pv_ok, unit * 2 + 3)
                            act.activation(prob_t[:, 1, :], turned[:, :], ACT.Copy).then_inc(prob_t_ok[1], 1)
                            out_rows(at, 0)
                        elif step == "drain_values":
                            out_rows(at, 1)
                        elif step == "drain_turn":
                            out_high(at)
                        else:
                            grp, k = at
                            n = n0 + p * NPAIR + grp
                            if k == 0:
                                high(t, p * NPAIR + grp + 1, grp + 1)
                            if grp == 3 and k == 2:
                                y_high(0)
                            if grp % 3 == 0 and k == KD - 1:
                                f = g * 2 + grp // 3
                                act.wait_ge(w_used, n + 3)
                                act.wait_ge(conv_step, f * 8 + 1)
                                act.activation(c_sb[:, :], bank[0][:, :], ACT.Copy).then_inc(c_ok, 1)
                    y_high(1)
                with act.Fori(0, FB) as f:
                    n, m = n0 + N_CXB + f * 4, t * FB + f
                    high(t, N_CXB + f * 4 + 1, 1, HP * P)
                    high(t, N_CXB + f * 4 + 2, 2)
                    act.wait_ge(w_used, n + 3)
                    act.wait_ge(y_lo_ok, t * FB + FB + 1)
                    act.wait_ge(o_lo_ok, t * 16 + 17)
                    act.wait_ge(m_step, m * 3 + 1)
                    act.activation(sig_a[:, :], bank[0][:, :], ACT.Sigmoid).then_inc(sig_a_ok, 1)
                    high(t, N_CXB + f * 4 + 3, 3)
                    act.wait_ge(w_used, n + 5)
                    act.activation(sig_c[:, :], bank[2][:, :], ACT.Sigmoid).then_inc(sig_c_ok, 1)
                    high(t, N_CXB + f * 4 + 4, 4)
                    act.wait_ge(m_step, m * 3 + 4)
                    act.activation(m_hi[:, bass.ds(f * TILE, TILE)], m_att[:, :], ACT.Copy).then_inc(m_hi_ok, 1)
                n1 = n0 + N_CXB + N_MERGE
                act.wait_ge(w_used, n1 + 2)
                for j in range(1, N_OUT):
                    src, landed = raw_out(j)
                    if j % 4 < 2:
                        act.wait_ge(landed, t * W_IN_TILE * 16 + (W_IN_TILE - 2 + j // 4) * 16 + 16)
                    else:
                        act.wait_ge(landed, t * 32 + (j // 4) * 16 + 16)
                    act.activation(out_hi[j], src, ACT.Copy).then_inc(w_hi_ok, 1)
                with act.If(t < NT - 1):
                    x_high(t)

                def store(s):
                    c = t * SUB_T + s
                    act.wait_ge(h_ok, c + 1)
                    act.dma_start(h_rows[bass.ds(c * P, P), :], rows[:, s, :]).then_inc(h_stored, 16)

                def copy_turned(s):
                    act.wait_ge(hturn_ok, t * SUB_T + s + 2)
                    act.activation(h_t[:, 0:512], bank[3][:, :], ACT.Copy).then_inc(h_t_ok[0], 1)

                def copy_logits(s):
                    c = t * SUB_T + s
                    act.wait_ge(log_ok, c + 1)
                    act.activation(logits[:, bass.ds(c * NLOG, NLOG)], bank[5][:, 0:NLOG], ACT.Copy)\
                       .then_inc(log_out, 1)

                store(0)
                store(1)
                with act.If(t < NT - 1):
                    act.wait_ge(w_in[0], (t + 1) * W_IN_TILE * 16 + 16)
                    act.wait_ge(w_used, n1 + 3)
                    act.activation(w_hi[:, 0, :], w_raw[:, 0, :], ACT.Copy).then_inc(w_hi_ok, 1)
                copy_turned(0)
                store(2)
                for s in range(SUB_T):
                    copy_logits(s)
                    if s == SUB_T - 2:
                        store(SUB_T - 1)
                    if s < SUB_T - 1:
                        copy_turned(s + 1)
            act.wait_ge(h_stored, NSUB * 16 + 1)

        @block.vector
        def _(dve):
            dve.sem_inc(w_lo_ok, 2)
            dve.sem_inc(x_lo_ok, 2)

            def low(n, half, width=D):
                dve.wait_ge(w_hi_ok, n + 1)
                dve.wait_ge(w_used, n + 1)
                dve.tensor_tensor(w_lo[:, half % 2, 0:width], w_raw[:, half % 2, 0:width],
                                  w_hi[:, half % 2, 0:width].bitcast(F32), ALU.subtract).then_inc(w_lo_ok, 1)

            def x_low(t):
                for j in range(4):
                    dve.wait_ge(x_hi_ok, t * 4 + j + 1)
                    dve.tensor_tensor(x_lo[:, 2 * j:2 * j + 2, :].rearrange("p k n -> p (k n)"), x_raw[:, j % 2, :],
                                      x_hi[:, 2 * j:2 * j + 2, :].rearrange("p k n -> p (k n)").bitcast(F32),
                                      ALU.subtract).then_inc(x_lo_ok, 1)

            low(0, 0)
            with dve.Fori(0, NT) as t:
                n0 = t * N_TILE
                with dve.Fori(0, HP) as p:
                    g = t * HP + p

                    def one_over_sum(cb, h):
                        u2 = (g * NCB + cb) * 2 + h
                        dve.wait_ge(exp_ok, u2 + 3)
                        dve.wait_ge(o_ok, u2 + 1)
                        dve.reciprocal(rsum[:, h:h + 1], ssum[:, h:h + 1]).then_inc(sum_ok, 1)

                    def out_low(cb):
                        dve.wait_ge(o_hi_ok, g * NCB + cb + 1)
                        dve.tensor_tensor(o_block(o_lo, p, cb),
                                          outp[:, P:2 * P].rearrange("p (r c) -> p r c", c=16),
                                          o_block(o_hi, p, cb).bitcast(F32), ALU.subtract).then_inc(o_lo_ok, 1)

                    def y_low(f):
                        dve.wait_ge(y_hi_ok, g * 2 + f + 1)
                        at = bass.ds((p * 2 + f) * TILE, TILE)
                        dve.tensor_tensor(y_lo[:, at], y[:, :], y_hi[:, at].bitcast(F32), ALU.subtract)\
                           .then_inc(y_lo_ok, 1)

                    for step, at in attention_schedule():
                        if step == "scores":
                            for h in range(2):
                                u2 = (g * NCB + at) * 2 + h
                                here, used = dve.to_reg(u2 + 2), dve.to_reg(u2 + 1)
                                dve.wait_ge(const_ok, 3)
                                dve.wait_ge(scores_ok, here)
                                dve.wait_ge(exp_ok, used)
                                dve.tensor_tensor_reduce(
                                    out=sbias[:, h, NKEY:], in0=score[h][:, NKEY:NKEY + NMETA], in1=zeros[:, :],
                                    scale=1.0, scalar=NEG, op0=ALU.add, op1=ALU.max,
                                    accum_out=smeta[:, h:h + 1]).then_inc(max_step, 1)
                                meta_done, landed = dve.to_reg(u2 * 2 + 1), dve.to_reg((g + 1) * ROWS_T * 16)
                                dve.wait_ge(const_ok, 3)
                                dve.wait_ge(max_step, meta_done)
                                dve.wait_ge(bias_in, landed)
                                dve.tensor_tensor_reduce(
                                    out=sbias[:, h, 0:NKEY].rearrange("p (r c) -> p r c", c=KCOLS),
                                    in0=score[h][:, 0:NKEY].rearrange("p (r c) -> p r c", c=KCOLS),
                                    in1=bias[:, h, :].rearrange("p (r c) -> p r c", c=64)
                                    [:, :, 16 + key_start(at) - 16 * at:][:, :, 0:KCOLS],
                                    scale=1.0, scalar=smeta[:, h:h + 1], op0=ALU.add, op1=ALU.max,
                                    accum_out=smax[:, h:h + 1]).then_inc(max_step, 1)
                                dve.wait_ge(max_step, u2 * 2 + 2)
                                dve.tensor_scalar(nmax[:, h:h + 1], smax[:, h:h + 1], -1.0, None, ALU.mult)\
                                   .then_inc(max_ok, 1)
                        elif step == "turn0":
                            one_over_sum(at, 0)
                            unit = g * NCB + at
                            dve.wait_ge(turn_ok, unit * 2 + 3)
                            dve.wait_ge(pv_ok, unit * 2 + 2)
                            dve.tensor_copy(prob_t[:, 0, :], turned[:, :]).then_inc(prob_t_ok[0], 1)
                            one_over_sum(at, 1)
                            if at:
                                out_low(at - 1)
                        elif step == "drain_turn":
                            out_low(at)
                        elif step == "chunk":
                            grp, k = at
                            n = n0 + p * NPAIR + grp
                            f = g * 2 + grp // 3
                            wb = lambda j: conv_wb[:, bass.ds(p * 8 + grp // 3 * 4 + j, 1)]
                            edge = lambda e: edges[:, bass.ds((p * 2 + grp // 3) * NEDGE + e, 1)]
                            if k == 0:
                                low(n + 1, grp + 1)
                            if grp == 3 and k == 3:
                                y_low(0)
                            if k == 1 and grp % 3 == 2:
                                dve.wait_ge(w_used, n + 2)
                                dve.wait_ge(c_ok, f + 2)
                                dve.tensor_tensor(u[:, 1:TILE + 1], c_sb[:, :], bank[1][:, :], ALU.mult)\
                                   .then_inc(conv_step, 1)
                                dve.tensor_copy(u[:, 0:1], edge(t * 2)).then_inc(conv_step, 1)
                                dve.tensor_copy(u[:, TILE + 1:], edge(t + RIGHT)).then_inc(conv_step, 1)
                                dve.wait_ge(conv_step, f * 8 + 4)
                                dve.tensor_copy(edge(t * 3 + 2), u[:, TILE:TILE + 1]).then_inc(conv_step, 1)
                                dve.wait_ge(const_in, 64)
                                dve.wait_ge(y_lo_ok, f + 1)
                                dve.tensor_scalar(y[:, :], u[:, 0:TILE], wb(0), wb(3), ALU.mult, ALU.add)\
                                   .then_inc(conv_step, 1)
                                for j in (1, 2):
                                    dve.wait_ge(conv_step, f * 8 + 4 + j + 1)
                                    dve.scalar_tensor_tensor(y[:, :], u[:, j:TILE + j], wb(j), y[:, :], ALU.mult, ALU.add)\
                                       .then_inc(conv_step, 1)
                            if k == KD - 1 and grp % 3 == 2:
                                dve.wait_ge(w_used, n + 3)
                                dve.wait_ge(conv_step, f * 8 + 8)
                                dve.tensor_tensor(y[:, :], y[:, :], bank[2][:, :], ALU.mult).then_inc(conv_step, 1)
                    y_low(1)
                with dve.Fori(0, FB) as f:
                    n, m = n0 + N_CXB + f * 4, t * FB + f
                    low(n + 1, 1, HP * P)
                    low(n + 2, 2)
                    dve.wait_ge(w_used, n + 4)
                    dve.wait_ge(sig_a_ok, m + 2)
                    dve.wait_ge(m_hi_ok, m + 1)
                    dve.tensor_tensor(m_att[:, :], sig_a[:, :], bank[1][:, :], ALU.mult).then_inc(m_step, 1)
                    low(n + 3, 3)
                    low(n + 4, 4)
                    dve.wait_ge(w_used, n + 6)
                    dve.wait_ge(sig_c_ok, m + 2)
                    dve.tensor_tensor(sig_c[:, :], sig_c[:, :], bank[7][:, :], ALU.mult).then_inc(m_step, 1)
                    dve.wait_ge(m_step, m * 3 + 3)
                    dve.tensor_tensor(m_att[:, :], m_att[:, :], sig_c[:, :], ALU.add).then_inc(m_step, 1)
                    dve.wait_ge(m_hi_ok, m + 2)
                    at = bass.ds(f * TILE, TILE)
                    dve.tensor_tensor(m_lo[:, at], m_att[:, :], m_hi[:, at].bitcast(F32), ALU.subtract)\
                       .then_inc(m_lo_ok, 1)
                n1 = n0 + N_CXB + N_MERGE
                dve.wait_ge(w_used, n1 + 2)
                for j in range(1, N_OUT):
                    dve.wait_ge(w_hi_ok, n1 + j + 1)
                    dve.tensor_tensor(out_lo[j], raw_out(j)[0], out_hi[j].bitcast(F32), ALU.subtract)\
                       .then_inc(w_lo_ok, 1)
                with dve.If(t < NT - 1):
                    x_low(t)
                dve.wait_ge(rows_in, t * 16 + 16)

                def residual(s, half, step=None):
                    if s < SUB_T - 1:
                        dve.wait_ge(made, t * 4 + step)
                    else:
                        dve.wait_ge(w_used, n1 + 4 * half + 6)
                    part = rows[:, s, half * 512:(half + 1) * 512]
                    dve.scalar_tensor_tensor(part, part, ALPHA, bank[OUT_BANK[s][half]][:, :], ALU.mult, ALU.add)\
                       .then_inc(res_step, 1)

                def moments(s):
                    c = t * SUB_T + s
                    dve.wait_ge(res_step, c * 2 + 2)
                    dve.wait_ge(mom_ok, c + 1)
                    for half in range(2):
                        dve.bn_stats(stats[:, half * 6:half * 6 + 6], rows[:, s, half * 512:(half + 1) * 512])\
                           .then_inc(res_bn, 1)
                    taken = dve.to_reg(c * 2 + 2)
                    dve.wait_ge(const_in, 64)
                    dve.wait_ge(res_bn, taken)
                    dve.bn_aggr(mom[:, s, 0:2], stats[:, :]).then_inc(mom_ok, 1)

                def norm(s):
                    dve.wait_ge(rstd_ok, t * SUB_T + s + 1)
                    dve.tensor_scalar(rows[:, s, :], rows[:, s, :], mom[:, s, 0:1], mom[:, s, 2:3],
                                      ALU.subtract, ALU.mult).then_inc(norm_ok, 1)

                def offset(s):
                    dve.wait_ge(gain_ok, t * SUB_T + s + 1)
                    dve.tensor_tensor(rows[:, s, :], rows[:, s, :], ln_b[:, :], ALU.add).then_inc(h_ok, 1)

                def copy_turned(s):
                    dve.wait_ge(hturn_ok, t * SUB_T + s + 2)
                    dve.tensor_copy(h_t[:, 512:], bank[4][:, :]).then_inc(h_t_ok[1], 1)

                for s in range(2):
                    for half in range(2):
                        residual(s, half, half + 1)
                    moments(s)
                    norm(s)
                offset(0)
                residual(2, 0, 3)
                offset(1)
                residual(2, 1, 4)
                moments(2)
                norm(2)
                with dve.If(t < NT - 1):
                    dve.wait_ge(w_hi_ok, n0 + N_TILE + 1)
                    dve.tensor_tensor(w_lo[:, 0, :], w_raw[:, 0, :], w_hi[:, 0, :].bitcast(F32), ALU.subtract)\
                       .then_inc(w_lo_ok, 1)
                copy_turned(0)
                residual(3, 0)
                offset(2)
                residual(3, 1)
                copy_turned(1)
                moments(3)
                norm(3)
                copy_turned(2)
                offset(3)
                copy_turned(3)

        @block.tensor
        def _(pe):
            pe.sem_inc(w_used, 2)

            def product(ps, half, w, hi, lo, start, stop):
                pe.matmul(ps, w_hi[:, half % 2, w], hi, start=start, stop=False)
                pe.matmul(ps, w_hi[:, half % 2, w], lo, start=False, stop=False)
                return pe.matmul(ps, w_lo[:, half % 2, w], hi, start=False, stop=stop)

            with pe.Fori(0, NT) as t:
                n0 = t * N_TILE
                split, landed, copied = pe.to_reg(t * 4 + 2), pe.to_reg(t * 16 + 16), pe.to_reg(t * SUB_T + 1)
                pe.wait_ge(const_ok, 3)
                pe.wait_ge(x_lo_ok, split)
                pe.wait_ge(mask_in, landed)
                pe.wait_ge(log_out, copied)
                with pe.Fori(0, HP) as p:
                    g = t * HP + p

                    def values(cb, h):
                        u2 = (g * NCB + cb) * 2 + h
                        pe.wait_ge(vkeys_ok, g * NCB + cb + 1)
                        pe.wait_ge(prob_t_ok[h], g * NCB + cb + 2)
                        if h == 0:
                            pe.wait_ge(o_lo_ok, g * NCB + cb + 1)
                        else:
                            pe.wait_ge(o_ok, u2 + 2)
                        ps, c = outp[:, h * DH:(h + 1) * DH], slice(h * DH, (h + 1) * DH)
                        for j in range(NKEY // P):
                            pe.matmul(ps, prob_t[:, h, j * P:(j + 1) * P],
                                      vkeys[:, cb % 2, j * P + h * DH:j * P + (h + 1) * DH], start=(j == 0), stop=False)
                        pe.matmul(ps, prob_t[0:NMETA, h, NKEY:512], vmeta[:, c], start=False, stop=True)\
                          .then_inc(pv_ok, 1)

                    def turn_probs(cb, h):
                        pe.wait_ge(exp_ok, (g * NCB + cb) * 2 + h + 3)
                        for j in range(4):
                            last = pe.transpose(turned[:, j * P:(j + 1) * P], prob[:, h, j * P:(j + 1) * P], ident[:, :])
                        last.then_inc(turn_ok, 1)

                    def turn_outputs(cb):
                        pe.wait_ge(o_ok, (g * NCB + cb) * 2 + 4)
                        pe.transpose(outp[:, P:2 * P], o_rows[:, :], ident[:, :]).then_inc(oturn_ok, 1)

                    for step, at in attention_schedule():
                        unit = g * NCB + (at if step != "chunk" else 0)
                        if step == "scores":
                            if at:
                                values(at - 1, 1)
                            pe.wait_ge(key_in, (g + 1) * 32)
                            pe.wait_ge(q_cut_ok, g + 2)
                            pe.wait_ge(v_cut_ok, unit + 2)
                            pe.wait_ge(prob_t_ok[1], unit + 1)
                            for j in range(NKEY // P):
                                last = pe.transpose(turned[:, j * P:(j + 1) * P],
                                                    v_cut[:, at * NKEY + j * P:at * NKEY + (j + 1) * P], ident[:, :])
                            if at == 0:
                                last = pe.matmul(turned[0:NMETA, NKEY:512], val[:, KROWS * GRID:], ident[:, :],
                                                 start=True, stop=True)
                            last.then_inc(vturn_ok, 1)
                            rr, cc = window(at)
                            for h in range(2):
                                hh = slice(h * DH, (h + 1) * DH)
                                qs = q_cut[hh, at * P:(at + 1) * P]
                                pe.wait_ge(max_ok, unit * 2 + h + 1)
                                pe.matmul(score[h][:, 0:NKEY].rearrange("p (r c) -> p r c", c=KCOLS), qs,
                                          grid(key[hh, 0:KROWS * GRID])[:, rr, cc], start=True, stop=False)
                                pe.matmul(score[h][:, 0:NKEY], ident_b[:, :], mask[:, at * NKEY:(at + 1) * NKEY],
                                          start=False, stop=True)
                                pe.matmul(score[h][:, NKEY:NKEY + NMETA], qs, key[hh, KROWS * GRID:],
                                          start=True, stop=True).then_inc(scores_ok, 1)
                        elif step == "turn0":
                            pe.wait_ge(vkeys_ok, unit + 1)
                            turn_probs(at, 0)
                            if at:
                                turn_outputs(at - 1)
                        elif step == "turn1":
                            pe.wait_ge(prob_t_ok[0], unit + 2)
                            turn_probs(at, 1)
                            values(at, 0)
                        elif step == "drain_values":
                            values(at, 1)
                        elif step == "drain_turn":
                            turn_outputs(at)
                        else:
                            grp, k = at
                            n, f = n0 + p * NPAIR + grp, g * 2 + grp // 3
                            if k == 0:
                                pe.wait_ge(w_lo_ok, n + 3)
                                if grp % 3 == 0:
                                    pe.wait_ge(c_ok, f + 1)
                                elif grp % 3 == 1:
                                    pe.wait_ge(conv_step, f * 8 + 1)
                                else:
                                    pe.wait_ge(conv_step, f * 8 + 1)
                            last = product(bank[grp % 3][:, :], grp, slice(k * P, (k + 1) * P), x_hi[:, k, :], x_lo[:, k, :],
                                           k == 0, k == KD - 1)
                            if k == KD - 1:
                                last.then_inc(w_used, 1)
                c_read = pe.to_reg(t * FB + FB + 1)
                y_split, o_split = pe.to_reg(t * FB + FB + 1), pe.to_reg(t * 16 + 17)
                pe.wait_ge(const_ok, 3)
                pe.wait_ge(c_ok, c_read)
                with pe.Fori(0, FB) as f:
                    n, m = n0 + N_CXB + f * 4, t * FB + f

                    def branch(j, ps, nk, hi, lo, free, value):
                        pe.wait_ge(w_lo_ok, n + j + 3)
                        pe.wait_ge(free, value + 1)
                        for k in range(nk):
                            last = product(ps[:, :], j, slice(k * P, (k + 1) * P), hi(k), lo(k), k == 0, k == nk - 1)
                        last.then_inc(w_used, 1)

                    cut = lambda x: lambda k: x[:, k * TILE:(k + 1) * TILE]
                    xc = lambda x: lambda k: x[:, k, :]
                    branch(0, bank[0], KD, xc(x_hi), xc(x_lo), sig_a_ok, m)
                    pe.wait_ge(o_lo_ok, o_split)
                    pe.wait_ge(y_lo_ok, y_split)
                    branch(1, bank[1], HP, cut(o_hi), cut(o_lo), m_step, m * 3)
                    branch(2, bank[2], KD, xc(x_hi), xc(x_lo), sig_c_ok, m)
                    branch(3, bank[7], KD, cut(y_hi), cut(y_lo), m_step, m * 3)
                n1 = n0 + N_CXB + N_MERGE

                def out_product(subtiles, half):
                    for j in range(4 * half, 4 * half + 4):
                        if subtiles[0] == 0:
                            pe.wait_ge(w_lo_ok, n1 + j + 3)
                            pe.wait_ge(m_lo_ok, t * FB + 2 * (j % 4) + 2)
                        for kk in range(2):
                            k, w = 2 * (j % 4) + kk, slice(kk * 512, (kk + 1) * 512)
                            for s in subtiles:
                                ps = bank[OUT_BANK[s][half]][:, :]
                                ms = slice(k * TILE + s * P, k * TILE + (s + 1) * P)
                                pe.matmul(ps, m_hi[:, ms], out_hi[j][:, w], start=(k == 0), stop=False)
                                pe.matmul(ps, m_hi[:, ms], out_lo[j][:, w], start=False, stop=False)
                                last = pe.matmul(ps, m_lo[:, ms], out_hi[j][:, w], start=False, stop=(k == KD - 1))
                        if subtiles[-1] == SUB_T - 1:
                            last.then_inc(w_used, 1)
                    if subtiles[-1] < SUB_T - 1:
                        last.then_inc(made, 1)

                def turn(s):
                    c = t * SUB_T + s
                    pe.wait_ge(h_ok, c + 1)
                    pe.wait_ge(h_t_ok[0], c + 1)
                    pe.wait_ge(h_t_ok[1], c + 1)
                    for k in range(KD):
                        last = pe.transpose(bank[3 + k // 4][:, (k % 4) * P:(k % 4 + 1) * P],
                                            rows[:, s, k * P:(k + 1) * P], ident[:, :])
                    last.then_inc(hturn_ok, 1)

                def route_logits(s):
                    c = t * SUB_T + s
                    pe.wait_ge(h_t_ok[0], c + 2)
                    pe.wait_ge(h_t_ok[1], c + 2)
                    pe.wait_ge(log_out, c + 1)
                    if s == 0:
                        pe.wait_ge(res_step, t * 8 + 4)
                    for k in range(KD):
                        last = pe.matmul(bank[5][:, 0:NLOG], h_t[:, k * P:(k + 1) * P], w_router[:, k, :],
                                         start=(k == 0), stop=(k == KD - 1))
                    last.then_inc(log_ok, 1)

                out_product((0, 1), 0)
                out_product((0, 1), 1)
                out_product((2,), 0)
                out_product((2,), 1)
                out_product((3,), 0)
                turn(0)
                out_product((3,), 1)
                for s in range(SUB_T):
                    route_logits(s)
                    if s < SUB_T - 1:
                        turn(s + 1)


GU, DN = 4, 2


def load_expert(sp, a, r, raw, raw_in, b, part, free):
    e = sp.value_load(r["owner"][0:1, bass.ds(b, 1)], min_val=0, max_val=NEXP - 1)
    for c in range((GU, DN)[part]):
        slot = part * GU + c
        src = a[("w_e_gate", "w_e_up", "w_e_down")[slot // 2]][bass.ds(e, 1), :, :]
        half = slice((c % 2) * 512, (c % 2) * 512 + 512)
        src = src[:, half, :] if part == 0 else src[:, :, half]
        free(c)
        sp.dma_start(raw[:, slot, :].rearrange("p (k n) -> p k n", k=4),
                     src.rearrange("a (k p) n -> p (a k) n", p=P)).then_inc(raw_in[slot], 16)


def route(nc, a, logits, ident, r, raw, raw_in):
    NP = 2 * NSUB
    MARKS = 4
    with ExitStack() as ctx:
        sb = lambda n, s, d=F32: ctx.enter_context(nc.sbuf_tensor(n, s, d))
        sem = lambda n: ctx.enter_context(nc.semaphore(n))
        ints = sb("ints", [P, 512], I32)
        lane = sb("lane", [P, P])
        block_no = sb("block_no", [P, NPLAN])
        edge128 = sb("edge128", [P, NSUB])
        token = sb("token", [P, NP])
        spare = sb("spare", [P, 1])
        rank_g, rank_e = sb("rank_g", [P, NG]), sb("rank_e", [P, NEXP])
        ones = sb("ones", [P, NEXP])
        below = sb("below", [P, P], BF16)
        all_one = sb("all_one", [P, P], BF16)
        gdiff, gexp, ghot = (sb(n, [P, NSUB, NG]) for n in ("gdiff", "gexp", "ghot"))
        masked = sb("masked", [P, NSUB, NEXP])
        weight = sb("weight", [P, NSUB, NEXP])
        hot = [sb(f"hot{c}", [P, NSUB, NEXP]) for c in range(2)]
        chosen = sb("chosen", [P, NSUB, NEXP], BF16)
        col = [sb(f"col{j}", [P, NSUB]) for j in range(8)]
        gmax, gsum, best, top1, top2, ediff, e2, den = col
        place = sb("place", [P, NSUB, NEXP])
        count, blocks, pend, pstart = (sb(n, [P, NEXP]) for n in ("count", "blocks", "pend", "pstart"))
        over = sb("over", [P, NEXP, NSUB])
        under, begins = sb("under", [P, NEXP]), sb("begins", [P, NEXP])
        plan_col = sb("plan_col", [P, 2])
        one_row = sb("one_row", [1, NPLAN])
        fresh_f, visit_f = sb("fresh_f", [1, NPLAN]), sb("visit_f", [1, NPLAN])
        slot_f, slot_i = sb("slot_f", [P, NP]), sb("slot_i", [P, NP], I32)
        code, empty, second = (sb(n, [P, NPLAN]) for n in ("code", "empty", "second"))
        part_i = sb("part_i", [P, 2, NP], I32)
        part_f = sb("part_f", [P, 2, NP])
        at_lane = sb("at_lane", [P, MARKS, P])
        at_block = sb("at_block", [P, MARKS, NPLAN])
        ranks_ps = ctx.enter_context(nc.psum_tensor("ranks_ps", [P, 512], F32))
        count_ps = ctx.enter_context(nc.psum_tensor("count_ps", [P, 512], F32))
        table_ps = ctx.enter_context(nc.psum_tensor("table_ps", [P, 512], F32))
        plan_ps = ctx.enter_context(nc.psum_tensor("plan_ps", [P, 512], F32))
        iota_step = sem("iota_step")
        gdiff_ok, gexp_ok = sem("gdiff_ok"), sem("gexp_ok")
        ediff_ok, e2_ok = sem("ediff_ok"), sem("e2_ok")
        chosen_ok = sem("chosen_ok")
        counted = sem("counted")
        plan_ok = sem("plan_ok")
        owner_ok = sem("owner_ok")
        plan_rows = sem("plan_rows")
        hots_ok = sem("hots_ok")
        hots_used = sem("hots_used")
        step = sem("route_step")
        block = ctx.enter_context(nc.Block())

        def spread(t, n):
            return t.unsqueeze(2).broadcast_to([t.shape[0], t.shape[1], n])

        @block.sync
        def _(sp):
            sp.wait_ge(owner_ok, 1)
            for part in range(2):
                load_expert(sp, a, r, raw, raw_in, 0, part, lambda c: None)

        @block.gpsimd
        def _(pool):
            done = [0]

            def link(ins):
                done[0] += 1
                ins.then_inc(iota_step, 1)
                pool.wait_ge(iota_step, done[0])

            for t, pattern, mult, base in ((rank_g, [[-1, NG]], 0, NG), (rank_e, [[-1, NEXP]], 0, NEXP),
                                           (lane, [[1, P]], 0, 0), (block_no, [[1, NPLAN]], 0, 0),
                                           (edge128, [[P, NSUB]], 0, 0), (token, [[P, NP]], 1, 1),
                                           (spare, [[1, 1]], 1, 2 * NTOK + 1)):
                n = pattern[0][1]
                link(pool.iota(ints[:, 0:n], pattern=pattern, base=base, channel_multiplier=mult))
                link(pool.tensor_copy(t[:, :], ints[:, 0:n]))
            link(pool.memset(ones[:, :], 1.0))
            link(pool.memset(all_one[:, :], 1.0))
            link(pool.affine_select(out=below[:, :], in_=all_one[:, :], compare_op=ALU.is_gt, fill=0.0, base=0,
                                    pattern=[[1, P]], channel_multiplier=-1))

        @block.scalar
        def _(act):
            act.wait_ge(gdiff_ok, 1)
            act.activation(gexp[:, :, :].rearrange("p s g -> p (s g)"), gdiff[:, :, :].rearrange("p s g -> p (s g)"),
                           ACT.Exp).then_inc(gexp_ok, 1)
            act.wait_ge(ediff_ok, 1)
            act.activation(e2[:, :], ediff[:, :], ACT.Exp).then_inc(e2_ok, 1)

        @block.vector
        def _(dve):
            done = [0]

            def link(ins):
                done[0] += 1
                ins.then_inc(step, 1)
                dve.wait_ge(step, done[0])

            lg = logits[:, :].rearrange("p (s n) -> p s n", n=NLOG)
            link(dve.reduce_max(gmax[:, :], lg[:, :, 0:NG], AX.X))
            dve.tensor_tensor(gdiff[:, :, :], lg[:, :, 0:NG], spread(gmax[:, :], NG), ALU.subtract).then_inc(gdiff_ok, 1)
            dve.wait_ge(gdiff_ok, 1)
            link(dve.tensor_scalar(ghot[:, :, :], gdiff[:, :, :], 0.0, None, ALU.is_equal))
            dve.wait_ge(iota_step, 4)
            link(dve.tensor_tensor(ghot[:, :, :], ghot[:, :, :],
                                   rank_g[:, :].unsqueeze(1).broadcast_to([P, NSUB, NG]), ALU.mult))
            link(dve.reduce_max(best[:, :], ghot[:, :, :], AX.X))
            link(dve.tensor_tensor(ghot[:, :, :], ghot[:, :, :], spread(best[:, :], NG), ALU.is_equal))
            dve.wait_ge(gexp_ok, 1)
            link(dve.reduce_sum(gsum[:, :], gexp[:, :, :], AX.X))
            link(dve.tensor_scalar(ghot[:, :, :], ghot[:, :, :], -NEG, NEG, ALU.mult, ALU.add))
            link(dve.tensor_tensor(
                masked[:, :, :].rearrange("p s (g e) -> p s g e", g=NG),
                lg[:, :, NG:].rearrange("p s (g e) -> p s g e", g=NG),
                ghot[:, :, :].unsqueeze(3).broadcast_to([P, NSUB, NG, EPG]), ALU.add))
            for c, top in ((0, top1), (1, top2)):
                link(dve.reduce_max(top[:, :], masked[:, :, :], AX.X))
                link(dve.tensor_tensor(weight[:, :, :], masked[:, :, :], spread(top[:, :], NEXP), ALU.is_equal))
                link(dve.tensor_tensor(weight[:, :, :], weight[:, :, :],
                                       rank_e[:, :].unsqueeze(1).broadcast_to([P, NSUB, NEXP]), ALU.mult))
                link(dve.reduce_max(best[:, :], weight[:, :, :], AX.X))
                link(dve.tensor_tensor(hot[c][:, :, :], weight[:, :, :], spread(best[:, :], NEXP), ALU.is_equal))
                if c == 0:
                    link(dve.scalar_tensor_tensor(masked[:, :, :], hot[0][:, :, :], 3 * NEG, masked[:, :, :],
                                                  ALU.mult, ALU.add))
            dve.tensor_tensor(chosen[:, :, :], hot[0][:, :, :], hot[1][:, :, :], ALU.add).then_inc(chosen_ok, 1)
            dve.tensor_tensor(ediff[:, :], top2[:, :], top1[:, :], ALU.subtract).then_inc(ediff_ok, 1)
            dve.wait_ge(e2_ok, 1)
            link(dve.tensor_scalar(den[:, :], e2[:, :], 1.0, None, ALU.add))
            link(dve.tensor_tensor(den[:, :], den[:, :], gsum[:, :], ALU.mult))
            link(dve.reciprocal(r["gates"][:, 0:NSUB], den[:, :]))
            link(dve.tensor_tensor(r["gates"][:, NSUB:], r["gates"][:, 0:NSUB], e2[:, :], ALU.mult))
            dve.wait_ge(iota_step, 17)
            dve.wait_ge(counted, 1)
            link(dve.tensor_copy(count[:, :], count_ps[:, 0:NEXP]))
            link(dve.tensor_tensor(over[:, :, :], spread(count[:, :], NSUB),
                                   edge128[:, :].unsqueeze(1).broadcast_to([P, NEXP, NSUB]), ALU.is_gt))
            link(dve.reduce_sum(blocks[:, :], over[:, :, :], AX.X))
            link(dve.tensor_tensor_scan(pend[:, :], ones[:, :], blocks[:, :], 0.0, ALU.mult, ALU.add))
            link(dve.tensor_tensor(pstart[:, :], pend[:, :], blocks[:, :], ALU.subtract))
            link(dve.tensor_scalar(under[:, :], pend[:, :], token[:, 0:1], None, ALU.is_lt))
            link(dve.reduce_sum(plan_col[:, 0:1], under[:, :], AX.X))
            link(dve.tensor_scalar(plan_col[:, 0:1], plan_col[:, 0:1], float(NEXP - 1), None, ALU.min))
            link(dve.tensor_scalar(under[:, :], blocks[:, :], 0.0, None, ALU.is_gt))
            link(dve.tensor_scalar(begins[:, :], pstart[:, :], 1.0, token[:, 0:1], ALU.add, ALU.is_equal))
            link(dve.tensor_tensor(under[:, :], begins[:, :], under[:, :], ALU.mult))
            dve.reduce_sum(plan_col[:, 1:2], under[:, :], AX.X).then_inc(plan_ok, 1)
            link(dve.tensor_copy(r["used"][:, :], pend[0:1, NEXP - 1:NEXP]))
            link(dve.memset(one_row[:, :], 1.0))
            link(dve.tensor_scalar(pstart[:, :], pstart[:, :], float(P), None, ALU.mult))
            link(dve.tensor_tensor(place[:, :, :], ranks_ps[:, 0:NSUB * NEXP].rearrange("p (s e) -> p s e", e=NEXP),
                                   pstart[:, :].unsqueeze(1).broadcast_to([P, NSUB, NEXP]), ALU.add))
            for c in range(2):
                link(dve.tensor_tensor(weight[:, :, :], hot[c][:, :, :], place[:, :, :], ALU.mult))
                link(dve.reduce_sum(slot_f[:, c * NSUB:(c + 1) * NSUB], weight[:, :, :], AX.X))
            link(dve.tensor_copy(slot_i[:, :], slot_f[:, :]))
            link(dve.tensor_scalar(part_i[:, 0, :], slot_i[:, :], P - 1, None, ALU.bitwise_and))
            link(dve.tensor_scalar(part_i[:, 1, :], slot_i[:, :], 7, None, ALU.logical_shift_right))
            link(dve.tensor_copy(part_f[:, :, :], part_i[:, :, :]))
            dve.wait_ge(plan_rows, 1)
            dve.tensor_copy(r["owner"][:, :], plan_ps[0:1, 0:NPLAN]).then_inc(owner_ok, 1)
            link(dve.tensor_copy(fresh_f[:, :], plan_ps[0:1, P:P + NPLAN]))
            link(dve.tensor_tensor_scan(visit_f[:, :], one_row[:, :], fresh_f[:, :], -1.0, ALU.mult, ALU.add))
            link(dve.tensor_copy(r["fresh"][:, :], fresh_f[:, :]))
            link(dve.tensor_copy(r["visit"][:, :], visit_f[:, :]))
            for g in range(NP):
                dve.wait_ge(hots_used, g + 1)
                dve.tensor_scalar(at_lane[:, g % MARKS, :], lane[:, :], part_f[:, 0, g:g + 1], None, ALU.is_equal)
                dve.tensor_scalar(at_block[:, g % MARKS, :], block_no[:, :], part_f[:, 1, g:g + 1],
                                  token[:, g:g + 1], ALU.is_equal, ALU.mult).then_inc(hots_ok, 1)
            dve.wait_ge(hots_used, NP + MARKS)
            link(dve.tensor_copy(code[:, :], table_ps[:, 0:NPLAN]))
            link(dve.tensor_scalar(empty[:, :], code[:, :], 0.0, None, ALU.is_equal))
            link(dve.tensor_scalar(second[:, :], code[:, :], NTOK + 0.5, -float(NTOK), ALU.is_gt, ALU.mult))
            link(dve.tensor_scalar(code[:, :], code[:, :], 1.0, None, ALU.subtract))
            link(dve.tensor_tensor(second[:, :], code[:, :], second[:, :], ALU.add))
            link(dve.tensor_scalar(second[:, :], second[:, :], 0.0, None, ALU.max))
            link(dve.tensor_copy(r["table"][:, :], second[:, :]))
            link(dve.scalar_tensor_tensor(code[:, :], empty[:, :], spare[:, 0:1], code[:, :], ALU.mult, ALU.add))
            link(dve.tensor_copy(r["dest"][:, :], code[:, :]))

        @block.tensor
        def _(pe):
            pe.sem_inc(hots_used, MARKS)
            pe.wait_ge(iota_step, 17)
            pe.wait_ge(chosen_ok, 1)
            for i in range(NSUB):
                ps = ranks_ps[:, i * NEXP:(i + 1) * NEXP]
                for j in range(i):
                    pe.matmul(ps, all_one[:, :], chosen[:, j, :], start=(j == 0), stop=False)
                pe.matmul(ps, below[:, :], chosen[:, i, :], start=(i == 0), stop=True)
            for j in range(NSUB):
                last = pe.matmul(count_ps[:, 0:NEXP], all_one[:, :], chosen[:, j, :], start=(j == 0), stop=(j == NSUB - 1))
            last.then_inc(counted, 1)
            pe.wait_ge(plan_ok, 1)
            for j in range(2):
                last = pe.matmul(plan_ps[0:1, j * P:(j + 1) * P], plan_col[:, j:j + 1], ident[:, :], start=True, stop=True)
            last.then_inc(plan_rows, 1)
            for g in range(NP):
                pe.wait_ge(hots_ok, g + 1)
                pe.matmul(table_ps[:, 0:NPLAN], at_lane[:, g % MARKS, :], at_block[:, g % MARKS, :],
                          start=(g == 0), stop=(g == NP - 1)).then_inc(hots_used, 1)


def experts(nc, a, h_rows, y_rows, ident, r, raw, raw_in, ahead):
    with ExitStack() as ctx:
        sb = lambda n, s, d=F32: ctx.enter_context(nc.sbuf_tensor(n, s, d))
        sem = lambda n: ctx.enter_context(nc.semaphore(n))
        hi, lo = sb("e_hi", [P, GU + DN, 2048], F32R), sb("e_lo", [P, GU + DN, 2048], F32R)
        xg = sb("e_xg", [P, 2, D])
        index = sb("e_index", [P, 2], I32)
        out_index = sb("e_out_index", [P, 2], I32)
        x_hi, x_lo = sb("e_x_hi", [P, D], F32R), sb("e_x_lo", [P, D], F32R)
        gate, hid = sb("e_gate", [P, DE]), sb("e_hid", [P, DE])
        h_hi, h_lo = sb("e_h_hi", [P, DE], F32R), sb("e_h_lo", [P, DE], F32R)
        y = sb("e_y", [P, 2, D])
        ps = [ctx.enter_context(nc.psum_tensor(f"e_ps{j}", [P, 512], F32)) for j in range(7)]
        gate_ps, up_ps, x_ps, h_ps, y_ps = ps[0], ps[1], ps[2:4], ps[4], ps[5:7]
        hi_ok = [sem("e_gu_hi_ok"), sem("e_dn_hi_ok")]
        lo_ok = [sem("e_gu_lo_ok"), sem("e_dn_lo_ok")]
        used = [sem("e_gu_used"), sem("e_dn_used")]
        index_ok = sem("e_index_ok")
        dest_ok = sem("e_dest_ok")
        xg_in = [sem(f"e_xg_in{s}") for s in range(2)]
        xt_ok = sem("e_xt_ok")
        x_hi_ok = [sem("e_x_hi0_ok"), sem("e_x_hi1_ok")]
        x_lo_ok = [sem("e_x_lo0_ok"), sem("e_x_lo1_ok")]
        gate_ok = sem("e_gate_ok")
        hid_ok = sem("e_hid_ok")
        ht_ok = sem("e_ht_ok")
        h_hi_ok, h_lo_ok = sem("e_h_hi_ok"), sem("e_h_lo_ok")
        y_ok = [sem("e_y0_ok"), sem("e_y1_ok")]
        y_out = [sem("e_y_out0"), sem("e_y_out1")]
        scrap = sb("e_scrap", [1, 4])
        block = ctx.enter_context(nc.Block())

        def plan(eng, name, b, top=NEXP - 1):
            return eng.value_load(r[name][0:1, bass.ds(b, 1)], min_val=0, max_val=top)

        def rounds(eng, body):
            n = eng.value_load(r["used"][0:1, 0:1], min_val=1, max_val=NBLK - 1)
            with eng.Fori(0, NBLK // 2) as i:
                for s in range(2):
                    with eng.If(i * 2 + s < n):
                        body(i * 2 + s, i, s, i * 2 + s + 1 < n)

        def chunks(part):
            return [(c, part * GU + c) for c in range((GU, DN)[part])]

        @block.sync
        def _(sp):
            def load(b, part):
                with sp.If(plan(sp, "fresh", b, 1) > 0):
                    v = plan(sp, "visit", b)
                    load_expert(sp, a, r, raw, raw_in, b, part,
                                lambda c: sp.wait_ge(lo_ok[part], v * (GU, DN)[part] + c + 1))

            def body(b, i, s, more):
                load(b + 1, 1)
                load(b + 3, 0)

            load(1, 0)
            load(2, 0)
            rounds(sp, body)
            sp.dma_start(ahead["ln_g"][:, :], a["ln"][2:3, :].broadcast_to([P, D])).then_inc(ahead["ln_in"], 16)
            sp.dma_start(ahead["ln_b"][:, :], a["ln"][3:4, :].broadcast_to([P, D])).then_inc(ahead["ln_in"], 16)
            for t in range(AHEAD):
                sp.dma_start(ahead["h"][:, t, :], h_rows[t * P:(t + 1) * P, :]).then_inc(ahead["rows_in"][t], 16)

        @block.gpsimd
        def _(pool):
            for s in (gate_ok, hid_ok, ht_ok, *x_lo_ok, xt_ok, h_lo_ok, *y_ok):
                pool.sem_inc(s, 1)

            def gather(b, i, s):
                copied, turned, last = pool.to_reg(b + 1), pool.to_reg(b), pool.to_reg(i * 16 + 16)
                pool.wait_ge(x_lo_ok[0], 1)
                if not isinstance(b, int) or b >= 2:
                    pool.wait_ge(xt_ok, turned)
                    pool.wait_ge(xg_in[s], last)
                pool.tensor_copy(index[:, s:s + 1], r["table"][:, bass.ds(b, 1)]).then_inc(index_ok, 1)
                pool.wait_ge(x_lo_ok[0], 1)
                pool.wait_ge(index_ok, copied)
                pool.indirect_dma_start(out=xg[:, s, :], out_offset=None, in_=h_rows,
                                        in_offset=bass.IndirectOffsetOnAxis(ap=index[:, s:s + 1], axis=0))\
                    .then_inc(xg_in[s], 16)

            def body(b, i, s, more):
                gather(b + 3, i + 1 + s, 1 - s)
                halves, copied = pool.to_reg(b + 2), pool.to_reg(b + 1)
                before, last = pool.to_reg(i * 16 + 16), pool.to_reg((i + s) * 16 + 16)
                pool.wait_ge(index_ok, 1)
                pool.wait_ge(y_out[s], before)
                pool.tensor_copy(out_index[:, s:s + 1], r["dest"][:, bass.ds(b, 1)]).then_inc(dest_ok, 1)
                pool.wait_ge(index_ok, 1)
                pool.wait_ge(dest_ok, copied)
                pool.wait_ge(y_ok[0], halves)
                pool.wait_ge(y_ok[1], halves)
                pool.wait_ge(y_out[1 - s], last)
                pool.indirect_dma_start(out=y_rows, in_=y[:, s, :], in_offset=None,
                                        out_offset=bass.IndirectOffsetOnAxis(ap=out_index[:, s:s + 1], axis=0))\
                    .then_inc(y_out[s], 16)

            gather(0, 0, 0)
            gather(1, 0, 1)
            for j, s in enumerate((*xg_in, *y_out)):
                pool.dma_start(scrap[:, j:j + 1], a["ln"][0:1, 0:1]).then_inc(s, 16)
            gather(2, 1, 0)
            rounds(pool, body)
            n = pool.value_load(r["used"][0:1, 0:1], min_val=1, max_val=NBLK - 1)
            pool.wait_ge(y_out[0], (n + 1) // 2 * 16 + 16)
            pool.wait_ge(y_out[1], n // 2 * 16 + 16)
            pool.wait_ge(xg_in[0], (n + 4) // 2 * 16 + 16)
            pool.wait_ge(xg_in[1], (n + 3) // 2 * 16 + 16)

        @block.scalar
        def _(act):
            def high(b, v, part, c, slot):
                act.wait_ge(raw_in[slot], v * 16 + 16)
                act.wait_ge(used[part], b * (GU, DN)[part] + c + 1)
                act.activation(hi[:, slot, :], raw[:, slot, :], ACT.Copy).then_inc(hi_ok[part], 1)

            def x_high(b):
                for j in range(2):
                    act.wait_ge(xt_ok, b + 2)
                    act.activation(x_hi[:, j * 512:(j + 1) * 512], x_ps[j][:, :], ACT.Copy).then_inc(x_hi_ok[j], 1)

            def gate_up(b):
                with act.If(plan(act, "fresh", b, 1) > 0):
                    v = plan(act, "visit", b)
                    for c, slot in chunks(0)[:3]:
                        high(b, v, 0, c, slot)
                    x_high(b)
                    high(b, v, 0, *chunks(0)[3])
                with act.Else():
                    x_high(b)

            def silu(b):
                act.wait_ge(used[0], b * GU + 2 + GU)
                act.wait_ge(hid_ok, b + 1)
                act.activation(gate[:, :], gate_ps[:, :], ACT.Silu).then_inc(gate_ok, 1)

            def body(b, i, s, more):
                with act.If(plan(act, "fresh", b, 1) > 0):
                    v = plan(act, "visit", b)
                    for c, slot in chunks(1):
                        high(b, v, 1, c, slot)
                act.wait_ge(ht_ok, b + 2)
                act.activation(h_hi[:, :], h_ps[:, :], ACT.Copy).then_inc(h_hi_ok, 1)
                with act.If(more):
                    silu(b + 1)
                    gate_up(b + 2)
                act.wait_ge(used[1], b * DN + 1 + DN)
                act.wait_ge(y_out[s], i * 16 + 16)
                act.activation(y[:, s, 0:512], y_ps[0][:, :], ACT.Copy).then_inc(y_ok[0], 1)

            gate_up(0)
            silu(0)
            gate_up(1)
            rounds(act, body)

        @block.vector
        def _(dve):
            dve.sem_inc(lo_ok[0], GU)
            dve.sem_inc(lo_ok[1], DN)

            def low(b, v, part, c, slot):
                dve.wait_ge(hi_ok[part], v * (GU, DN)[part] + c + 1)
                dve.wait_ge(used[part], b * (GU, DN)[part] + c + 1)
                dve.tensor_tensor(lo[:, slot, :], raw[:, slot, :], hi[:, slot, :].bitcast(F32), ALU.subtract)\
                   .then_inc(lo_ok[part], 1)

            def x_low(b):
                for j in range(2):
                    at = slice(j * 512, (j + 1) * 512)
                    dve.wait_ge(x_hi_ok[j], b + 1)
                    dve.tensor_tensor(x_lo[:, at], x_ps[j][:, :], x_hi[:, at].bitcast(F32), ALU.subtract)\
                       .then_inc(x_lo_ok[j], 1)

            def hidden(b):
                dve.wait_ge(used[0], b * GU + 4 + GU)
                dve.wait_ge(gate_ok, b + 2)
                dve.wait_ge(ht_ok, b + 1)
                dve.tensor_tensor(hid[:, :], gate[:, :], up_ps[:, :], ALU.mult).then_inc(hid_ok, 1)

            def gate_up(b):
                with dve.If(plan(dve, "fresh", b, 1) > 0):
                    v = plan(dve, "visit", b)
                    for c, slot in chunks(0)[:3]:
                        low(b, v, 0, c, slot)
                    if not isinstance(b, int) or b > 0:
                        hidden(b - 1)
                    x_low(b)
                    low(b, v, 0, *chunks(0)[3])
                with dve.Else():
                    if not isinstance(b, int) or b > 0:
                        hidden(b - 1)
                    x_low(b)

            def body(b, i, s, more):
                with dve.If(plan(dve, "fresh", b, 1) > 0):
                    v = plan(dve, "visit", b)
                    for c, slot in chunks(1):
                        low(b, v, 1, c, slot)
                dve.wait_ge(h_hi_ok, b + 1)
                dve.tensor_tensor(h_lo[:, :], h_ps[:, :], h_hi[:, :].bitcast(F32), ALU.subtract).then_inc(h_lo_ok, 1)
                with dve.If(more):
                    gate_up(b + 2)
                dve.wait_ge(used[1], b * DN + 2 + DN)
                dve.wait_ge(y_out[s], i * 16 + 16)
                dve.tensor_copy(y[:, s, 512:], y_ps[1][:, :]).then_inc(y_ok[1], 1)

            gate_up(0)
            gate_up(1)
            rounds(dve, body)

        @block.tensor
        def _(pe):
            pe.sem_inc(used[0], GU)
            pe.sem_inc(used[1], DN)

            def turn_rows(b, i, s):
                pe.wait_ge(xg_in[s], i * 16 + 32)
                pe.wait_ge(x_lo_ok[1], b + 1)
                for k in range(KD):
                    last = pe.transpose(x_ps[k // 4][:, (k % 4) * P:(k % 4 + 1) * P], xg[:, s, k * P:(k + 1) * P],
                                        ident[:, :])
                last.then_inc(xt_ok, 1)

            def chunk(v, part, c, slot, out, left_hi, left_lo, k0, first, last_k):
                pe.wait_ge(lo_ok[part], v * (GU, DN)[part] + c + 1 + (GU, DN)[part])
                for j in range(4):
                    w, t = slice(j * 512, (j + 1) * 512), slice((k0 + j) * P, (k0 + j + 1) * P)
                    pe.matmul(out[:, :], left_hi[:, t], hi[:, slot, w], start=(first and j == 0), stop=False)
                    pe.matmul(out[:, :], left_hi[:, t], lo[:, slot, w], start=False, stop=False)
                    last = pe.matmul(out[:, :], left_lo[:, t], hi[:, slot, w], start=False, stop=(last_k and j == 3))
                last.then_inc(used[part], 1)

            def gate_up(b):
                v = plan(pe, "visit", b)
                pe.wait_ge(x_lo_ok[0], b + 2)
                pe.wait_ge(x_lo_ok[1], b + 2)
                pe.wait_ge(gate_ok, b + 1)
                pe.wait_ge(hid_ok, b + 1)
                for c, slot in chunks(0):
                    chunk(v, 0, c, slot, (gate_ps, up_ps)[c // 2], x_hi, x_lo, (c % 2) * 4, c % 2 == 0, c % 2 == 1)

            def turn_hidden(b):
                pe.wait_ge(hid_ok, b + 2)
                pe.wait_ge(h_lo_ok, b + 1)
                for k in range(KE):
                    last = pe.transpose(h_ps[:, k * P:(k + 1) * P], hid[:, k * P:(k + 1) * P], ident[:, :])
                last.then_inc(ht_ok, 1)

            def body(b, i, s, more):
                turn_hidden(b)
                with pe.If(more):
                    gate_up(b + 1)
                    turn_rows(b + 2, i + 1, s)
                v = plan(pe, "visit", b)
                pe.wait_ge(h_lo_ok, b + 2)
                for c, slot in chunks(1):
                    pe.wait_ge(y_ok[c], b + 1)
                    chunk(v, 1, c, slot, y_ps[c], h_hi, h_lo, 0, True, True)

            turn_rows(0, 0, 0)
            gate_up(0)
            turn_rows(1, 0, 1)
            rounds(pe, body)


AHEAD = 4


def combine(nc, h_rows, y_rows, r, ahead, out):
    with ExitStack() as ctx:
        sb = lambda n, s, d=F32: ctx.enter_context(nc.sbuf_tensor(n, s, d))
        sem = lambda n: ctx.enter_context(nc.semaphore(n))
        S = 6
        ln_g, ln_b, ln_in = ahead["ln_g"], ahead["ln_b"], ahead["ln_in"]
        yc = [sb(f"c_y{c}", [P, S, D]) for c in range(2)]
        acc, res = sb("c_acc", [P, S, D]), sb("c_res", [P, S, D])
        h_more = sb("c_h", [P, S - AHEAD, D])
        h = [ahead["h"][:, s, :] for s in range(AHEAD)] + [h_more[:, s, :] for s in range(S - AHEAD)]
        stats = sb("c_stats", [P, S, 12])
        mom = sb("c_mom", [P, S, 4])
        neg_half = sb("c_neg_half", [P, 1])
        const_ok = sem("c_const_ok")
        rows_in = ahead["rows_in"] + [sem(f"c_rows_in{s}") for s in range(AHEAD, S)]
        acc_step = sem("c_acc_step")
        sum_step = sem("c_sum_step")
        stat_step = sem("c_stat_step")
        eps_ok, rstd_ok = sem("c_eps_ok"), sem("c_rstd_ok")
        shift_ok = sem("c_shift_ok")
        norm_ok = sem("c_norm_ok")
        gain_ok = sem("c_gain_ok")
        done = sem("c_done")
        stored = [sem(f"c_stored{s}") for s in range(S)]
        block = ctx.enter_context(nc.Block())
        n = NSUB // S

        def subtiles(i):
            return [(s, i * S + s) for s in range(S)]

        @block.sync
        def _(sp):
            for t in range(NSUB):
                s = t % S
                if t >= S:
                    sp.wait_ge(sum_step, t * 2 + 2)
                for c in range(2):
                    sp.dma_start(yc[c][:, s, :], y_rows[t * P + c * NTOK:(t + 1) * P + c * NTOK, :])\
                      .then_inc(rows_in[s], 16)
                if t >= AHEAD:
                    sp.dma_start(h[s], h_rows[t * P:(t + 1) * P, :]).then_inc(rows_in[s], 16)

        @block.gpsimd
        def _(pool):
            pool.sem_inc(norm_ok, S)
            pool.sem_inc(sum_step, 2 * S)
            for s in stored:
                pool.sem_inc(s, 1)
            pool.memset(neg_half[:, :], -0.5).then_inc(const_ok, 1)

            def gain(s, t):
                pool.wait_ge(ln_in, 32)
                pool.wait_ge(norm_ok, t + 1 + S)
                pool.tensor_tensor(res[:, s, :], res[:, s, :], ln_g[:, :], ALU.mult).then_inc(gain_ok, 1)

            with pool.Fori(0, n) as i:
                for s, t in subtiles(i):
                    known = pool.to_reg(t * 3 + 3)
                    pool.wait_ge(const_ok, 1)
                    pool.wait_ge(stat_step, known)
                    pool.tensor_scalar(mom[:, s, 1:2], mom[:, s, 1:2], EPS, None, ALU.add).then_inc(eps_ok, 1)
                    pool.wait_ge(eps_ok, t + 1)
                    pool.tensor_tensor(mom[:, s, 2:3], mom[:, s, 1:2], neg_half[:, :], ALU.pow).then_inc(rstd_ok, 1)
                    if s:
                        gain(s - 1, t - 1)
                gain(S - 1, i * S + S - 1)

        @block.scalar
        def _(act):
            def norm(s, t, i):
                act.wait_ge(shift_ok, t + 1)
                act.wait_ge(stored[s], i * 16 + 1)
                act.activation(res[:, s, :], acc[:, s, :], ACT.Identity, scale=mom[:, s, 2:3],
                               bias=mom[:, s, 3:4]).then_inc(norm_ok, 1)

            def store(s, t):
                act.wait_ge(done, t + 1)
                act.dma_start(out[bass.ds(t * P, P), :], res[:, s, :]).then_inc(stored[s], 16)

            with act.Fori(0, n) as i:
                for s, t in subtiles(i):
                    act.wait_ge(rows_in[s], i * 48 + 48)
                    act.wait_ge(norm_ok, t + 1)
                    act.activation(acc[:, s, :], yc[0][:, s, :], ACT.Copy,
                                   scale=r["gates"][:, bass.ds(t, 1)]).then_inc(acc_step, 1)
                    if s > 0:
                        norm(s - 1, t - 1, i)
                    if s > 2:
                        store(s - 3, t - 3)
                norm(S - 1, i * S + S - 1, i)
                for s in range(S - 3, S):
                    store(s, i * S + s)
            for s in range(S):
                act.wait_ge(stored[s], n * 16 + 1)

        @block.vector
        def _(dve):
            dve.wait_ge(ln_in, 32)

            def offset(s, t):
                dve.wait_ge(gain_ok, t + 1)
                dve.tensor_tensor(res[:, s, :], res[:, s, :], ln_b[:, :], ALU.add).then_inc(done, 1)

            with dve.Fori(0, n) as i:
                for s, t in subtiles(i):
                    dve.wait_ge(acc_step, t + 1)
                    dve.wait_ge(rows_in[s], i * 48 + 48)
                    dve.scalar_tensor_tensor(acc[:, s, :], yc[1][:, s, :], r["gates"][:, bass.ds(t + NSUB, 1)],
                                             acc[:, s, :], ALU.mult, ALU.add).then_inc(sum_step, 1)
                    dve.wait_ge(sum_step, t * 2 + 1 + 2 * S)
                    dve.scalar_tensor_tensor(acc[:, s, :], h[s], ALPHA, acc[:, s, :], ALU.mult, ALU.add)\
                       .then_inc(sum_step, 1)
                    dve.wait_ge(sum_step, t * 2 + 2 + 2 * S)
                    for half in range(2):
                        dve.bn_stats(stats[:, s, half * 6:half * 6 + 6], acc[:, s, half * 512:(half + 1) * 512])\
                           .then_inc(stat_step, 1)
                    taken = dve.to_reg(t * 3 + 2)
                    dve.wait_ge(ln_in, 32)
                    dve.wait_ge(stat_step, taken)
                    dve.bn_aggr(mom[:, s, 0:2], stats[:, s, :]).then_inc(stat_step, 1)
                    if s > 1:
                        offset(s - 2, t - 2)
                    dve.wait_ge(rstd_ok, t + 1)
                    dve.scalar_tensor_tensor(mom[:, s, 3:4], mom[:, s, 0:1], -1.0, mom[:, s, 2:3], ALU.mult, ALU.mult)\
                       .then_inc(shift_ok, 1)
                for s in (S - 2, S - 1):
                    offset(s, i * S + s)


def encoder(nc, a, out):
    qkv = nc.dram_tensor("qkv", [3 * HP, P, NCOL], F32, kind="Internal").ap()
    h_rows = nc.dram_tensor("h_rows", [NTOK, D], F32, kind="Internal").ap()
    y_rows = nc.dram_tensor("y_rows", [2 * NTOK + P, D], F32, kind="Internal").ap()
    with ExitStack() as ctx:
        sb = lambda n, s, d=F32: ctx.enter_context(nc.sbuf_tensor(n, s, d))
        ident = sb("ident", [P, P])
        logits = sb("logits", [P, NSUB * NLOG])
        r = {
            "gates": sb("gates", [P, 2 * NSUB]),
            "table": sb("table", [P, NPLAN], I32),
            "dest": sb("dest", [P, NPLAN], I32),
            "owner": sb("owner", [1, NPLAN], I32),
            "fresh": sb("fresh", [1, NPLAN], I32),
            "visit": sb("visit", [1, NPLAN], I32),
            "used": sb("used", [1, 1], I32),
        }
        edges = sb("edges", [P, FB * NEDGE])
        stored = [ctx.enter_context(nc.semaphore(f"qkv_stored{s}")) for s in range(2)]
        with nc.sbuf_tensor("x_hi", [P, KD, TILE], F32R) as x_hi, nc.sbuf_tensor("x_lo", [P, KD, TILE], F32R) as x_lo:
            project_qkv(nc, a, x_hi, x_lo, ident, qkv, edges, stored)
            mixer(nc, a, x_hi, x_lo, qkv, edges, ident, logits, h_rows)
        with ExitStack() as late:
            raw = late.enter_context(nc.sbuf_tensor("e_raw", [P, GU + DN, 2048], F32))
            raw_in = [late.enter_context(nc.semaphore(f"e_raw_in{c}")) for c in range(GU + DN)]
            ahead = {
                "ln_g": late.enter_context(nc.sbuf_tensor("ln2_g", [P, D], F32)),
                "ln_b": late.enter_context(nc.sbuf_tensor("ln2_b", [P, D], F32)),
                "h": late.enter_context(nc.sbuf_tensor("c_h_ahead", [P, AHEAD, D], F32)),
                "ln_in": late.enter_context(nc.semaphore("c_ln_in")),
                "rows_in": [late.enter_context(nc.semaphore(f"c_rows_in{s}")) for s in range(AHEAD)],
            }
            route(nc, a, logits, ident, r, raw, raw_in)
            experts(nc, a, h_rows, y_rows, ident, r, raw, raw_in, ahead)
            combine(nc, h_rows, y_rows, r, ahead, out)


def layouts(inp):
    a = {k: np.asarray(v) for k, v in inp.items()}
    x = np.concatenate([a["x_prompt"].reshape(PROMPT, D), a["x_sample"].reshape(SAMPLE, D)], 0)
    cols = np.concatenate([x, a["meta_tokens"]], 0).T.reshape(KD, P, NCOL)
    w_in = a["w_in"][0].reshape(KD, P, 52, P).transpose(2, 1, 0, 3).reshape(52, P, D)
    out = {}
    out["x_rows"] = np.ascontiguousarray(x)
    out["x_cols"] = np.ascontiguousarray(cols.transpose(1, 0, 2))
    none = np.zeros((D,), np.float32)
    meta = a["meta_tokens"][NMETA - 1]
    halo = np.stack([np.stack([meta, x[TILE]]), np.stack([x[TILE - 1], none]), np.stack([meta, none])])
    out["x_halo"] = np.ascontiguousarray(halo.reshape(NT, 2, KD, P).transpose(0, 3, 2, 1).reshape(NT, P, KD * 2))
    out["w_qkv"] = np.ascontiguousarray(w_in[0:12])
    b, c, xc, ga, gc = (w_in[12 + 8 * i:20 + 8 * i] for i in range(5))
    out["w_cxb"] = np.ascontiguousarray(np.stack([c, xc, b], 1).reshape(3 * FB, P, D))
    w_conv = a["w_conv_proj"][0].reshape(KD, P, FB, P).transpose(2, 1, 0, 3).reshape(FB, P, D)
    out["w_gates"] = np.ascontiguousarray(np.stack([ga, gc, w_conv], 1).reshape(3 * FB, P, D))
    out["w_att"] = np.ascontiguousarray(
        a["w_att_proj"][0].reshape(HP, P, FB, P).transpose(2, 1, 0, 3).reshape(FB, P, HP * P))
    out["w_out"] = np.ascontiguousarray(
        a["w_out"][0].reshape(KD // 2, 2, P, 2, 512).transpose(3, 0, 2, 1, 4).reshape(KD, P, D))
    cw = np.concatenate([a["conv_w"][0], a["conv_b"]], 0)
    out["conv_wb"] = np.ascontiguousarray(cw.reshape(4, FB, P).transpose(2, 1, 0).reshape(P, 4 * FB))
    plane = np.zeros((HEADS, 16, BP_ROWS * 64 + 64), np.float32)
    rpb = a["rpb"][0]
    for i in range(16):
        for y in range(2 * WIN_H - 1):
            at = (y + 4) * 64 + 16 - (15 - i)
            plane[:, i, at:at + 2 * WIN_W - 1] = rpb[:, y]
    out["bias_planes"] = plane
    out["masks"] = window_masks()
    out["ln"] = np.ascontiguousarray(np.concatenate([a["ln1_g"], a["ln1_b"], a["ln2_g"], a["ln2_b"]], 0))
    wr = np.concatenate([a["w_router_group"][0], a["w_router_expert"][0]], 1)
    out["w_router"] = np.ascontiguousarray(wr.reshape(KD, P, NLOG).transpose(1, 0, 2).reshape(P, KD * NLOG))
    out["w_e_gate"] = a["w_e_gate"][0]
    out["w_e_up"] = a["w_e_up"][0]
    out["w_e_down"] = a["w_e_down"][0]
    return out


def kernel(**inputs):
    import concourse.bacc as bacc
    from concourse.bass_utils import run_bass_kernel_spmd

    arrays = layouts(inputs)
    nc = bacc.Bacc("TRN2", target_bir_lowering=False, num_devices=1)
    a = {n: nc.dram_tensor(f"in_{n}", v.shape, mybir.dt.from_np(v.dtype), kind="ExternalInput").ap()
         for n, v in arrays.items()}
    out = nc.dram_tensor("out", [NTOK, D], F32, kind="ExternalOutput").ap()
    encoder(nc, a, out)
    got = run_bass_kernel_spmd(nc, [{f"in_{n}": v for n, v in arrays.items()}], core_ids=[0]).results[0]["out"]
    return got[:PROMPT].reshape(1, PROMPT, D), got[PROMPT:].reshape(1, SAMPLE, D)
```
